# Optimizing a Trainium2 kernel written in Bass

```python
import math
import jax, jax.numpy as jnp
from jax import lax
import numpy as np
import jax
import jax.numpy as jnp

D_MODEL = 1024
BATCH = 1
SEQ = 256
DEPTH = 2

CTX_LEN = 256
GRID_W = 64
HEAD_DIM = 64
A_Q_HEADS = 6
A_KV_HEADS = 2
F_GROUPS = 4
F_GROUP_CH = 64
C_Q_HEADS = 6
C_KV_HEADS = 2
WINDOW = 128
Q_BLOCK = 128
ROPE_THETA = 10000.0
AXIS_ROT = HEAD_DIM // 2
D_FF = -(-8 * D_MODEL // (3 * 256)) * 256
NORM_EPS = 1e-6
NEG_INF = -1e30

Q_A_W = A_Q_HEADS * HEAD_DIM
KV_A_W = A_KV_HEADS * HEAD_DIM
F_W = F_GROUPS * F_GROUP_CH
Q_C_W = C_Q_HEADS * HEAD_DIM
KV_C_W = C_KV_HEADS * HEAD_DIM
IN_WIDTH = Q_A_W + 2 * KV_A_W + F_W + Q_C_W + 2 * KV_C_W
MIX_WIDTH = Q_A_W + F_W + Q_C_W


def rms_norm(x, g):
    xf = x.astype(jnp.float32)
    y = xf * lax.rsqrt(jnp.mean(xf * xf, axis=-1, keepdims=True) + NORM_EPS)
    return (y * g.astype(jnp.float32)).astype(x.dtype)

def adaln(cond, w_ada, b_ada):
    m = jax.nn.silu(cond) @ w_ada + b_ada
    return jnp.split(m, 6, axis=-1)

def axial_rope_tables(n_tokens):
    rows = n_tokens // GRID_W
    row = jnp.repeat(jnp.arange(rows, dtype=jnp.float32), GRID_W)
    col = jnp.tile(jnp.arange(GRID_W, dtype=jnp.float32), rows)
    inv_freq = ROPE_THETA ** (-jnp.arange(0, AXIS_ROT, 2, dtype=jnp.float32) / AXIS_ROT)
    ang = jnp.concatenate([row[:, None] * inv_freq, col[:, None] * inv_freq], axis=-1)
    return jnp.cos(ang), jnp.sin(ang)

def apply_rope(x, cos, sin):
    xf = x.astype(jnp.float32)
    half = HEAD_DIM // 2
    x1, x2 = xf[..., :half], xf[..., half:]
    c = cos[None, :, None, :]
    s = sin[None, :, None, :]
    return jnp.concatenate([x1 * c - x2 * s, x2 * c + x1 * s], axis=-1).astype(x.dtype)

def gqa_logits(q, k):
    b, lq, h, dh = q.shape
    kvh = k.shape[2]
    qg = q.reshape(b, lq, kvh, h // kvh, dh)
    return jnp.einsum('bqhgd,bkhd->bhgqk', qg, k, preferred_element_type=jnp.float32) * (dh ** -0.5)

def gqa_combine(p, v):
    o = jnp.einsum('bhgqk,bkhd->bqhgd', p.astype(v.dtype), v)
    return o.reshape(o.shape[0], o.shape[1], -1)

def sink_logits(sink, like):
    kvh, g = like.shape[1], like.shape[2]
    return jnp.broadcast_to(sink.astype(jnp.float32).reshape(1, kvh, g, 1, 1), like.shape[:-1] + (1,))

def dense_attention(q, k, v, sink=None):
    s = gqa_logits(q, k)
    if sink is None:
        return gqa_combine(jax.nn.softmax(s, axis=-1), v)
    s = jnp.concatenate([s, sink_logits(sink, s)], axis=-1)
    p = jax.nn.softmax(s, axis=-1)[..., :-1]
    return gqa_combine(p, v)

def global_attention(q, k, v, k_ctx, v_ctx):
    b, s, h, dh = q.shape
    nb = s // Q_BLOCK
    k_all = jnp.concatenate([k_ctx, k], axis=1)
    v_all = jnp.concatenate([v_ctx, v], axis=1)
    qb = jnp.moveaxis(q.reshape(b, nb, Q_BLOCK, h, dh), 1, 0)
    ob = lax.map(lambda qi: dense_attention(qi, k_all, v_all), qb)
    return jnp.moveaxis(ob, 0, 1).reshape(b, s, h * dh)

def window_attention(q, k, v, k_ctx, v_ctx, sink):
    b, s, h, dh = q.shape
    nb = s // Q_BLOCK
    band = Q_BLOCK + 2 * WINDOW
    n_ctx = k_ctx.shape[1]
    pad = ((0, 0), (WINDOW, WINDOW), (0, 0), (0, 0))
    kp = jnp.pad(k, pad)
    vp = jnp.pad(v, pad)
    qb = jnp.moveaxis(q.reshape(b, nb, Q_BLOCK, h, dh), 1, 0)
    qi_idx = jnp.arange(Q_BLOCK)[:, None]
    kj = jnp.arange(band)[None, :]
    in_window = jnp.abs(kj - WINDOW - qi_idx) <= WINDOW

    def one_block(args):
        qi, n = args
        start = n * Q_BLOCK
        kb = lax.dynamic_slice_in_dim(kp, start, band, axis=1)
        vb = lax.dynamic_slice_in_dim(vp, start, band, axis=1)
        kpos = start - WINDOW + kj
        valid = in_window & (kpos >= 0) & (kpos < s)
        s_loc = jnp.where(valid, gqa_logits(qi, kb), NEG_INF)
        s_ctx = gqa_logits(qi, k_ctx)
        logits = jnp.concatenate([s_loc, s_ctx, sink_logits(sink, s_loc)], axis=-1)
        p = jax.nn.softmax(logits, axis=-1)
        return gqa_combine(p[..., :band], vb) + gqa_combine(p[..., band:band + n_ctx], v_ctx)

    ob = lax.map(one_block, (qb, jnp.arange(nb)))
    return jnp.moveaxis(ob, 0, 1).reshape(b, s, h * dh)

def fourier_mix(u):
    b, l, _ = u.shape
    ug = u.astype(jnp.float32).reshape(b, l, F_GROUPS, F_GROUP_CH)
    f = jnp.fft.fftn(ug, axes=(1, 3), norm='ortho').real
    return f.reshape(b, l, F_W).astype(u.dtype)

def mixer_inputs(h, w_in, q_norm, k_norm, rope):
    b, l, _ = h.shape
    widths = (Q_A_W, KV_A_W, KV_A_W, F_W, Q_C_W, KV_C_W, KV_C_W)
    points = [int(p) for p in np.cumsum(widths)[:-1]]
    qa, ka, va, fb, qc, kc, vc = jnp.split(h @ w_in, points, axis=-1)
    qa = rms_norm(qa.reshape(b, l, A_Q_HEADS, HEAD_DIM), q_norm)
    ka = rms_norm(ka.reshape(b, l, A_KV_HEADS, HEAD_DIM), k_norm)
    va = va.reshape(b, l, A_KV_HEADS, HEAD_DIM)
    qc = qc.reshape(b, l, C_Q_HEADS, HEAD_DIM)
    kc = kc.reshape(b, l, C_KV_HEADS, HEAD_DIM)
    vc = vc.reshape(b, l, C_KV_HEADS, HEAD_DIM)
    if rope is not None:
        cos, sin = rope
        qa, ka = apply_rope(qa, cos, sin), apply_rope(ka, cos, sin)
        qc, kc = apply_rope(qc, cos, sin), apply_rope(kc, cos, sin)
    return qa, ka, va, fb, qc, kc, vc

def swiglu(h, w_gate, w_up, w_down):
    return (jax.nn.silu(h @ w_gate) * (h @ w_up)) @ w_down

def first_inputs(seed: int = 0) -> dict:
    key = jax.random.key(seed)
    ks = jax.random.split(key, 18)
    n = jax.random.normal
    f32 = jnp.float32
    return {
        'x': n(ks[0], (BATCH, SEQ, D_MODEL), f32),
        'c': n(ks[1], (BATCH, D_MODEL), f32),
        'ctx': n(ks[2], (BATCH, CTX_LEN, D_MODEL), f32),
        'c_ctx': n(ks[3], (D_MODEL,), f32),
        'w_ada': 0.02 * n(ks[4], (DEPTH, D_MODEL, 6 * D_MODEL), f32),
        'b_ada': 0.01 * n(ks[5], (DEPTH, 6 * D_MODEL), f32),
        'g_mix': 1.0 + 0.05 * n(ks[6], (DEPTH, D_MODEL), f32),
        'g_ffn': 1.0 + 0.05 * n(ks[7], (DEPTH, D_MODEL), f32),
        'w_in': n(ks[8], (DEPTH, D_MODEL, IN_WIDTH), f32) * D_MODEL ** -0.5,
        'q_norm': 1.0 + 0.05 * n(ks[9], (DEPTH, HEAD_DIM), f32),
        'k_norm': 1.0 + 0.05 * n(ks[10], (DEPTH, HEAD_DIM), f32),
        'sink': 0.5 * n(ks[11], (DEPTH, C_Q_HEADS), f32),
        'w_out': n(ks[12], (DEPTH, MIX_WIDTH, D_MODEL), f32) * MIX_WIDTH ** -0.5,
        'w_gate': n(ks[13], (DEPTH, D_MODEL, D_FF), f32) * D_MODEL ** -0.5,
        'w_up': n(ks[14], (DEPTH, D_MODEL, D_FF), f32) * D_MODEL ** -0.5,
        'w_down': n(ks[15], (DEPTH, D_FF, D_MODEL), f32) * D_FF ** -0.5,
        'g_final': 1.0 + 0.05 * n(ks[16], (D_MODEL,), f32),
    }

def first_block(x, c, ctx, c_ctx, w_ada, b_ada, g_mix, g_ffn, w_in, q_norm, k_norm, sink, w_out, w_gate, w_up, w_down, g_final):
    rope = axial_rope_tables(x.shape[1])
    for l in range(DEPTH):
        update_ctx = l < DEPTH - 1
        sh1, sc1, gt1, sh2, sc2, gt2 = [m[:, None, :] for m in adaln(c, w_ada[l], b_ada[l])]
        csh1, csc1, cgt1, csh2, csc2, cgt2 = adaln(c_ctx, w_ada[l], b_ada[l])
        h = rms_norm(x, g_mix[l]) * (1 + sc1) + sh1
        hc = rms_norm(ctx, g_mix[l]) * (1 + csc1) + csh1
        qa, ka, va, fb, qc, kc, vc = mixer_inputs(h, w_in[l], q_norm[l], k_norm[l], rope)
        qac, kac, vac, fbc, qcc, kcc, vcc = mixer_inputs(hc, w_in[l], q_norm[l], k_norm[l], None)
        o = jnp.concatenate([
            global_attention(qa, ka, va, kac, vac),
            fourier_mix(fb),
            window_attention(qc, kc, vc, kcc, vcc, sink[l]),
        ], axis=-1)
        x = x + gt1 * (o @ w_out[l])
        x = x + gt2 * swiglu(rms_norm(x, g_ffn[l]) * (1 + sc2) + sh2, w_gate[l], w_up[l], w_down[l])
        if update_ctx:
            oc = jnp.concatenate([
                dense_attention(qac, kac, vac),
                fourier_mix(fbc),
                dense_attention(qcc, kcc, vcc, sink[l]),
            ], axis=-1)
            ctx = ctx + cgt1 * (oc @ w_out[l])
            ctx = ctx + cgt2 * swiglu(rms_norm(ctx, g_ffn[l]) * (1 + csc2) + csh2, w_gate[l], w_up[l], w_down[l])
    return rms_norm(x, g_final)


NEG_INF_2 = -1e30
FORCE_SCORE = 1e6

DA_HEADS = 4
DA_HEAD_DIM = 64
DA_V_DIM = 2 * DA_HEAD_DIM
SSM_HEADS = 8
SSM_HEAD_DIM = 64
SSM_D_INNER = SSM_HEADS * SSM_HEAD_DIM
SSM_GROUPS = 2
SSM_STATE = 128
SSM_CONV = 4
SSM_CHUNK = 256
SSM_CONV_CH = SSM_D_INNER + 2 * SSM_GROUPS * SSM_STATE
NSA_HEADS = 8
NSA_KV_GROUPS = 2
NSA_HEAD_DIM = 64
NSA_CMP_BLOCK = 32
NSA_CMP_STRIDE = 16
NSA_SEL_BLOCK = 64
NSA_TOP_N = 16
NSA_WINDOW = 512
NSA_KV = NSA_KV_GROUPS * NSA_HEAD_DIM
MLA_HEADS = 4
MLA_Q_RANK = 256
MLA_KV_RANK = 128
MLA_NOPE_DIM = 128
MLA_ROPE_DIM = 64
MLA_V_DIM = 128
D_FF_2 = 2816
N_EXPERTS = 8
TOP_K = 2

EVEN_SPLITS = (DA_HEADS * 2 * DA_HEAD_DIM, DA_HEADS * 2 * DA_HEAD_DIM, DA_HEADS * DA_V_DIM,
               SSM_D_INNER, SSM_CONV_CH, SSM_HEADS)
EVEN_IN = sum(EVEN_SPLITS)
EVEN_MIX = DA_HEADS * DA_V_DIM + SSM_D_INNER
ODD_SPLITS = (NSA_HEADS * NSA_HEAD_DIM, NSA_KV, NSA_KV, NSA_KV, NSA_KV, NSA_KV, NSA_KV,
              NSA_HEADS * 3, MLA_Q_RANK, MLA_KV_RANK, MLA_ROPE_DIM)
ODD_IN = sum(ODD_SPLITS)
ODD_MIX = NSA_HEADS * NSA_HEAD_DIM + MLA_HEADS * MLA_V_DIM


def rms_norm_2(t, gain):
    tf = t.astype(jnp.float32)
    y = tf * lax.rsqrt(jnp.mean(tf * tf, axis=-1, keepdims=True) + NORM_EPS)
    return (y * gain.astype(jnp.float32)).astype(t.dtype)

def split_cols(t, sizes):
    return jnp.split(t, [int(v) for v in np.cumsum(sizes)[:-1]], axis=-1)

def rope_tables(seq_len, dim):
    inv_freq = 1.0 / (ROPE_THETA ** (jnp.arange(0, dim, 2, dtype=jnp.float32) / dim))
    ang = jnp.arange(seq_len, dtype=jnp.float32)[:, None] * inv_freq[None, :]
    return jnp.cos(ang), jnp.sin(ang)

def apply_rope_2(t, cos, sin):
    half = t.shape[-1] // 2
    c = cos[:, None, :].astype(t.dtype)
    s = sin[:, None, :].astype(t.dtype)
    t1, t2 = t[..., :half], t[..., half:]
    return jnp.concatenate([t1 * c - t2 * s, t2 * c + t1 * s], axis=-1)

def swiglu_2(h, w_gate, w_up, w_down):
    return (jax.nn.silu(h @ w_gate) * (h @ w_up)) @ w_down

def causal_attention_blocked(q, k, v, scale):
    b, s, h, dq = q.shape
    nb = s // Q_BLOCK
    qb = q.reshape(b, nb, Q_BLOCK, h, dq).transpose(1, 0, 2, 3, 4)
    k_pos = jnp.arange(s)

    def one_block(args):
        q_blk, blk = args
        q_pos = blk * Q_BLOCK + jnp.arange(Q_BLOCK)
        causal = k_pos[None, :] <= q_pos[:, None]
        sc = jnp.einsum('bqhd,bkhd->bhqk', q_blk, k).astype(jnp.float32) * scale
        p = jax.nn.softmax(jnp.where(causal, sc, NEG_INF_2), axis=-1)
        return jnp.einsum('bhqk,bkhd->bqhd', p.astype(v.dtype), v)

    o = lax.map(one_block, (qb, jnp.arange(nb)))
    return o.transpose(1, 0, 2, 3, 4).reshape(b, s, h, v.shape[-1])

def diff_attention(q, k, v, q_gain, k_gain, lam, subln_gain, layer_idx):
    b, s, _ = q.shape
    h, d = DA_HEADS, DA_HEAD_DIM
    cos, sin = rope_tables(s, d)
    q = apply_rope_2(rms_norm_2(q.reshape(b, s, 2 * h, d), q_gain), cos, sin).reshape(b, s, h, 2, d)
    k = apply_rope_2(rms_norm_2(k.reshape(b, s, 2 * h, d), k_gain), cos, sin).reshape(b, s, h, 2, d)
    v = v.reshape(b, s, h, DA_V_DIM)
    lam_init = 0.8 - 0.6 * math.exp(-0.3 * layer_idx)
    lf = lam.astype(jnp.float32)
    lam_full = jnp.exp(jnp.sum(lf[0] * lf[1])) - jnp.exp(jnp.sum(lf[2] * lf[3])) + lam_init
    scale = d ** -0.5
    nb = s // Q_BLOCK
    qb = q.reshape(b, nb, Q_BLOCK, h, 2, d).transpose(1, 0, 2, 3, 4, 5)
    k_pos = jnp.arange(s)

    def one_block(args):
        q_blk, blk = args
        q_pos = blk * Q_BLOCK + jnp.arange(Q_BLOCK)
        causal = k_pos[None, :] <= q_pos[:, None]
        sc = jnp.einsum('bqhcd,bkhcd->bhcqk', q_blk, k).astype(jnp.float32) * scale
        p = jax.nn.softmax(jnp.where(causal, sc, NEG_INF_2), axis=-1)
        attn = p[:, :, 0] - lam_full * p[:, :, 1]
        return jnp.einsum('bhqk,bkhe->bqhe', attn.astype(v.dtype), v)

    o = lax.map(one_block, (qb, jnp.arange(nb)))
    o = o.transpose(1, 0, 2, 3, 4).reshape(b, s, h, DA_V_DIM)
    o = rms_norm_2(o, subln_gain) * (1.0 - lam_init)
    return o.reshape(b, s, h * DA_V_DIM)

def causal_depthwise_conv(t, w, bias):
    width, ch = w.shape
    y = lax.conv_general_dilated(t, w[:, None, :].astype(t.dtype), window_strides=(1,),
                                 padding=[(width - 1, 0)],
                                 dimension_numbers=('NWC', 'WIO', 'NWC'),
                                 feature_group_count=ch)
    return y + bias.astype(t.dtype)

def segsum(a):
    t = a.shape[-1]
    cs = jnp.cumsum(a, axis=-1)
    diff = cs[..., :, None] - cs[..., None, :]
    return jnp.where(jnp.tril(jnp.ones((t, t), dtype=bool)), diff, -jnp.inf)

def ssd_chunked_scan(xh, dt, a, bmat, cmat):
    b, L, h, p = xh.shape
    n = bmat.shape[-1]
    nc = L // SSM_CHUNK
    xs = (xh * dt[..., None]).reshape(b, nc, SSM_CHUNK, h, p)
    ad = (dt * a).reshape(b, nc, SSM_CHUNK, h).transpose(0, 3, 1, 2)
    bc = bmat.reshape(b, nc, SSM_CHUNK, h, n)
    cc = cmat.reshape(b, nc, SSM_CHUNK, h, n)
    a_cs = jnp.cumsum(ad, axis=-1)
    decay_in = jnp.exp(segsum(ad))
    y_diag = jnp.einsum('bclhn,bcshn,bhcls,bcshp->bclhp', cc, bc, decay_in, xs)
    decay_to_end = jnp.exp(a_cs[..., -1:] - a_cs)
    chunk_states = jnp.einsum('bclhn,bhcl,bclhp->bchpn', bc, decay_to_end, xs)
    chunk_decay = jnp.exp(a_cs[..., -1])

    def step(state, inp):
        st, dec = inp
        return state * dec[:, :, None, None] + st, state

    init = jnp.zeros((b, h, p, n), xs.dtype)
    _, prev = lax.scan(step, init, (chunk_states.transpose(1, 0, 2, 3, 4),
                                    chunk_decay.transpose(2, 0, 1)))
    prev = prev.transpose(1, 0, 2, 3, 4)
    y_off = jnp.einsum('bclhn,bchpn,bhcl->bclhp', cc, prev, jnp.exp(a_cs))
    return (y_diag + y_off).reshape(b, L, h, p)

def mamba2_ssd(z, xbc, dt_raw, conv_w, conv_b, dt_bias, a_log, d_skip, norm_gain):
    b, s, _ = z.shape
    f32 = jnp.float32
    xbc = jax.nn.silu(causal_depthwise_conv(xbc, conv_w, conv_b))
    xs, bm, cm = split_cols(xbc, (SSM_D_INNER, SSM_GROUPS * SSM_STATE, SSM_GROUPS * SSM_STATE))
    rep = SSM_HEADS // SSM_GROUPS
    xh = xs.reshape(b, s, SSM_HEADS, SSM_HEAD_DIM)
    bm = jnp.repeat(bm.reshape(b, s, SSM_GROUPS, SSM_STATE), rep, axis=2)
    cm = jnp.repeat(cm.reshape(b, s, SSM_GROUPS, SSM_STATE), rep, axis=2)
    dt = jax.nn.softplus(dt_raw.astype(f32) + dt_bias.astype(f32))
    a = -jnp.exp(a_log.astype(f32))
    pad = (-s) % SSM_CHUNK

    def padf(t):
        return jnp.pad(t.astype(f32), [(0, 0), (0, pad)] + [(0, 0)] * (t.ndim - 2))

    y = ssd_chunked_scan(padf(xh), padf(dt), a, padf(bm), padf(cm))[:, :s]
    y = y + xh.astype(f32) * d_skip.astype(f32)[:, None]
    y = y.reshape(b, s, SSM_D_INNER) * jax.nn.silu(z.astype(f32))
    y = rms_norm_2(y.reshape(b, s, SSM_GROUPS, SSM_D_INNER // SSM_GROUPS),
                 norm_gain.reshape(SSM_GROUPS, SSM_D_INNER // SSM_GROUPS))
    return y.reshape(b, s, SSM_D_INNER).astype(z.dtype)

def compress_blocks(t, pos_emb, w1, w2):
    b, s, g, d = t.shape
    r = NSA_CMP_BLOCK // NSA_CMP_STRIDE
    n_chunks = s // NSA_CMP_STRIDE
    n_cmp = n_chunks - r + 1
    ch = t.reshape(b, n_chunks, NSA_CMP_STRIDE, g, d)
    blocks = jnp.concatenate([ch[:, j:j + n_cmp] for j in range(r)], axis=2)
    blocks = blocks + pos_emb[None, None, :, None, :].astype(t.dtype)
    flat = blocks.transpose(0, 1, 3, 2, 4).reshape(b, n_cmp, g, NSA_CMP_BLOCK * d)
    return jax.nn.silu(flat @ w1) @ w2

def nsa_overlap(n_cmp, n_sel):
    c_start = np.arange(n_cmp)[:, None] * NSA_CMP_STRIDE
    s_start = np.arange(n_sel)[None, :] * NSA_SEL_BLOCK
    hit = (c_start < s_start + NSA_SEL_BLOCK) & (c_start + NSA_CMP_BLOCK > s_start)
    return jnp.asarray(hit.astype(np.float32))

def _take_blocks(blocks, idx):
    return blocks[idx]

_gather_blocks = jax.vmap(jax.vmap(_take_blocks))

def nsa_attention(q, kc, vc, ksl, vsl, kwn, vwn, gate_logits, q_gain, k_gain, cmp_pos, cmp_w1, cmp_w2):
    b, s, _ = q.shape
    h, g, d = NSA_HEADS, NSA_KV_GROUPS, NSA_HEAD_DIM
    r = h // g
    scale = d ** -0.5
    cos, sin = rope_tables(s, d)
    q = apply_rope_2(rms_norm_2(q.reshape(b, s, h, d), q_gain), cos, sin).reshape(b, s, g, r, d)
    n_cmp = s // NSA_CMP_STRIDE - NSA_CMP_BLOCK // NSA_CMP_STRIDE + 1
    cmp_end = jnp.arange(n_cmp) * NSA_CMP_STRIDE + NSA_CMP_BLOCK - 1
    ck = compress_blocks(kc.reshape(b, s, g, d), cmp_pos[0], cmp_w1[0], cmp_w2[0])
    ck = apply_rope_2(rms_norm_2(ck, k_gain[0]), cos[cmp_end], sin[cmp_end])
    cv = compress_blocks(vc.reshape(b, s, g, d), cmp_pos[1], cmp_w1[1], cmp_w2[1])
    n_sel = s // NSA_SEL_BLOCK
    n_top = min(NSA_TOP_N, n_sel)
    ks_full = apply_rope_2(rms_norm_2(ksl.reshape(b, s, g, d), k_gain[1]), cos, sin)
    ks_blocks = ks_full.reshape(b, n_sel, NSA_SEL_BLOCK, g, d).transpose(0, 3, 1, 2, 4)
    vs_blocks = vsl.reshape(b, n_sel, NSA_SEL_BLOCK, g, d).transpose(0, 3, 1, 2, 4)
    overlap = nsa_overlap(n_cmp, n_sel)
    sel_idx = jnp.arange(n_sel)
    sel_start = sel_idx * NSA_SEL_BLOCK
    kw = apply_rope_2(rms_norm_2(kwn.reshape(b, s, g, d), k_gain[2]), cos, sin)
    pad_w = ((0, 0), (NSA_WINDOW, 0), (0, 0), (0, 0))
    kw_pad = jnp.pad(kw, pad_w)
    vw_pad = jnp.pad(vwn.reshape(b, s, g, d), pad_w)
    gates = jax.nn.sigmoid(gate_logits.astype(jnp.float32)).reshape(b, s, g, r, 3)
    nb = s // Q_BLOCK
    qb = q.reshape(b, nb, Q_BLOCK, g, r, d).transpose(1, 0, 2, 3, 4, 5)
    gb = gates.reshape(b, nb, Q_BLOCK, g, r, 3).transpose(1, 0, 2, 3, 4, 5)

    def one_block(args):
        q_blk, g_blk, blk = args
        q_pos = blk * Q_BLOCK + jnp.arange(Q_BLOCK)
        valid_c = cmp_end[None, :] <= q_pos[:, None]
        s_c = jnp.einsum('bqgrd,bngd->bgrqn', q_blk, ck).astype(jnp.float32) * scale
        p_c = jax.nn.softmax(jnp.where(valid_c, s_c, NEG_INF_2), axis=-1) * valid_c
        o_c = jnp.einsum('bgrqn,bngd->bqgrd', p_c.astype(cv.dtype), cv)
        imp = jnp.einsum('bgrqn,nj->bgqj', p_c, overlap)
        cur = (q_pos // NSA_SEL_BLOCK)[:, None]
        forced = (sel_idx[None, :] == 0) | (sel_idx[None, :] == cur) | (sel_idx[None, :] == cur - 1)
        future = sel_start[None, :] > q_pos[:, None]
        imp = jnp.where(future, -FORCE_SCORE, jnp.where(forced, FORCE_SCORE, imp))
        _, idx = lax.top_k(imp, n_top)
        k_sel = _gather_blocks(ks_blocks, idx).reshape(b, g, Q_BLOCK, n_top * NSA_SEL_BLOCK, d)
        v_sel = _gather_blocks(vs_blocks, idx).reshape(b, g, Q_BLOCK, n_top * NSA_SEL_BLOCK, d)
        pos_sel = (idx[..., None] * NSA_SEL_BLOCK + jnp.arange(NSA_SEL_BLOCK)).reshape(
            b, g, Q_BLOCK, n_top * NSA_SEL_BLOCK)
        valid_s = pos_sel <= q_pos[None, None, :, None]
        s_s = jnp.einsum('bqgrd,bgqkd->bgrqk', q_blk, k_sel).astype(jnp.float32) * scale
        p_s = jax.nn.softmax(jnp.where(valid_s[:, :, None], s_s, NEG_INF_2), axis=-1)
        o_s = jnp.einsum('bgrqk,bgqkd->bqgrd', p_s.astype(v_sel.dtype), v_sel)
        start = blk * Q_BLOCK
        k_win = lax.dynamic_slice_in_dim(kw_pad, start, NSA_WINDOW + Q_BLOCK, axis=1)
        v_win = lax.dynamic_slice_in_dim(vw_pad, start, NSA_WINDOW + Q_BLOCK, axis=1)
        pos_w = start - NSA_WINDOW + jnp.arange(NSA_WINDOW + Q_BLOCK)
        valid_w = ((pos_w[None, :] <= q_pos[:, None]) & (pos_w[None, :] > q_pos[:, None] - NSA_WINDOW)
                   & (pos_w[None, :] >= 0))
        s_w = jnp.einsum('bqgrd,bkgd->bgrqk', q_blk, k_win).astype(jnp.float32) * scale
        p_w = jax.nn.softmax(jnp.where(valid_w, s_w, NEG_INF_2), axis=-1)
        o_w = jnp.einsum('bgrqk,bkgd->bqgrd', p_w.astype(v_win.dtype), v_win)
        out = g_blk[..., 0:1] * o_c + g_blk[..., 1:2] * o_s + g_blk[..., 2:3] * o_w
        return out.astype(q_blk.dtype)

    o = lax.map(one_block, (qb, gb, jnp.arange(nb)))
    return o.transpose(1, 0, 2, 3, 4, 5).reshape(b, s, h * d)

def mla_attention(c_q, c_kv, k_rope, cq_gain, ckv_gain, w_uq, w_ukv, qn_gain, qr_gain, kn_gain, kr_gain):
    b, s, _ = c_q.shape
    h = MLA_HEADS
    cos, sin = rope_tables(s, MLA_ROPE_DIM)
    q = (rms_norm_2(c_q, cq_gain) @ w_uq).reshape(b, s, h, MLA_NOPE_DIM + MLA_ROPE_DIM)
    kv = (rms_norm_2(c_kv, ckv_gain) @ w_ukv).reshape(b, s, h, MLA_NOPE_DIM + MLA_V_DIM)
    q_nope = rms_norm_2(q[..., :MLA_NOPE_DIM], qn_gain)
    q_rope = apply_rope_2(rms_norm_2(q[..., MLA_NOPE_DIM:], qr_gain), cos, sin)
    k_nope = rms_norm_2(kv[..., :MLA_NOPE_DIM], kn_gain)
    v = kv[..., MLA_NOPE_DIM:]
    k_r = apply_rope_2(rms_norm_2(k_rope.reshape(b, s, 1, MLA_ROPE_DIM), kr_gain), cos, sin)
    q_full = jnp.concatenate([q_nope, q_rope], axis=-1)
    k_full = jnp.concatenate([k_nope, jnp.broadcast_to(k_r, (b, s, h, MLA_ROPE_DIM))], axis=-1)
    o = causal_attention_blocked(q_full, k_full, v, (MLA_NOPE_DIM + MLA_ROPE_DIM) ** -0.5)
    return o.reshape(b, s, h * MLA_V_DIM)

def moe_swiglu(h, router, w_gate, w_up, w_down):
    b, s, d = h.shape
    t = h.reshape(b * s, d)
    logits = (t @ router).astype(jnp.float32)
    top_val, top_idx = lax.top_k(logits, TOP_K)
    top_w = jax.nn.softmax(top_val, axis=-1)
    gates = jnp.sum(jax.nn.one_hot(top_idx, N_EXPERTS, dtype=jnp.float32) * top_w[..., None], axis=1)
    out = jnp.zeros_like(t)
    for e in range(N_EXPERTS):
        out = out + gates[:, e:e + 1].astype(t.dtype) * swiglu_2(t, w_gate[e], w_up[e], w_down[e])
    return out.reshape(b, s, d)

def second_inputs(seed: int = 0) -> dict:
    key = jax.random.key(seed)
    ks = jax.random.split(key, 40)
    f32 = jnp.float32
    n_ev = (DEPTH + 1) // 2
    n_od = DEPTH // 2

    def nrm(k, shape, scale):
        return jax.random.normal(k, shape, f32) * scale

    def gain(k, shape):
        return 1.0 + 0.1 * jax.random.normal(k, shape, f32)

    dt0 = jnp.exp(jax.random.uniform(ks[9], (n_ev, SSM_HEADS), f32, math.log(1e-3), math.log(1e-1)))
    return {
        'x': jax.random.normal(ks[0], (BATCH, SEQ, D_MODEL), f32),
        'ev_norm_mix': gain(ks[1], (n_ev, D_MODEL)),
        'ev_w_in': nrm(ks[2], (n_ev, D_MODEL, EVEN_IN), D_MODEL ** -0.5),
        'da_q_gain': gain(ks[3], (n_ev, DA_HEAD_DIM)),
        'da_k_gain': gain(ks[4], (n_ev, DA_HEAD_DIM)),
        'da_lambda': nrm(ks[5], (n_ev, 4, DA_HEAD_DIM), 0.1),
        'da_subln_gain': gain(ks[6], (n_ev, DA_V_DIM)),
        'ssm_conv_w': nrm(ks[7], (n_ev, SSM_CONV, SSM_CONV_CH), SSM_CONV ** -0.5),
        'ssm_conv_b': nrm(ks[8], (n_ev, SSM_CONV_CH), 0.02),
        'ssm_dt_bias': dt0 + jnp.log(-jnp.expm1(-dt0)),
        'ssm_a_log': jnp.log(jax.random.uniform(ks[10], (n_ev, SSM_HEADS), f32, 1.0, 16.0)),
        'ssm_d': gain(ks[11], (n_ev, SSM_HEADS)),
        'ssm_norm_gain': gain(ks[12], (n_ev, SSM_D_INNER)),
        'ev_w_out': nrm(ks[13], (n_ev, EVEN_MIX, D_MODEL), EVEN_MIX ** -0.5),
        'ev_norm_ffn': gain(ks[14], (n_ev, D_MODEL)),
        'ffn_w_gate': nrm(ks[15], (n_ev, D_MODEL, D_FF_2), D_MODEL ** -0.5),
        'ffn_w_up': nrm(ks[16], (n_ev, D_MODEL, D_FF_2), D_MODEL ** -0.5),
        'ffn_w_down': nrm(ks[17], (n_ev, D_FF_2, D_MODEL), D_FF_2 ** -0.5),
        'od_norm_mix': gain(ks[18], (n_od, D_MODEL)),
        'od_w_in': nrm(ks[19], (n_od, D_MODEL, ODD_IN), D_MODEL ** -0.5),
        'nsa_q_gain': gain(ks[20], (n_od, NSA_HEAD_DIM)),
        'nsa_k_gain': gain(ks[21], (n_od, 3, NSA_HEAD_DIM)),
        'nsa_cmp_pos': nrm(ks[22], (n_od, 2, NSA_CMP_BLOCK, NSA_HEAD_DIM), 0.1),
        'nsa_cmp_w1': nrm(ks[23], (n_od, 2, NSA_CMP_BLOCK * NSA_HEAD_DIM, NSA_HEAD_DIM),
                          (NSA_CMP_BLOCK * NSA_HEAD_DIM) ** -0.5),
        'nsa_cmp_w2': nrm(ks[24], (n_od, 2, NSA_HEAD_DIM, NSA_HEAD_DIM), NSA_HEAD_DIM ** -0.5),
        'mla_cq_gain': gain(ks[25], (n_od, MLA_Q_RANK)),
        'mla_ckv_gain': gain(ks[26], (n_od, MLA_KV_RANK)),
        'mla_w_uq': nrm(ks[27], (n_od, MLA_Q_RANK, MLA_HEADS * (MLA_NOPE_DIM + MLA_ROPE_DIM)), MLA_Q_RANK ** -0.5),
        'mla_w_ukv': nrm(ks[28], (n_od, MLA_KV_RANK, MLA_HEADS * (MLA_NOPE_DIM + MLA_V_DIM)), MLA_KV_RANK ** -0.5),
        'mla_qn_gain': gain(ks[29], (n_od, MLA_NOPE_DIM)),
        'mla_qr_gain': gain(ks[30], (n_od, MLA_ROPE_DIM)),
        'mla_kn_gain': gain(ks[31], (n_od, MLA_NOPE_DIM)),
        'mla_kr_gain': gain(ks[32], (n_od, MLA_ROPE_DIM)),
        'od_w_out': nrm(ks[33], (n_od, ODD_MIX, D_MODEL), ODD_MIX ** -0.5),
        'od_norm_ffn': gain(ks[34], (n_od, D_MODEL)),
        'moe_router': nrm(ks[35], (n_od, D_MODEL, N_EXPERTS), D_MODEL ** -0.5),
        'moe_w_gate': nrm(ks[36], (n_od, N_EXPERTS, D_MODEL, D_FF_2), D_MODEL ** -0.5),
        'moe_w_up': nrm(ks[37], (n_od, N_EXPERTS, D_MODEL, D_FF_2), D_MODEL ** -0.5),
        'moe_w_down': nrm(ks[38], (n_od, N_EXPERTS, D_FF_2, D_MODEL), D_FF_2 ** -0.5),
    }

def second_block(x, ev_norm_mix, ev_w_in, da_q_gain, da_k_gain, da_lambda, da_subln_gain,
              ssm_conv_w, ssm_conv_b, ssm_dt_bias, ssm_a_log, ssm_d, ssm_norm_gain,
              ev_w_out, ev_norm_ffn, ffn_w_gate, ffn_w_up, ffn_w_down,
              od_norm_mix, od_w_in, nsa_q_gain, nsa_k_gain, nsa_cmp_pos, nsa_cmp_w1, nsa_cmp_w2,
              mla_cq_gain, mla_ckv_gain, mla_w_uq, mla_w_ukv, mla_qn_gain, mla_qr_gain,
              mla_kn_gain, mla_kr_gain, od_w_out, od_norm_ffn,
              moe_router, moe_w_gate, moe_w_up, moe_w_down):
    for layer in range(DEPTH):
        i = layer // 2
        if layer % 2 == 0:
            h = rms_norm_2(x, ev_norm_mix[i])
            q, k, v, z, xbc, dt = split_cols(h @ ev_w_in[i], EVEN_SPLITS)
            a_out = diff_attention(q, k, v, da_q_gain[i], da_k_gain[i], da_lambda[i],
                                   da_subln_gain[i], layer)
            b_out = mamba2_ssd(z, xbc, dt, ssm_conv_w[i], ssm_conv_b[i], ssm_dt_bias[i],
                               ssm_a_log[i], ssm_d[i], ssm_norm_gain[i])
            x = x + jnp.concatenate([a_out, b_out], axis=-1) @ ev_w_out[i]
            x = x + swiglu_2(rms_norm_2(x, ev_norm_ffn[i]), ffn_w_gate[i], ffn_w_up[i], ffn_w_down[i])
        else:
            h = rms_norm_2(x, od_norm_mix[i])
            q, kc, vc, ksl, vsl, kwn, vwn, gl, cq, ckv, kr = split_cols(h @ od_w_in[i], ODD_SPLITS)
            c_out = nsa_attention(q, kc, vc, ksl, vsl, kwn, vwn, gl, nsa_q_gain[i], nsa_k_gain[i],
                                  nsa_cmp_pos[i], nsa_cmp_w1[i], nsa_cmp_w2[i])
            d_out = mla_attention(cq, ckv, kr, mla_cq_gain[i], mla_ckv_gain[i], mla_w_uq[i],
                                  mla_w_ukv[i], mla_qn_gain[i], mla_qr_gain[i], mla_kn_gain[i],
                                  mla_kr_gain[i])
            x = x + jnp.concatenate([c_out, d_out], axis=-1) @ od_w_out[i]
            x = x + moe_swiglu(rms_norm_2(x, od_norm_ffn[i]), moe_router[i], moe_w_gate[i],
                               moe_w_up[i], moe_w_down[i])
    return x


def setup_inputs(seed=0):
    out = dict(first_inputs(seed))
    for name, value in second_inputs(seed + 1).items():
        if name != "x":
            out[name + "_2"] = value
    return out


def reference(
    x, c, ctx, c_ctx, w_ada, b_ada, g_mix, g_ffn, w_in, q_norm, k_norm, sink, w_out, w_gate,
    w_up, w_down, g_final, ev_norm_mix_2, ev_w_in_2, da_q_gain_2, da_k_gain_2, da_lambda_2,
    da_subln_gain_2, ssm_conv_w_2, ssm_conv_b_2, ssm_dt_bias_2, ssm_a_log_2, ssm_d_2,
    ssm_norm_gain_2, ev_w_out_2, ev_norm_ffn_2, ffn_w_gate_2, ffn_w_up_2, ffn_w_down_2,
    od_norm_mix_2, od_w_in_2, nsa_q_gain_2, nsa_k_gain_2, nsa_cmp_pos_2, nsa_cmp_w1_2,
    nsa_cmp_w2_2, mla_cq_gain_2, mla_ckv_gain_2, mla_w_uq_2, mla_w_ukv_2, mla_qn_gain_2,
    mla_qr_gain_2, mla_kn_gain_2, mla_kr_gain_2, od_w_out_2, od_norm_ffn_2, moe_router_2,
    moe_w_gate_2, moe_w_up_2, moe_w_down_2,
):
    x = first_block(
        x, c, ctx, c_ctx, w_ada, b_ada, g_mix, g_ffn, w_in, q_norm, k_norm, sink, w_out, w_gate,
        w_up, w_down, g_final,
    )
    return second_block(
        x, ev_norm_mix_2, ev_w_in_2, da_q_gain_2, da_k_gain_2, da_lambda_2, da_subln_gain_2,
        ssm_conv_w_2, ssm_conv_b_2, ssm_dt_bias_2, ssm_a_log_2, ssm_d_2, ssm_norm_gain_2,
        ev_w_out_2, ev_norm_ffn_2, ffn_w_gate_2, ffn_w_up_2, ffn_w_down_2, od_norm_mix_2,
        od_w_in_2, nsa_q_gain_2, nsa_k_gain_2, nsa_cmp_pos_2, nsa_cmp_w1_2, nsa_cmp_w2_2,
        mla_cq_gain_2, mla_ckv_gain_2, mla_w_uq_2, mla_w_ukv_2, mla_qn_gain_2, mla_qr_gain_2,
        mla_kn_gain_2, mla_kr_gain_2, od_w_out_2, od_norm_ffn_2, moe_router_2, moe_w_gate_2,
        moe_w_up_2, moe_w_down_2,
    )


_drawn_inputs = setup_inputs


def setup_inputs(seed=0):
    import zlib

    import numpy as np

    out = dict(_drawn_inputs(seed))
    spreads = {}
    factors = {'g_mix': 2.932,
     'q_norm': 2.96,
     'k_norm': 3.81,
     'sink': 64.0,
     'nsa_q_gain_2': 4.528,
     'nsa_k_gain_2': 5.41,
     'mla_cq_gain_2': 3.252,
     'mla_qn_gain_2': 3.255,
     'mla_qr_gain_2': 3.277,
     'mla_kn_gain_2': 3.705,
     'mla_kr_gain_2': 4.889}
    for name, (base, spread) in spreads.items():
        noise = np.random.default_rng([zlib.crc32(name.encode()), seed]).standard_normal(out[name].shape)
        drawn = base * np.exp(spread * noise) if base else spread * noise
        out[name] = jnp.asarray(drawn.astype(out[name].dtype))
    for name, factor in factors.items():
        out[name] = (out[name] * factor).astype(out[name].dtype)
    return out
```

```python
import math

import numpy as np

import concourse.bass as bass
from concourse import mybir

F32 = mybir.dt.float32
U32 = mybir.dt.uint32
ALU = mybir.AluOpType
ACT = mybir.ActivationFunctionType
AX_X = mybir.AxisListType.X

P = 128
T = 256
NT = T // P
D = 1024
KT = D // P
HD = 64
F = 2816
FC = F // P
NE = 8
EPS = 1e-6
NEG = -1e30

RING = 6
SLOT = 3 * KT * P
PC = 256
AC = 384

A_COLS = 1536
E_COLS = 3080
O_COLS = 1752
SSM_H = 8
N_CMP = T // 16 - 1
LAM_INIT = 0.8 - 0.6 * math.exp(-0.3 * 0)


def pack(fields):
    at, where = 0, {}
    for name, n in fields:
        where[name] = (at, at + n)
        at += n
    return where, at


COLS, N_COLS = pack([("g_mix", 16), ("g_ffn", 16), ("ev_mix", 8), ("ev_ffn", 8), ("od_mix", 8),
                     ("od_ffn", 8), ("c", 16), ("conv_w", 32), ("conv_b", 8), ("cmp_pos", 64)])
ROWS1, N_ROWS1 = pack([("q_norm", 2 * HD), ("k_norm", 2 * HD), ("sink", 12), ("g_final", D)])
ROWS2, N_ROWS2 = pack([("da_q", HD), ("da_k", HD), ("da_lam", 4 * HD), ("subln", 128), ("dt_bias", 8),
                       ("a_log", 8), ("ssm_d", 8), ("ssm_norm", 512), ("nsa_q", HD), ("nsa_k", 3 * HD),
                       ("cq", 256), ("ckv", 128), ("qn", 128), ("qr", HD), ("kn", 128), ("kr", HD)])
N_ROWS = max(N_ROWS1, N_ROWS2)
CON1, N_CON1 = pack([("window", NT * 2 * T), ("dft_seq", NT * 2 * T), ("dft_cos", P), ("dft_sin", P),
                     ("rope_c", NT * HD), ("rope_s", NT * HD), ("sel2", 2 * P)])
CON2, N_CON2 = pack([("causal", NT * T), ("tri", NT * T), ("tri_mask", NT * T), ("rope_c", NT * HD),
                     ("rope_s", NT * HD), ("cmp_c", HD), ("cmp_s", HD), ("cmp_mask", NT * N_CMP),
                     ("cmp_valid", NT * N_CMP), ("iota", NE), ("sel8", NE * P)])
N_CON = max(N_CON1, N_CON2)


class Signal:

    def __init__(self, nc, name):
        self.sem, self.base = nc.alloc_semaphore(name), 0

    def __call__(self, n):
        return self.sem, self.base + n

    def passed(self, n):
        self.base += n


class Chain:

    def __init__(self, eng, steps):
        self.eng, self.steps = eng, steps

    def __call__(self, ins):
        ins.then_inc(self.steps.sem, 1)
        self.steps.passed(1)
        self.eng.wait_ge(*self.steps(0))


class Stream:

    def __init__(self, src, n, width):
        self.src, self.n, self.width = src, n, width


class Program:
    def __init__(self, nc, ap):
        self.nc, self.ap = nc, ap

        def sb(name, *shape):
            return nc.alloc_sbuf_tensor(name, [P, *shape], F32)

        self.ring = sb("ring", RING, SLOT)
        self.x = sb("x_res", NT, D)
        self.ctx = sb("ctx_res", NT, D)
        self.hT = sb("hT", KT, T)
        self.oT = sb("oT", KT, T)
        self.proj = sb("proj", NT, 2056)
        self.projc = sb("projc", NT, A_COLS)
        self.big = sb("big", 24 * T)
        self.work = sb("work", 3072)
        self.gates = sb("gates", 2, 2, D)
        self.cols = sb("cols", N_COLS)
        self.rows = sb("rows", N_ROWS)
        self.con = sb("con", N_CON)
        self.ident = sb("ident", P)
        self.mod = sb("mod", 32, 2)
        self.scl = sb("scl", 2, 2, KT)
        self.small = sb("small", 256)
        self.neg_half = sb("neg_half", 8)
        self.stat = sb("stat", 4, 4)
        self.side = sb("side", KT, NE)
        self.idx = nc.alloc_sbuf_tensor("idx", [P, 8], U32)
        self.ps = [nc.alloc_psum_tensor(f"bank{i}", [P, 512], F32) for i in range(8)]

        self.slot_loaded = [Signal(nc, f"slot_loaded{i}") for i in range(RING)]
        self.slot_free = Signal(nc, "slot_free")
        self.names = {}
        self.meansq, self.rstd, self.roots = Signal(nc, "meansq_ready"), Signal(nc, "rstd_ready"), 0
        self.streams, self.stream_at = [], 0
        self.used = 0
        self.preloaded = 0

    def sig(self, name):
        if name not in self.names:
            self.names[name] = Signal(self.nc, name)
        return self.names[name]

    def con_at(self, where, name, *shape):
        a, b = where[name]
        v = self.con[:, a:b]
        return v if not shape else v.rearrange("p (a b) -> p a b", a=shape[0])

    def row(self, where, name, i=0, n=None):
        a, b = where[name]
        n = n or b - a
        return self.rows[:, a + i * n:a + i * n + n]

    def col(self, name, i=0, n=KT):
        a = COLS[name][0]
        return self.cols[:, a + i * n:a + i * n + n]

    def load_chunk(self, sp, stream, c, g, turn=0, wait=True):
        slot = g % RING
        if wait:
            sp.wait_ge(self.slot_free.sem, turn * RING + (g - RING + 1))
        src = self.ap[stream.src]
        src = src[c] if isinstance(c, int) else src[bass.ds(c, 1)].rearrange("o p f -> (o p) f")
        sp.dma_start(self.ring[:, slot, 0:stream.width], src).then_inc(self.slot_loaded[slot].sem, 16)

    def load_stream(self, sp):
        s = self.streams[self.stream_at]
        g0, c = self.used, self.preloaded
        while g0 + c < RING:
            self.load_chunk(sp, s, c, g0 + c, wait=False)
            c += 1
        turns = (s.n - c) // RING
        if turns > 1:
            with sp.Fori(0, turns) as i:
                for r in range(RING):
                    self.load_chunk(sp, s, i * RING + (c + r), g0 + c + r, i)
            c += turns * RING
        for c in range(c, s.n):
            self.load_chunk(sp, s, c, g0 + c)
        self.preloaded = 0
        if self.stream_at + 1 < len(self.streams):
            after = self.streams[self.stream_at + 1]
            self.preloaded = min(RING, after.n)
            for c in range(self.preloaded):
                self.load_chunk(sp, after, c, g0 + s.n + c)

    def end_stream(self):
        s = self.streams[self.stream_at]
        self.used += s.n
        self.stream_at += 1

    def wait_chunk(self, pe, g, turn=0):
        pe.wait_ge(self.slot_loaded[g % RING].sem, 16 * turn + 16 * (g // RING + 1))


def load_small(p, jobs):
    done = p.sig("small_loaded")
    with p.nc.Block(no_gpsimd_drain=True) as block:
        @block.scalar
        def _(act):
            for dst, src in jobs:
                act.dma_start(dst, src).then_inc(done.sem, 16)
            act.wait_ge(*done(16 * len(jobs)))

        @block.vector
        def _(dve):
            chain = Chain(dve, p.sig("dve_chain"))
            chain(dve.memset(p.neg_half[:], -0.5))
    done.passed(16 * len(jobs))


def adaln(p, l):
    nc = p.nc
    mrow = p.big[0:2, 0:6 * D]
    cT = p.col("c", 0, 16).rearrange("p (k v) -> p k v", v=2)
    scT = p.small[:, 0:16].rearrange("p (k v) -> p k v", v=2)
    bias_in, silu_e, silu_done = p.sig("ada_bias_loaded"), p.sig("silu_exp"), p.sig("ada_silu")
    ready, added = p.sig("ada_chunk_ready"), p.sig("ada_chunk_added")
    turned, spread, copied = p.sig("ada_turned"), p.sig("ada_spread"), p.sig("ada_copied")
    n = 6 * D // AC
    g0 = p.used
    wanted = [8 * b + k for b in (0, 1, 3, 4) for k in range(8)]
    with nc.Block(no_gpsimd_drain=True) as block:
        @block.sync
        def _(sp):
            p.load_stream(sp)

        @block.scalar
        def _(act):
            act.dma_start(mrow, p.ap["b_ada"][l:l + 1, :].broadcast_to([2, 6 * D])).then_inc(bias_in.sem, 16)
            act.activation(p.small[:, 16:32], p.col("c", 0, 16), ACT.Exp, scale=-1.0).then_inc(silu_e.sem, 1)

        @block.tensor
        def _(pe):
            pe.wait_ge(*silu_done(1))
            for c in range(n):
                p.wait_chunk(pe, g0 + c)
                if c >= 2:
                    pe.wait_ge(*added(c - 1))
                w = p.ring[:, (g0 + c) % RING, 0:KT * AC].rearrange("p (k n) -> p k n", k=KT)
                for k in range(KT):
                    mm = pe.matmul(p.ps[c % 2][0:2, 0:AC], scT[:, k, :], w[:, k, :], start=k == 0, stop=k == KT - 1)
                mm.then_inc(ready.sem, 1)
                pe.wait_ge(*ready(c + 1))
                pe.sem_inc(p.slot_free.sem, 1)
            pe.wait_ge(*added(n))
            for j, f in enumerate(wanted):
                mm = pe.transpose(p.ps[2][:, 2 * j:2 * j + 2], mrow[:, f * P:f * P + P], p.ident[0:2, 0:2])
            mm.then_inc(turned.sem, 1)
            sel = p.con_at(CON1, "sel2", 2)
            for j in range(8):
                r, gt, hf = j // 4, (j // 2) % 2, j % 2
                if j >= 4:
                    pe.wait_ge(*copied(j - 3))
                a = (2 + 3 * gt) * D + hf * 512
                pe.matmul(p.ps[4 + j % 4][:, :], sel[0:2, r, :], mrow[:, a:a + 512], start=True,
                          stop=True).then_inc(spread.sem, 1)

        @block.vector
        def _(dve):
            chain = Chain(dve, p.sig("dve_chain"))
            dve.wait_ge(*silu_e(1))
            chain(dve.tensor_scalar(p.small[:, 16:32], p.small[:, 16:32], 1.0, None, ALU.add))
            chain(dve.reciprocal(p.small[:, 32:48], p.small[:, 16:32]))
            dve.tensor_tensor(p.small[:, 0:16], p.col("c", 0, 16), p.small[:, 32:48],
                              ALU.mult).then_inc(silu_done.sem, 1)
            dve.wait_ge(*bias_in(16))
            for c in range(n):
                dve.wait_ge(*ready(c + 1))
                m = mrow[:, c * AC:c * AC + AC]
                dve.tensor_tensor(m, m, p.ps[c % 2][0:2, 0:AC], ALU.add).then_inc(added.sem, 1)
            dve.wait_ge(*turned(1))
            mod = p.mod[:].rearrange("p f v -> p (f v)")
            chain(dve.tensor_copy(mod, p.ps[2][:, 0:64]))
            for i, name in enumerate(("g_mix", "g_ffn")):
                for r in range(2):
                    chain(dve.scalar_tensor_tensor(out=p.scl[:, i, r, :], in0=p.mod[:, 16 * i + 8:16 * i + 16, r],
                                                   scalar=1.0, in1=p.col(name, l), op0=ALU.add, op1=ALU.mult))
            for j in range(8):
                r, gt, hf = j // 4, (j // 2) % 2, j % 2
                dve.wait_ge(*spread(j + 1))
                dve.tensor_copy(p.gates[:, r, gt, hf * 512:hf * 512 + 512], p.ps[4 + j % 4][:, :]).then_inc(copied.sem, 1)
    for s, k in ((bias_in, 16), (silu_e, 1), (silu_done, 1), (ready, n), (added, n), (turned, 1), (spread, 8),
                 (copied, 8)):
        s.passed(k)
    p.slot_free.passed(n)
    p.end_stream()


def rsqrt(p, dve, st):
    p.meansq.passed(1)
    p.rstd.passed(1)
    dve.wait_ge(*p.rstd(0))


def rsqrts(p, pool, widths, parts=P):
    for w in widths:
        p.roots += 1
        pool.wait_ge(p.meansq.sem, p.roots)
        v = p.small[0:parts, 0:w]
        pool.tensor_tensor(v, v, p.neg_half[0:parts, 0:w], ALU.pow).then_inc(p.rstd.sem, 1)


def rstd_of(p, chain, dve, src, n, junk, out):
    heads = src.shape[1]
    sq = junk[:, 0:heads * n].rearrange("p (h d) -> p h d", h=heads)
    chain(dve.tensor_tensor(sq, src, src, ALU.mult))
    chain(dve.tensor_reduce(out, sq, AX_X, ALU.add))
    dve.tensor_scalar(out, out, 1.0 / n, EPS, ALU.mult, ALU.add).then_inc(p.meansq.sem, 1)
    rsqrt(p, dve, out)


def head_norm(p, chain, dve, src, gain, junk, stat):
    parts, heads, n = src.shape
    st = stat[:, 0:heads]
    rstd_of(p, chain, dve, src, n, junk, st)
    chain(dve.tensor_tensor(src, src, st.unsqueeze(2).broadcast_to([parts, heads, n]), ALU.mult))
    chain(dve.tensor_tensor(src, src, gain.unsqueeze(1).broadcast_to([parts, heads, n]), ALU.mult))


def rope(chain, dve, src, cos, sin, tmp):
    parts, heads, n = src.shape
    h = n // 2
    a = tmp[:, 0:heads * n].rearrange("p (h d) -> p h d", h=heads)
    b = tmp[:, heads * n:2 * heads * n].rearrange("p (h d) -> p h d", h=heads)

    def wide(t, k):
        return t.unsqueeze(1).broadcast_to([parts, heads, k])
    dve.tensor_tensor(b[:, :, 0:h], src[:, :, h:n], wide(sin[:, 0:h], h), ALU.mult)
    dve.tensor_tensor(b[:, :, h:n], src[:, :, 0:h], wide(sin[:, h:n], h), ALU.mult)
    chain(dve.tensor_tensor(a, src, wide(cos, n), ALU.mult))
    chain(dve.tensor_tensor(src, a, b, ALU.add))


def norm_to_hT(p, src, scale, bias=None):
    nc = p.nc
    xn = p.oT[:].rearrange("p k t -> p (k t)").rearrange("p (t d) -> p t d", t=NT)
    normed, turned, kept = p.sig("x_normed"), p.sig("x_turned"), p.sig("hT_kept")
    with nc.Block(no_gpsimd_drain=True) as block:
        @block.vector
        def _(dve):
            chain = Chain(dve, p.sig("dve_chain"))
            st = p.small[:, 0:NT]
            for t in range(NT):
                chain(dve.tensor_tensor_reduce(out=p.work[:, 0:D], in0=src[:, t, :], in1=src[:, t, :], scale=1.0,
                                               scalar=0.0, op0=ALU.mult, op1=ALU.add, accum_out=st[:, t:t + 1]))
            dve.tensor_scalar(st, st, 1.0 / D, EPS, ALU.mult, ALU.add).then_inc(p.meansq.sem, 1)
            rsqrt(p, dve, st)
            for t in range(NT):
                dve.tensor_scalar(xn[:, t, :], src[:, t, :], st[:, t:t + 1], None, ALU.mult).then_inc(normed.sem, 1)
            for k in range(KT):
                dve.wait_ge(*turned(k + 1))
                dve.tensor_scalar(p.hT[:, k, :], p.ps[k][:, 0:T], scale[:, k:k + 1],
                                  0.0 if bias is None else bias[:, k:k + 1], ALU.mult, ALU.add).then_inc(kept.sem, 1)

        @block.gpsimd
        def _(pool):
            rsqrts(p, pool, [NT])

        @block.tensor
        def _(pe):
            pe.wait_ge(*normed(NT))
            for k in range(KT):
                for t in range(NT):
                    mm = pe.transpose(p.ps[k][:, t * P:t * P + P], xn[:, t, k * P:k * P + P], p.ident[:, :])
                mm.then_inc(turned.sem, 1)
    normed.passed(NT)
    turned.passed(KT)
    kept.passed(KT)


def turn(p, groups):
    turned, kept_v, kept_a = p.sig("group_turned"), p.sig("group_kept_dve"), p.sig("group_kept_act")
    n = len(groups)
    with p.nc.Block(no_gpsimd_drain=True) as block:
        @block.tensor
        def _(pe):
            for j, (sources, _) in enumerate(groups):
                if j >= 4:
                    pe.wait_ge(*(kept_a if j % 2 else kept_v)((j - 4) // 2 + 1))
                for i, s in enumerate(sources):
                    parts, w = s.shape
                    mm = pe.transpose(p.ps[j % 4][0:w, i * P:i * P + parts], s, p.ident[0:parts, 0:parts])
                mm.then_inc(turned.sem, 1)

        @block.vector
        def _(dve):
            for j in range(0, n, 2):
                sources, dst = groups[j]
                dve.wait_ge(*turned(j + 1))
                dve.tensor_copy(dst, p.ps[j % 4][0:sources[0].shape[1], 0:dst.shape[1]]).then_inc(kept_v.sem, 1)

        @block.scalar
        def _(act):
            for j in range(1, n, 2):
                sources, dst = groups[j]
                act.wait_ge(*turned(j + 1))
                act.activation(dst, p.ps[j % 4][0:sources[0].shape[1], 0:dst.shape[1]],
                               ACT.Copy).then_inc(kept_a.sem, 1)
    turned.passed(n)
    kept_v.passed((n + 1) // 2)
    kept_a.passed(n // 2)


def linear(p, src, n_tok, n_feat=0, out=None, out_feat=None, residual=None, gate=None, side=None):
    nc = p.nc
    ready, taken = p.sig("chunk_ready"), p.sig("chunk_taken")
    n, g0 = n_tok + n_feat, p.used
    total = n + (1 if side is not None else 0)
    with nc.Block(no_gpsimd_drain=True) as block:
        @block.sync
        def _(sp):
            p.load_stream(sp)

        @block.tensor
        def _(pe):
            for c in range(n):
                bank = p.ps[c % 4]
                p.wait_chunk(pe, g0 + c)
                if c >= 4:
                    pe.wait_ge(*taken(c - 3))
                w = p.ring[:, (g0 + c) % RING, 0:KT * PC].rearrange("p (k n) -> p k n", k=KT)
                for m in range(2):
                    for k in range(KT):
                        if c < n_tok:
                            mm = pe.matmul(bank[:, m * PC:m * PC + PC], src[:, k, m * P:m * P + P], w[:, k, :],
                                           start=k == 0, stop=k == KT - 1)
                        else:
                            mm = pe.matmul(bank[:, m * T:m * T + T], w[:, k, m * P:m * P + P], src[:, k, :],
                                           start=k == 0, stop=k == KT - 1)
                mm.then_inc(ready.sem, 1)
                pe.wait_ge(*ready(c + 1))
                pe.sem_inc(p.slot_free.sem, 1)
            if side is not None:
                for m in range(NT):
                    for k in range(KT):
                        mm = pe.matmul(p.ps[4][:, m * NE:m * NE + NE], src[:, k, m * P:m * P + P], p.side[:, k, :],
                                       start=k == 0, stop=k == KT - 1)
                mm.then_inc(ready.sem, 1)

        @block.vector
        def _(dve):
            chain = Chain(dve, p.sig("dve_chain"))
            for c in range(n):
                dve.wait_ge(*ready(c + 1))
                bank = p.ps[c % 4][:, :].rearrange("p (m n) -> p m n", m=2)
                if c >= n_tok:
                    f = c - n_tok
                    dve.tensor_copy(out_feat[:, 2 * f:2 * f + 2, :], bank).then_inc(taken.sem, 1)
                    continue
                cut = slice(c * PC, c * PC + PC)
                if residual is None:
                    w = min(PC, out.shape[2] - c * PC)
                    dve.tensor_copy(out[:, :, c * PC:c * PC + w], bank[:, :, 0:w]).then_inc(taken.sem, 1)
                elif gate is None:
                    dve.tensor_tensor(residual[:, :, cut], residual[:, :, cut], bank, ALU.add).then_inc(taken.sem, 1)
                else:
                    y = p.work[:, 0:2 * PC].rearrange("p (m n) -> p m n", m=2)
                    chain(dve.tensor_tensor(y, bank, gate[:, cut].unsqueeze(1).broadcast_to([P, 2, PC]), ALU.mult))
                    chain(dve.tensor_tensor(residual[:, :, cut], residual[:, :, cut], y, ALU.add))
                    dve.sem_inc(taken.sem, 1)
            if side is not None:
                dve.wait_ge(*ready(n + 1))
                dve.tensor_copy(side, p.ps[4][:, 0:NT * NE].rearrange("p (m n) -> p m n", m=NT)).then_inc(taken.sem, 1)
    ready.passed(total)
    taken.passed(total)
    p.slot_free.passed(n)
    p.end_stream()


def ffn(p, residual, gate=None, experts=0, weight=None):
    nc = p.nc
    n = FC * max(experts, 1)
    g0 = p.used
    steps = 5 if experts else 4
    gu_ready, exp_ready, act_ready = p.sig("gate_up_ready"), p.sig("ffn_exp_ready"), p.sig("ffn_act_ready")
    dve_step, y_zero, y_ready = p.sig("ffn_dve_step"), p.sig("ffn_zero"), p.sig("ffn_y_ready")
    ex = p.work[:, 0:512].rearrange("p (b t) -> p b t", b=2)
    rc = p.work[:, 512:1024].rearrange("p (b t) -> p b t", b=2)
    aT = p.work[:, 1024:1536].rearrange("p (b t) -> p b t", b=2)
    turns = (n - 2) // RING

    def loop(eng, step):
        step(True, 0, 0)
        step(True, 0, 1)
        if turns:
            with eng.Fori(0, turns) as i:
                for r in range(RING):
                    step(False, i, 2 + r)
        for c in range(2 + turns * RING, n):
            step(False, 0, c)

    with nc.Block(no_gpsimd_drain=True) as block:
        @block.sync
        def _(sp):
            p.load_stream(sp)

        @block.tensor
        def _(pe):
            pe.wait_ge(*y_zero(1))
            for b in range(4):
                pe.matmul(p.ps[b][:, :], aT[:, 0, 0:P], p.work[:, 1024:1536], start=True, stop=False,
                          skip_group_check=True)

            def down(turn, c):
                g = g0 + c
                pe.wait_ge(act_ready.sem, turn * RING + (act_ready.base + c + 1))
                w = p.ring[:, g % RING, 2 * KT * P:3 * KT * P]
                for b in range(4):
                    mm = pe.matmul(p.ps[b][:, :], aT[:, c % 2, (b // 2) * P:(b // 2) * P + P],
                                   w[:, (b % 2) * 512:(b % 2) * 512 + 512], start=False, stop=False,
                                   skip_group_check=True)
                mm.then_inc(p.slot_free.sem, 1)

            def step(first, turn, c):
                g = g0 + c
                p.wait_chunk(pe, g, turn)
                if not first:
                    pe.wait_ge(act_ready.sem, turn * RING + (act_ready.base + c - 1))
                w = p.ring[:, g % RING, 0:2 * KT * P].rearrange("p (u k f) -> p u k f", u=2, k=KT)
                for u in range(2):
                    for k in range(KT):
                        mm = pe.matmul(p.ps[4 + c % 2][:, u * T:u * T + T], w[:, u, k, :], p.hT[:, k, :],
                                       start=k == 0, stop=k == KT - 1)
                mm.then_inc(gu_ready.sem, 1)
                if not first or c:
                    down(turn, c - 1)
            loop(pe, step)
            down(0, n - 1)
            for b in range(4):
                mm = pe.matmul(p.ps[b][:, :], p.work[:, 1536:1536 + P], p.work[:, 1536:2048], start=False, stop=True,
                               skip_group_check=True)
            mm.then_inc(y_ready.sem, 1)

        @block.scalar
        def _(act):
            def step(first, turn, c):
                act.wait_ge(gu_ready.sem, turn * RING + (gu_ready.base + c + 1))
                if not first:
                    act.wait_ge(act_ready.sem, turn * RING + (act_ready.base + c - 1))
                act.activation(ex[:, c % 2, :], p.ps[4 + c % 2][:, 0:T], ACT.Exp,
                               scale=-1.0).then_inc(exp_ready.sem, 1)
            loop(act, step)

        @block.vector
        def _(dve):
            dve.memset(p.work[:, 1024:2048], 0.0).then_inc(y_zero.sem, 1)

            def step(first, turn, c):
                e, r, a = ex[:, c % 2, :], rc[:, c % 2, :], aT[:, c % 2, :]
                bank = p.ps[4 + c % 2]
                k = [0]

                def then(ins):
                    k[0] += 1
                    ins.then_inc(dve_step.sem, 1)
                    dve.wait_ge(dve_step.sem, turn * (RING * (steps - 1)) + (dve_step.base + c * (steps - 1) + k[0]))
                dve.wait_ge(exp_ready.sem, turn * RING + (exp_ready.base + c + 1))
                then(dve.tensor_scalar(e, e, 1.0, None, ALU.add))
                then(dve.reciprocal(r, e))
                then(dve.tensor_tensor(r, r, bank[:, 0:T], ALU.mult))
                if experts:
                    w = turn * RING + c if not isinstance(turn, int) else c
                    expert = w // FC
                    gb = weight[:, expert, :] if isinstance(expert, int) else \
                        weight[:, bass.ds(expert, 1), :].rearrange("p o t -> p (o t)")
                    then(dve.tensor_tensor(r, r, gb, ALU.mult))
                if first:
                    dve.wait_ge(*y_zero(1))
                else:
                    dve.wait_ge(p.slot_free.sem, turn * RING + (g0 + c - 1))
                dve.tensor_tensor(a, r, bank[:, T:2 * T], ALU.mult).then_inc(act_ready.sem, 1)
            loop(dve, step)
            dve_step.passed(n * (steps - 1))
            chain = Chain(dve, p.sig("dve_chain"))
            dve.wait_ge(*y_ready(1))
            for b in range(4):
                r = residual[:, b // 2, (b % 2) * 512:(b % 2) * 512 + 512]
                if gate is None:
                    chain(dve.tensor_tensor(r, r, p.ps[b][:, :], ALU.add))
                else:
                    chain(dve.tensor_tensor(p.work[:, 0:512], p.ps[b][:, :],
                                            gate[:, (b % 2) * 512:(b % 2) * 512 + 512], ALU.mult))
                    chain(dve.tensor_tensor(r, r, p.work[:, 0:512], ALU.add))
    for s, k in ((gu_ready, n), (exp_ready, n), (act_ready, n), (y_zero, 1), (y_ready, 1)):
        s.passed(k)
    p.slot_free.passed(n)
    p.end_stream()


def attention(p, items):
    n = len(items)
    scores, negmax, probs = p.sig("scores_ready"), p.sig("negmax_ready"), p.sig("probs_ready")
    masked, sunk = p.sig("probs_masked"), p.sig("sink_ready")
    pt_ready, pt_kept, pv, done = p.sig("pt_ready"), p.sig("pt_kept"), p.sig("pv_ready"), p.sig("attn_out")
    S = p.work[:, 0:1024].rearrange("p (b n) -> p b n", b=2)
    E = p.work[:, 1024:2048].rearrange("p (b n) -> p b n", b=2)
    PT = p.work[:, 2048:3072].rearrange("p (b n) -> p b n", b=2)
    has_valid = any(it.get("valid") is not None for it in items)
    has_sink = any(it.get("sink") is not None for it in items)

    def nk(i):
        return items[i]["qk"][0][1].shape[1]

    def blocks(i):
        return [min(P, nk(i) - b) for b in range(0, nk(i), P)]

    with p.nc.Block(no_gpsimd_drain=True) as block:
        @block.tensor
        def _(pe):
            for i in range(n + 2):
                if i < n:
                    if i >= 2:
                        pe.wait_ge(*probs(i - 1))
                    qk = items[i]["qk"]
                    for j, (q, k) in enumerate(qk):
                        mm = pe.matmul(p.ps[i % 2][:, 0:nk(i)], q, k, start=j == 0, stop=j == len(qk) - 1)
                    mm.then_inc(scores.sem, 1)
                if 1 <= i <= n:
                    j = i - 1
                    pe.wait_ge(*(masked if has_valid else probs)(j + 1))
                    if j >= 2:
                        pe.wait_ge(*pt_kept(j - 1))
                    for b, w in enumerate(blocks(j)):
                        mm = pe.transpose(p.ps[2 + j % 2][0:w, b * P:b * P + P], E[:, j % 2, b * P:b * P + w],
                                          p.ident[:, :])
                    mm.then_inc(pt_ready.sem, 1)
                if i >= 2:
                    j = i - 2
                    pe.wait_ge(*pt_kept(j + 1))
                    if j >= 2:
                        pe.wait_ge(*done(j - 1))
                    bl, v = blocks(j), items[j]["v"]
                    for b, w in enumerate(bl):
                        mm = pe.matmul(p.ps[4 + j % 2][:, 0:v[b].shape[1]], PT[0:w, j % 2, b * P:b * P + P], v[b],
                                       start=b == 0, stop=b == len(bl) - 1)
                    mm.then_inc(pv.sem, 1)

        @block.vector
        def _(dve):
            chain = Chain(dve, p.sig("dve_chain"))
            for i in range(n + 2):
                if i < n:
                    it, st = items[i], p.stat[:, i % 4, :]
                    dve.wait_ge(*scores(i + 1))
                    s = p.ps[i % 2][:, 0:nk(i)]
                    if it.get("mask") is not None:
                        if i >= 2:
                            dve.wait_ge(*probs(i - 1))
                        chain(dve.tensor_tensor(S[:, i % 2, 0:nk(i)], s, it["mask"], ALU.add))
                        s = S[:, i % 2, 0:nk(i)]
                    chain(dve.tensor_reduce(st[:, 0:1], s, AX_X, ALU.max))
                    if it.get("sink") is not None:
                        chain(dve.tensor_scalar(st[:, 0:1], st[:, 0:1], it["scale"], it["sink"], ALU.mult, ALU.max))
                        dve.tensor_scalar(st[:, 1:2], st[:, 0:1], -1.0, None, ALU.mult).then_inc(negmax.sem, 1)
                    else:
                        dve.tensor_scalar(st[:, 1:2], st[:, 0:1], -it["scale"], None, ALU.mult).then_inc(negmax.sem, 1)
                    if has_valid:
                        dve.wait_ge(*probs(i + 1))
                        e = E[:, i % 2, 0:nk(i)]
                        dve.tensor_tensor(e, e, it["valid"], ALU.mult).then_inc(masked.sem, 1)
                if i >= 2:
                    it, st = items[i - 2], p.stat[:, (i - 2) % 4, :]
                    dve.wait_ge(*pv(i - 1))
                    if it.get("sink") is not None:
                        dve.wait_ge(*sunk(i - 1))
                        chain(dve.tensor_tensor(st[:, 2:3], st[:, 2:3], st[:, 3:4], ALU.add))
                    chain(dve.reciprocal(st[:, 0:1], st[:, 2:3]))
                    dve.tensor_scalar(it["out"], p.ps[4 + i % 2][:, 0:it["out"].shape[1]], st[:, 0:1], None,
                                      ALU.mult).then_inc(done.sem, 1)

        @block.scalar
        def _(act):
            for i in range(n + 1):
                if i < n:
                    it, st = items[i], p.stat[:, i % 4, :]
                    act.wait_ge(*negmax(i + 1))
                    if has_sink:
                        act.activation(st[:, 3:4], it["sink"], ACT.Exp, bias=st[:, 1:2]).then_inc(sunk.sem, 1)
                    if i >= 2:
                        act.wait_ge(*pt_ready(i - 1))
                    s = p.ps[i % 2][:, 0:nk(i)] if it.get("mask") is None else S[:, i % 2, 0:nk(i)]
                    act.activation(E[:, i % 2, 0:nk(i)], s, ACT.Exp, bias=st[:, 1:2], scale=it["scale"],
                                   accum_out=st[:, 2:3]).then_inc(probs.sem, 1)
                if i >= 1:
                    j = i - 1
                    act.wait_ge(*pt_ready(j + 1))
                    if j >= 2:
                        act.wait_ge(*pv(j - 1))
                    w = blocks(j)
                    act.activation(PT[0:w[0], j % 2, 0:len(w) * P], p.ps[2 + j % 2][0:w[0], 0:len(w) * P],
                                   ACT.Copy).then_inc(pt_kept.sem, 1)
    for s in (scores, negmax, probs, pt_ready, pt_kept, pv, done):
        s.passed(n)
    if has_valid:
        masked.passed(n)
    if has_sink:
        sunk.passed(n)


def heads_to_T(src, first, count, dst, d=HD, at=None):
    groups = []
    for h in range(0, count, 2):
        hs = range(h, min(h + 2, count))
        groups.append(([src[:, t, first + a * d:first + a * d + d] for a in hs for t in range(NT)],
                       dst(h, len(hs))))
    return groups


def qk_rope1(p, proj, l, rotate):
    with p.nc.Block(no_gpsimd_drain=True) as block:
        @block.gpsimd
        def _(pool):
            rsqrts(p, pool, [6, 2] * NT)

        @block.vector
        def _(dve):
            chain = Chain(dve, p.sig("dve_chain"))
            for t in range(NT):
                def heads(a, n):
                    return proj[:, t, a:a + n * HD].rearrange("p (h d) -> p h d", h=n)
                head_norm(p, chain, dve, heads(0, 6), p.row(ROWS1, "q_norm", l, HD), p.work[:], p.small[:])
                head_norm(p, chain, dve, heads(384, 2), p.row(ROWS1, "k_norm", l, HD), p.work[:], p.small[:])
                if rotate:
                    c = p.con_at(CON1, "rope_c", NT)[:, t, :]
                    s = p.con_at(CON1, "rope_s", NT)[:, t, :]
                    rope(chain, dve, heads(0, 8), c, s, p.work[:])
                    rope(chain, dve, heads(896, 8), c, s, p.work[:])


def fourier(p, proj):
    seq_done, seq_kept, out_done, out_kept = (p.sig("dft_seq"), p.sig("dft_seq_kept"), p.sig("dft_out"),
                                              p.sig("dft_out_kept"))
    dft = p.con_at(CON1, "dft_seq", NT)
    A = p.work[:, 0:1024].rearrange("p (c n) -> p c n", c=2)
    with p.nc.Block(no_gpsimd_drain=True) as block:
        @block.tensor
        def _(pe):
            for c in range(2):
                for t in range(NT):
                    mm = pe.matmul(p.ps[c][:, :], proj[:, t, 640 + c * P:640 + c * P + P], dft[:, t, :],
                                   start=t == 0, stop=t == NT - 1)
                mm.then_inc(seq_done.sem, 1)
            for c in range(2):
                pe.wait_ge(*seq_kept(c + 1))
                pe.matmul(p.ps[2 + c][:, 0:T], p.con_at(CON1, "dft_cos"), A[:, c, 0:T], start=True, stop=False)
                pe.matmul(p.ps[2 + c][:, 0:T], p.con_at(CON1, "dft_sin"), A[:, c, T:2 * T], start=False,
                          stop=True).then_inc(out_done.sem, 1)

        @block.vector
        def _(dve):
            for c in range(2):
                dve.wait_ge(*seq_done(c + 1))
                dve.tensor_copy(A[:, c, :], p.ps[c][:, :]).then_inc(seq_kept.sem, 1)
            for c in range(2):
                dve.wait_ge(*out_done(c + 1))
                dve.tensor_copy(p.oT[:, 3 + c, :], p.ps[2 + c][:, 0:T]).then_inc(out_kept.sem, 1)
    for s in (seq_done, seq_kept, out_done, out_kept):
        s.passed(2)


def o_groups(p, cuts):
    out = []
    for i in range(0, len(cuts), 2):
        two = cuts[i:i + 2]
        assert len(two) == 1 or two[1][0] == two[0][0] + 1
        out.append(([f(t) for _, f in two for t in range(NT)],
                    p.oT[:, two[0][0]:two[0][0] + len(two), :].rearrange("p k t -> p (k t)")))
    return out


def block1_attention(p, proj, l, x_tokens, both):
    kT = p.big[:, 12 * T:20 * T].rearrange("p (h n) -> p h n", h=4)
    qT = p.big[:, 0:12 * T].rearrange("p (h n) -> p h n", h=12)

    def q_dst(first):
        return lambda h, m: qT[0:HD, first + h:first + h + m, :].rearrange("p h t -> p (h t)")
    turn(p, heads_to_T(proj, 0, 6, q_dst(0)) + heads_to_T(proj, 896, 6, q_dst(6)))
    items = []
    for h in range(12):
        for t in range(NT):
            kv, window = h // 3, h >= 6
            v_at = 512 + 64 * kv if kv < 2 else 1408 + 64 * (kv - 2)
            q_at = h * HD if not window else 896 + (h - 6) * HD
            v = [p.projc[:, b, v_at:v_at + HD] for b in range(NT)]
            if x_tokens:
                v += [p.proj[:, b, v_at:v_at + HD] for b in range(NT)]
            it = dict(qk=[(qT[0:HD, h, t * P:t * P + P], kT[0:HD, kv, 0:len(v) * P])], v=v, scale=HD ** -0.5,
                      out=proj[:, t, q_at:q_at + HD])
            if window:
                it["sink"] = p.row(ROWS1, "sink")[:, l * 6 + h - 6:l * 6 + h - 5]
                if x_tokens:
                    it["mask"] = p.con_at(CON1, "window", NT)[:, t, :]
            items.append(it)
    attention(p, items[:12])
    attention(p, items[12:])


def block1_keys(p, proj, at):
    kT = p.big[:, 12 * T:20 * T].rearrange("p (h n) -> p h n", h=4)
    groups = []
    for g, first in enumerate((384, 1280)):
        for h in range(2):
            groups.append(([proj[:, t, first + h * HD:first + h * HD + HD] for t in range(NT)],
                           kT[0:HD, 2 * g + h, at:at + T]))
    turn(p, groups)


def block1_mix_out(p, proj, residual, gate):
    def cut(a):
        return lambda t: proj[:, t, a:a + P]
    turn(p, o_groups(p, [(0, cut(0)), (1, cut(P))]) + o_groups(p, [(2, cut(2 * P))])
         + o_groups(p, [(5, cut(896)), (6, cut(896 + P))]) + o_groups(p, [(7, cut(896 + 2 * P))]))
    linear(p, p.oT, 4, residual=residual, gate=gate)


def block1(p):
    x, ctx = p.x, p.ctx
    px = p.proj[:, :, 0:A_COLS]
    pc = p.projc[:]
    for l in range(2):
        adaln(p, l)
        norm_to_hT(p, x, p.scl[:, 0, 0, :], p.mod[:, 0:8, 0])
        linear(p, p.hT, 6, out=px)
        norm_to_hT(p, ctx, p.scl[:, 0, 1, :], p.mod[:, 0:8, 1])
        linear(p, p.hT, 6, out=pc)
        qk_rope1(p, px, l, True)
        qk_rope1(p, pc, l, False)
        block1_keys(p, pc, 0)
        block1_keys(p, px, T)
        block1_attention(p, px, l, True, True)
        fourier(p, px)
        block1_mix_out(p, px, x, p.gates[:, 0, 0, :])
        norm_to_hT(p, x, p.scl[:, 1, 0, :], p.mod[:, 16:24, 0])
        ffn(p, x, p.gates[:, 0, 1, :])
        if l == 0:
            block1_attention(p, pc, l, False, True)
            fourier(p, pc)
            block1_mix_out(p, pc, ctx, p.gates[:, 1, 0, :])
            norm_to_hT(p, ctx, p.scl[:, 1, 1, :], p.mod[:, 16:24, 1])
            ffn(p, ctx, p.gates[:, 1, 1, :])
    with p.nc.Block(no_gpsimd_drain=True) as block:
        @block.gpsimd
        def _(pool):
            rsqrts(p, pool, [1] * NT)

        @block.vector
        def _(dve):
            chain = Chain(dve, p.sig("dve_chain"))
            for t in range(NT):
                head_norm(p, chain, dve, x[:, t:t + 1, :], p.row(ROWS1, "g_final"), p.work[:], p.small[:])


def silu_by_parts(p, jobs):
    e = p.sig("silu_exp")
    with p.nc.Block(no_gpsimd_drain=True) as block:
        @block.scalar
        def _(act):
            for v, s in jobs:
                act.activation(s, v, ACT.Exp, scale=-1.0).then_inc(e.sem, 1)

        @block.vector
        def _(dve):
            chain = Chain(dve, p.sig("dve_chain"))
            for i, (v, s) in enumerate(jobs):
                dve.wait_ge(*e(i + 1))
                chain(dve.tensor_scalar(s, s, 1.0, None, ALU.add))
                chain(dve.reciprocal(s, s))
                chain(dve.tensor_tensor(v, v, s, ALU.mult))
    e.passed(len(jobs))


def rope_tables2(p, t):
    return p.con_at(CON2, "rope_c", NT)[:, t, :], p.con_at(CON2, "rope_s", NT)[:, t, :]


def diff_attention(p):
    proj = p.proj
    lam = p.small[:, 40:41]
    exp_ready = p.sig("lam_exp")
    dots_ready = p.sig("lam_dots")
    with p.nc.Block(no_gpsimd_drain=True) as block:
        @block.gpsimd
        def _(pool):
            rsqrts(p, pool, [8, 8] * NT)

        @block.vector
        def _(dve):
            chain = Chain(dve, p.sig("dve_chain"))
            lr = p.row(ROWS2, "da_lam").rearrange("p (a b d) -> p a b d", a=2, b=2)
            prod = p.work[:, 0:128].rearrange("p (a d) -> p a d", a=2)
            chain(dve.tensor_tensor(prod, lr[:, :, 0, :], lr[:, :, 1, :], ALU.mult))
            dve.tensor_reduce(p.small[:, 36:38], prod, AX_X, ALU.add).then_inc(dots_ready.sem, 1)
            dve.wait_ge(*dots_ready(1))
            for t in range(NT):
                def heads(a, n):
                    return proj[:, t, a:a + n * HD].rearrange("p (h d) -> p h d", h=n)
                head_norm(p, chain, dve, heads(0, 8), p.row(ROWS2, "da_q"), p.work[:], p.small[:])
                head_norm(p, chain, dve, heads(512, 8), p.row(ROWS2, "da_k"), p.work[:], p.small[:])
                rope(chain, dve, heads(0, 16), *rope_tables2(p, t), p.work[:])
            dve.wait_ge(*exp_ready(1))
            chain(dve.tensor_tensor(lam, p.small[:, 38:39], p.small[:, 39:40], ALU.subtract))
            chain(dve.tensor_scalar(lam, lam, LAM_INIT, None, ALU.add))

        @block.scalar
        def _(act):
            act.wait_ge(*dots_ready(1))
            act.activation(p.small[:, 38:40], p.small[:, 36:38], ACT.Exp).then_inc(exp_ready.sem, 1)
    exp_ready.passed(1)
    dots_ready.passed(1)
    qT = p.big[:, 0:8 * T].rearrange("p (h n) -> p h n", h=8)
    kT = p.big[:, 12 * T:20 * T].rearrange("p (h n) -> p h n", h=8)

    def to(dst):
        return lambda h, m: dst[0:HD, h:h + m, :].rearrange("p h t -> p (h t)")
    turn(p, heads_to_T(proj, 0, 8, to(qT)) + heads_to_T(proj, 512, 8, to(kT)))
    items = []
    for h in range(4):
        for c in range(2):
            for t in range(NT):
                n = (t + 1) * P
                items.append(dict(qk=[(qT[0:HD, 2 * h + c, t * P:t * P + P], kT[0:HD, 2 * h + c, 0:n])],
                                  v=[proj[:, b, 1024 + h * P:1024 + h * P + P] for b in range(t + 1)],
                                  mask=p.con_at(CON2, "causal", NT)[:, t, 0:n], scale=HD ** -0.5,
                                  out=proj[:, t, (2 * h + c) * P:(2 * h + c) * P + P]))
    attention(p, items)
    with p.nc.Block(no_gpsimd_drain=True) as block:
        @block.gpsimd
        def _(pool):
            rsqrts(p, pool, [4] * NT)

        @block.vector
        def _(dve):
            chain = Chain(dve, p.sig("dve_chain"))
            for t in range(NT):
                o = proj[:, t, 0:1024].rearrange("p (h c d) -> p h c d", h=4, c=2)
                w = p.work[:, 1024:1536].rearrange("p (h d) -> p h d", h=4)
                chain(dve.tensor_scalar(w, o[:, :, 1, :], lam, None, ALU.mult))
                chain(dve.tensor_tensor(w, o[:, :, 0, :], w, ALU.subtract))
                head_norm(p, chain, dve, w, p.row(ROWS2, "subln"), p.work[:], p.small[:])
                chain(dve.tensor_scalar(proj[:, t, 0:512].rearrange("p (h d) -> p h d", h=4), w, 1.0 - LAM_INIT, None,
                                        ALU.mult))


def mamba(p):
    nc = p.nc
    raw = p.projc[:].rearrange("p t c -> p (t c)")[:, 0:KT * T].rearrange("p (k t) -> p k t", k=KT)
    cv = p.hT
    xs = p.projc[:].rearrange("p t c -> p (t c)")[:, 2048:3072].rearrange("p (t c) -> p t c", t=NT)
    dt = p.small[:, 48:64].rearrange("p (t h) -> p t h", t=NT)
    tiny = [p.small[:, 64 + 16 * i:80 + 16 * i].rearrange("p (t h) -> p t h", t=NT) for i in range(8)]
    ad, ncs, u, z, z2, acc, neg_a, ex = tiny
    conv_w = p.col("conv_w", 0, 32).rearrange("p (k j) -> p k j", j=4)
    dt_u, dt_e = p.sig("dt_abs"), p.sig("dt_exp")
    with nc.Block(no_gpsimd_drain=True) as block:
        @block.vector
        def _(dve):
            chain = Chain(dve, p.sig("dve_chain"))
            bias = p.row(ROWS2, "dt_bias").unsqueeze(1).broadcast_to([P, NT, 8])
            chain(dve.tensor_tensor(dt, p.proj[:, :, 2048:2056], bias, ALU.add))
            chain(dve.tensor_scalar(u, dt, -1.0, None, ALU.mult))
            dve.tensor_tensor(u, u, dt, ALU.min).then_inc(dt_u.sem, 1)
            for k in range(KT):
                a, b = raw[:, k, :], cv[:, k, :]
                chain(dve.tensor_scalar(b, a, conv_w[:, k, 3:4], p.col("conv_b")[:, k:k + 1], ALU.mult, ALU.add))
                for j in range(1, 4):
                    chain(dve.scalar_tensor_tensor(out=b[:, j:T], in0=a[:, 0:T - j], scalar=conv_w[:, k, 3 - j:4 - j],
                                                   in1=b[:, j:T], op0=ALU.mult, op1=ALU.add))
            dve.wait_ge(*dt_e(2))
            chain(dve.tensor_scalar(z, ex, 2.0, None, ALU.add))
            chain(dve.reciprocal(z, z))
            chain(dve.tensor_tensor(z, z, ex, ALU.mult))
            chain(dve.tensor_tensor(z2, z, z, ALU.mult))
            chain(dve.tensor_scalar(acc, z2, 2.0 / 17, 2.0 / 15, ALU.mult, ALU.add))
            for m in (13, 11, 9, 7, 5, 3, 1):
                chain(dve.tensor_tensor(acc, acc, z2, ALU.mult))
                chain(dve.tensor_scalar(acc, acc, 2.0 / m, None, ALU.add))
            chain(dve.tensor_tensor(acc, acc, z, ALU.mult))
            chain(dve.tensor_scalar(dt, dt, 0.0, None, ALU.max))
            chain(dve.tensor_tensor(dt, dt, acc, ALU.add))
            chain(dve.tensor_tensor(ad, dt, neg_a[:, 0:1, :].broadcast_to([P, NT, 8]), ALU.mult))
            chain(dve.tensor_scalar(ad, ad, -1.0, None, ALU.mult))

        @block.scalar
        def _(act):
            act.wait_ge(*dt_u(1))
            act.activation(ex, u, ACT.Exp).then_inc(dt_e.sem, 1)
            act.activation(neg_a[:, 0, :], p.row(ROWS2, "a_log"), ACT.Exp).then_inc(dt_e.sem, 1)
    dt_u.passed(1)
    dt_e.passed(2)
    silu_by_parts(p, [(cv[:, 2 * k:2 * k + 2, :], raw[:, 2 * k:2 * k + 2, :]) for k in range(4)])
    turn(p, [([cv[:, k, t * P:t * P + P] for k in range(4)], xs[:, t, :]) for t in range(NT)])

    xdt = p.big[:, 0:1024].rearrange("p (t c) -> p t c", t=NT)
    y = p.big[:, 1024:2048].rearrange("p (t c) -> p t c", t=NT)
    adw = p.big[:, 2048:2048 + 2048].rearrange("p (t h m) -> p t h m", t=NT, h=8)
    dec = p.work[:, 0:512].rearrange("p (b n) -> p b n", b=2)
    MT = p.work[:, 1024:2048].rearrange("p (b s n) -> p b s n", b=2, s=2)
    tri = p.con_at(CON2, "tri", NT)
    mask = p.con_at(CON2, "tri_mask", NT)
    wide, sums, ncs_ready = p.sig("ad_wide"), p.sig("ssm_sums"), p.sig("ncs_ready")
    shifted, decayed, mt_ready, y_ready = (p.sig("decay_in"), p.sig("decay_out"), p.sig("mt_ready"), p.sig("ssm_y"))
    with nc.Block(no_gpsimd_drain=True) as block:
        @block.vector
        def _(dve):
            chain = Chain(dve, p.sig("dve_chain"))
            for t in range(NT):
                dve.tensor_copy(adw[:, t, :, :], ad[:, t, :].unsqueeze(2).broadcast_to([P, 8, P])).then_inc(wide.sem, 1)
            chain(dve.tensor_tensor(xdt[:].rearrange("p t (h d) -> p t h d", h=8),
                                    xs.rearrange("p t (h d) -> p t h d", h=8),
                                    dt.unsqueeze(3).broadcast_to([P, NT, 8, HD]), ALU.mult))
            dve.wait_ge(*sums(3))
            dve.tensor_scalar(ncs, p.ps[4][:, 0:16].rearrange("p (t h) -> p t h", t=NT), -1.0, None,
                              ALU.mult).then_inc(ncs_ready.sem, 1)

            def shift(i):
                h, s = i // 2, i % 2
                if i >= 2:
                    dve.wait_ge(*decayed(i - 1))
                dve.tensor_tensor(dec[:, s, :], p.ps[h // 2][:, (h % 2) * T:(h % 2) * T + T], mask[:, s, :],
                                  ALU.add).then_inc(shifted.sem, 1)
            shift(0)
            for i in range(16):
                if i + 1 < 16:
                    shift(i + 1)
                h, s = i // 2, i % 2
                dve.wait_ge(*decayed(i + 1))
                if h >= 2:
                    dve.wait_ge(*y_ready(h - 1))
                q = (h // 4) * 2 + s
                m = MT[:, h % 2, s, :]
                dve.tensor_tensor(m, m, p.ps[5 + q // 2][:, (q % 2) * T:(q % 2) * T + T],
                                  ALU.mult).then_inc(mt_ready.sem, 1)
            dve.wait_ge(*y_ready(8))
            for t in range(NT):
                h8 = [P, 8, HD]
                w = p.big[:, 4096:4608].rearrange("p (h d) -> p h d", h=8)
                chain(dve.tensor_tensor(w, xs[:, t, :].rearrange("p (h d) -> p h d", h=8),
                                        p.row(ROWS2, "ssm_d").unsqueeze(2).broadcast_to(h8), ALU.mult))
                chain(dve.tensor_tensor(y[:, t, :], p.big[:, 4096:4608], p.ps[7 if t == 0 else 4][:, :], ALU.add))

        @block.tensor
        def _(pe):
            pe.wait_ge(*wide(NT))
            for h in range(8):
                for t in range(NT):
                    mm = pe.matmul(p.ps[h // 2][:, (h % 2) * T:(h % 2) * T + T], adw[:, t, h, :], tri[:, t, :],
                                   start=t == 0, stop=t == NT - 1)
            mm.then_inc(sums.sem, 1)
            for q in range(4):
                g, s = q // 2, q % 2
                mm = pe.matmul(p.ps[5 + q // 2][:, (q % 2) * T:(q % 2) * T + T], cv[:, 4 + g, s * P:s * P + P],
                               cv[:, 6 + g, :], start=True, stop=True)
            mm.then_inc(sums.sem, 1)
            for lt in range(NT):
                for t in range(NT):
                    mm = pe.matmul(p.ps[4][:, lt * 8:lt * 8 + 8], tri[:, t, lt * P:lt * P + P], ad[:, t, :],
                                   start=t == 0, stop=t == NT - 1)
            mm.then_inc(sums.sem, 1)
            pe.wait_ge(*ncs_ready(1))
            for h in range(8):
                pe.wait_ge(*mt_ready(2 * h + 2))
                for lt in range(NT):
                    for s in range(NT):
                        mm = pe.matmul(p.ps[7 if lt == 0 else 4][:, h * HD:h * HD + HD],
                                       MT[:, h % 2, s, lt * P:lt * P + P], xdt[:, s, h * HD:h * HD + HD],
                                       start=s == 0, stop=s == NT - 1)
                mm.then_inc(y_ready.sem, 1)

        @block.scalar
        def _(act):
            act.wait_ge(*ncs_ready(1))
            for i in range(16):
                h, s = i // 2, i % 2
                act.wait_ge(*shifted(i + 1))
                if h >= 2:
                    act.wait_ge(*y_ready(h - 1))
                act.activation(MT[:, h % 2, s, :], dec[:, s, :], ACT.Exp,
                               bias=ncs[:, s, h:h + 1]).then_inc(decayed.sem, 1)
    for s, k in ((wide, NT), (sums, 3), (ncs_ready, 1), (shifted, 16), (decayed, 16), (mt_ready, 16), (y_ready, 8)):
        s.passed(k)
    silu_by_parts(p, [(p.proj[:, t, 1536:2048], p.work[:, t * 512:t * 512 + 512]) for t in range(NT)])
    with nc.Block(no_gpsimd_drain=True) as block:
        @block.gpsimd
        def _(pool):
            rsqrts(p, pool, [2] * NT)

        @block.vector
        def _(dve):
            chain = Chain(dve, p.sig("dve_chain"))
            for t in range(NT):
                chain(dve.tensor_tensor(y[:, t, :], y[:, t, :], p.proj[:, t, 1536:2048], ALU.mult))
                yg = y[:, t, :].rearrange("p (g d) -> p g d", g=2)
                rstd_of(p, chain, dve, yg, 256, p.work[:], p.small[:, 0:2])
                chain(dve.tensor_tensor(yg, yg, p.small[:, 0:2].unsqueeze(2).broadcast_to([P, 2, 256]), ALU.mult))
                chain(dve.tensor_tensor(y[:, t, :], y[:, t, :], p.row(ROWS2, "ssm_norm"), ALU.mult))
    return y


def even_layer(p):
    norm_to_hT(p, p.x, p.col("ev_mix"))
    raw = p.projc[:].rearrange("p t c -> p (t c)")[:, 0:KT * T].rearrange("p (k t) -> p k t", k=KT)
    linear(p, p.hT, 8, 4, out=p.proj[:, :, 0:2048], out_feat=raw, side=p.proj[:, :, 2048:2056])
    diff_attention(p)
    y = mamba(p)
    turn(p, o_groups(p, [(k, (lambda k: lambda t: p.proj[:, t, k * P:k * P + P])(k)) for k in range(4)])
         + o_groups(p, [(4 + k, (lambda k: lambda t: y[:, t, k * P:k * P + P])(k)) for k in range(4)]))
    linear(p, p.oT, 4, residual=p.x)
    norm_to_hT(p, p.x, p.col("ev_ffn"))
    ffn(p, p.x)


def nsa_compress(p, w1, w2):
    nc = p.nc
    kcT = p.big[0:HD, 2048:2048 + 4 * T].rearrange("p (k n) -> p k n", k=4)
    turn(p, heads_to_T(p.proj, 512, 4, lambda h, m: kcT[:, h:h + m, :].rearrange("p h t -> p (h t)")))
    flat = p.work[0:HD, 0:32 * 2 * N_CMP].rearrange("p (i g n) -> p i g n", i=32, g=2)
    posed, hid, act_exp, act_done = p.sig("cmp_posed"), p.sig("cmp_hidden"), p.sig("cmp_exp"), p.sig("cmp_act")
    out_ready, kept = p.sig("cmp_out"), p.sig("cmp_kept")
    hsb = p.work[0:HD, 1024:1024 + 3 * 2 * N_CMP].rearrange("p (a n) -> p a n", a=3)
    ckv = p.work[0:N_CMP, 1280:1280 + 4 * HD].rearrange("p (k g d) -> p k g d", k=2, g=2)
    ck_keep = p.big[0:N_CMP, 5120:5120 + 4 * HD].rearrange("p (k g d) -> p k g d", k=2, g=2)
    with nc.Block(no_gpsimd_drain=True) as block:
        @block.gpsimd
        def _(pool):
            rsqrts(p, pool, [2], parts=N_CMP)

        @block.vector
        def _(dve):
            chain = Chain(dve, p.sig("dve_chain"))
            for kind in range(2):
                pos = p.col("cmp_pos", kind, 32)[0:HD, :]
                if kind:
                    dve.wait_ge(*hid(1))
                for g in range(2):
                    for half in range(2):
                        src = kcT[:, 2 * kind + g, 16 * half:16 * half + 16 * N_CMP]\
                            .rearrange("p (n i) -> p i n", i=16)
                        dve.tensor_tensor(flat[:, 16 * half:16 * half + 16, g, :], src,
                                          pos[:, 16 * half:16 * half + 16].unsqueeze(2)
                                          .broadcast_to([HD, 16, N_CMP]), ALU.add).then_inc(posed.sem, 1)
                dve.wait_ge(*act_exp(kind + 1))
                chain(dve.tensor_scalar(hsb[:, 0, :], hsb[:, 0, :], 1.0, None, ALU.add))
                chain(dve.reciprocal(hsb[:, 1, :], hsb[:, 0, :]))
                dve.tensor_tensor(hsb[:, 2, :], hsb[:, 1, :], p.ps[0][0:HD, 0:2 * N_CMP],
                                  ALU.mult).then_inc(act_done.sem, 1)
                dve.wait_ge(*out_ready(kind + 1))
                chain(dve.tensor_copy(ck_keep[:, kind, :, :],
                                      p.ps[1][0:N_CMP, 0:2 * HD].rearrange("p (g d) -> p g d", g=2)))
                dve.sem_inc(kept.sem, 1)
            keys = ck_keep[:, 0, :, :]
            head_norm(p, chain, dve, keys, p.row(ROWS2, "nsa_k", 0, HD)[0:N_CMP, :], p.work[0:N_CMP, :],
                      p.small[0:N_CMP, :])
            rope(chain, dve, keys, p.con_at(CON2, "cmp_c")[0:N_CMP, :], p.con_at(CON2, "cmp_s")[0:N_CMP, :],
                 p.work[0:N_CMP, :])

        @block.tensor
        def _(pe):
            for kind in range(2):
                pe.wait_ge(*posed(4 * kind + 4))
                for i in range(32):
                    mm = pe.matmul(p.ps[0][0:HD, 0:2 * N_CMP], w1[:, kind, i, :],
                                   flat[:, i, :, :].rearrange("p g n -> p (g n)"), start=i == 0, stop=i == 31)
                mm.then_inc(hid.sem, 1)
                pe.wait_ge(*act_done(kind + 1))
                if kind:
                    pe.wait_ge(*kept(1))
                for g in range(2):
                    mm = pe.matmul(p.ps[1][0:N_CMP, g * HD:g * HD + HD], hsb[:, 2, g * N_CMP:g * N_CMP + N_CMP],
                                   w2[:, kind, :], start=True, stop=True)
                mm.then_inc(out_ready.sem, 1)

        @block.scalar
        def _(act):
            for kind in range(2):
                act.wait_ge(*hid(kind + 1))
                act.activation(hsb[:, 0, :], p.ps[0][0:HD, 0:2 * N_CMP], ACT.Exp, scale=-1.0).then_inc(act_exp.sem, 1)
    for s, k in ((posed, 8), (hid, 2), (act_exp, 2), (act_done, 2), (out_ready, 2), (kept, 2)):
        s.passed(k)
    ckT = p.big[0:HD, 5376:5376 + 256]
    turn(p, [([ck_keep[:, 0, g, :]], ckT[:, g * P:g * P + N_CMP]) for g in range(2)])
    return ck_keep, ckT


def nsa(p, w1, w2):
    proj = p.proj
    ck, ckT = nsa_compress(p, w1, w2)
    with p.nc.Block(no_gpsimd_drain=True) as block:
        @block.gpsimd
        def _(pool):
            rsqrts(p, pool, [8, 2, 2] * NT)

        @block.vector
        def _(dve):
            chain = Chain(dve, p.sig("dve_chain"))
            for t in range(NT):
                def heads(a, n):
                    return proj[:, t, a:a + n * HD].rearrange("p (h d) -> p h d", h=n)
                for a, n, gain in ((0, 8, p.row(ROWS2, "nsa_q")), (768, 2, p.row(ROWS2, "nsa_k", 1, HD)),
                                   (1024, 2, p.row(ROWS2, "nsa_k", 2, HD))):
                    head_norm(p, chain, dve, heads(a, n), gain, p.work[:], p.small[:])
                    rope(chain, dve, heads(a, n), *rope_tables2(p, t), p.work[:])
    qT = p.big[:, 0:8 * T].rearrange("p (h n) -> p h n", h=8)
    kT = p.big[:, 3072:3072 + 4 * T].rearrange("p (h n) -> p h n", h=4)

    def to(dst, first):
        return lambda h, m: dst[0:HD, first + h:first + h + m, :].rearrange("p h t -> p (h t)")
    turn(p, heads_to_T(proj, 0, 8, to(qT, 0)) + heads_to_T(proj, 768, 2, to(kT, 0))
         + heads_to_T(proj, 1024, 2, to(kT, 2)))
    ow = p.projc[:].rearrange("p t c -> p (t c)")[:, 0:2048].rearrange("p (w t c) -> p w t c", w=2, t=NT)
    items = []
    for h in range(8):
        for t in range(NT):
            g = h // 4
            items.append(dict(qk=[(qT[0:HD, h, t * P:t * P + P], ckT[:, g * P:g * P + N_CMP])],
                              v=[ck[:, 1, g, :]], mask=p.con_at(CON2, "cmp_mask", NT)[:, t, :],
                              valid=p.con_at(CON2, "cmp_valid", NT)[:, t, :], scale=HD ** -0.5,
                              out=proj[:, t, h * HD:h * HD + HD]))
    attention(p, items)
    items = []
    for w in range(2):
        for h in range(8):
            for t in range(NT):
                g, n = h // 4, (t + 1) * P
                a = 896 + 256 * w + g * HD
                items.append(dict(qk=[(qT[0:HD, h, t * P:t * P + P], kT[0:HD, 2 * w + g, 0:n])],
                                  v=[proj[:, b, a:a + HD] for b in range(t + 1)],
                                  mask=p.con_at(CON2, "causal", NT)[:, t, 0:n], scale=HD ** -0.5,
                                  out=ow[:, w, t, h * HD:h * HD + HD]))
    attention(p, items)
    gate_exp = p.sig("nsa_gate_exp")
    gx = p.small[:, 0:48].rearrange("p (t g) -> p t g", t=NT)
    with p.nc.Block(no_gpsimd_drain=True) as block:
        @block.scalar
        def _(act):
            act.activation(gx, proj[:, :, 1280:1304], ACT.Exp, scale=-1.0).then_inc(gate_exp.sem, 1)

        @block.vector
        def _(dve):
            chain = Chain(dve, p.sig("dve_chain"))
            dve.wait_ge(*gate_exp(1))
            chain(dve.tensor_scalar(gx, gx, 1.0, None, ALU.add))
            chain(dve.reciprocal(gx, gx))
            for t in range(NT):
                g3 = gx[:, t, :].rearrange("p (h c) -> p h c", c=3)
                outs = [v.rearrange("p (h d) -> p h d", h=8) for v in (proj[:, t, 0:512], ow[:, 0, t, :], ow[:, 1, t, :])]
                for c in range(3):
                    chain(dve.tensor_tensor(outs[c], outs[c], g3[:, :, c:c + 1].broadcast_to([P, 8, HD]), ALU.mult))
                chain(dve.tensor_tensor(outs[0], outs[0], outs[1], ALU.add))
                chain(dve.tensor_tensor(outs[0], outs[0], outs[2], ALU.add))
    gate_exp.passed(1)


def mla(p, w_uq, w_ukv):
    nc = p.nc
    proj = p.proj
    q = p.hT[:].rearrange("p k t -> p (k t)")[:, 0:1536].rearrange("p (t c) -> p t c", t=NT)
    flat = p.projc[:].rearrange("p t c -> p (t c)")
    kv = flat[:, 0:2048].rearrange("p (t c) -> p t c", t=NT)
    o = flat[:, 2048:3072].rearrange("p (t c) -> p t c", t=NT)
    big = p.big
    cT = big[:, 5120:5888].rearrange("p (k t) -> p k t", k=3)
    with nc.Block(no_gpsimd_drain=True) as block:
        @block.gpsimd
        def _(pool):
            rsqrts(p, pool, [1, 1, 1] * NT)

        @block.vector
        def _(dve):
            chain = Chain(dve, p.sig("dve_chain"))
            for t in range(NT):
                head_norm(p, chain, dve, proj[:, t:t + 1, 1304:1560], p.row(ROWS2, "cq"), p.work[:], p.small[:])
                head_norm(p, chain, dve, proj[:, t:t + 1, 1560:1688], p.row(ROWS2, "ckv"), p.work[:], p.small[:])
                head_norm(p, chain, dve, proj[:, t:t + 1, 1688:1752], p.row(ROWS2, "kr"), p.work[:], p.small[:])
                rope(chain, dve, proj[:, t:t + 1, 1688:1752], *rope_tables2(p, t), p.work[:])
    turn(p, [([proj[:, t, 1304 + k * P:1304 + k * P + P] for t in range(NT)], cT[:, k, :]) for k in range(3)])
    up, kept = p.sig("mla_up"), p.sig("mla_kept")
    jobs = []
    for t in range(NT):
        for c in range(2):
            jobs.append((q[:, t, c * 384:c * 384 + 384],
                         [(cT[:, k, t * P:t * P + P], w_uq[:, k, c * 384:c * 384 + 384]) for k in range(2)]))
            jobs.append((kv[:, t, c * 512:c * 512 + 512],
                         [(cT[:, 2, t * P:t * P + P], w_ukv[:, c * 512:c * 512 + 512])]))
    with nc.Block(no_gpsimd_drain=True) as block:
        @block.gpsimd
        def _(pool):
            rsqrts(p, pool, [4, 4, 4] * NT)

        @block.tensor
        def _(pe):
            for j, (dst, pairs) in enumerate(jobs):
                for i, (a, b) in enumerate(pairs):
                    mm = pe.matmul(p.ps[j][:, 0:dst.shape[1]], a, b, start=i == 0, stop=i == len(pairs) - 1)
                mm.then_inc(up.sem, 1)

        @block.vector
        def _(dve):
            chain = Chain(dve, p.sig("dve_chain"))
            for j, (dst, _) in enumerate(jobs):
                dve.wait_ge(*up(j + 1))
                chain(dve.tensor_copy(dst, p.ps[j][:, 0:dst.shape[1]]))
            for t in range(NT):
                qh = q[:, t, :].rearrange("p (h d) -> p h d", h=4)
                kh = kv[:, t, :].rearrange("p (h d) -> p h d", h=4)
                head_norm(p, chain, dve, qh[:, :, 0:128], p.row(ROWS2, "qn"), p.work[:], p.small[:])
                head_norm(p, chain, dve, qh[:, :, 128:192], p.row(ROWS2, "qr"), p.work[:], p.small[:])
                rope(chain, dve, qh[:, :, 128:192], *rope_tables2(p, t), p.work[:])
                head_norm(p, chain, dve, kh[:, :, 0:128], p.row(ROWS2, "kn"), p.work[:], p.small[:])
    up.passed(len(jobs))
    qn = big[:, 0:4 * T].rearrange("p (h n) -> p h n", h=4)
    kn = big[:, 4 * T:8 * T].rearrange("p (h n) -> p h n", h=4)
    qr = big[:, 8 * T:12 * T].rearrange("p (h n) -> p h n", h=4)
    kr = big[:, 12 * T:13 * T]

    def tiles(src, a, w):
        return [src[:, t, a:a + w] for t in range(NT)]
    turn(p, [(tiles(q, h * 192, 128), qn[:, h, :]) for h in range(4)]
         + [(tiles(kv, h * 256, 128), kn[:, h, :]) for h in range(4)]
         + [(tiles(q, h * 192 + 128, 64), qr[0:HD, h, :]) for h in range(4)]
         + [(tiles(proj, 1688, 64), kr[0:HD, :])])
    items = []
    for h in range(4):
        for t in range(NT):
            n = (t + 1) * P
            items.append(dict(qk=[(qn[:, h, t * P:t * P + P], kn[:, h, 0:n]),
                                  (qr[0:HD, h, t * P:t * P + P], kr[0:HD, 0:n])],
                              v=[kv[:, b, h * 256 + 128:h * 256 + 256] for b in range(t + 1)],
                              mask=p.con_at(CON2, "causal", NT)[:, t, 0:n], scale=192 ** -0.5,
                              out=o[:, t, h * P:h * P + P]))
    attention(p, items)
    return o


def route(p):
    nc = p.nc
    wide = p.big[:, 0:NE * T].rearrange("p (e t) -> p e t", e=NE)
    logits = p.small[:, 0:16].rearrange("p (t e) -> p t e", t=NT)
    top = p.small[:, 16:24]
    idx = p.small[:, 24:32]
    gates = p.small[:, 32:48].rearrange("p (t e) -> p t e", t=NT)
    gT = p.work[0:NE, 0:T]
    iota = p.con_at(CON2, "iota")
    logit, kept, diff, ex, gated = (p.sig("logits"), p.sig("logits_kept"), p.sig("top_diff"), p.sig("top_exp"),
                                    p.sig("gates_ready"))
    turned, gT_kept, spread, spread_kept = (p.sig("gates_turned"), p.sig("gates_kept"), p.sig("gates_spread"),
                                            p.sig("gates_wide"))
    with nc.Block(no_gpsimd_drain=True) as block:
        @block.tensor
        def _(pe):
            for t in range(NT):
                for k in range(KT):
                    mm = pe.matmul(p.ps[0][:, t * NE:t * NE + NE], p.hT[:, k, t * P:t * P + P], p.side[:, k, :],
                                   start=k == 0, stop=k == KT - 1)
            mm.then_inc(logit.sem, 1)
            pe.wait_ge(*gated(1))
            for t in range(NT):
                mm = pe.transpose(p.ps[1][0:NE, t * P:t * P + P], gates[:, t, :], p.ident[:, :])
            mm.then_inc(turned.sem, 1)
            pe.wait_ge(*gT_kept(1))
            sel = p.con_at(CON2, "sel8", NE)
            for e in range(NE):
                mm = pe.matmul(p.ps[2 + e // 2][:, (e % 2) * T:(e % 2) * T + T], sel[0:NE, e, :], gT, start=True, stop=True)
                if e % 2:
                    mm.then_inc(spread.sem, 1)

        @block.scalar
        def _(act):
            for t in range(NT):
                act.wait_ge(*diff(t + 1))
                act.activation(p.small[:, 49:50], p.small[:, 48:49], ACT.Exp).then_inc(ex.sem, 1)

        @block.vector
        def _(dve):
            chain = Chain(dve, p.sig("dve_chain"))
            dve.wait_ge(*logit(1))
            chain(dve.tensor_copy(logits, p.ps[0][:, 0:16].rearrange("p (t e) -> p t e", t=NT)))
            for t in range(NT):
                chain(dve.max(top, logits[:, t, :]))
                chain(dve.max_index(p.idx[:, :], top, logits[:, t, :]))
                chain(dve.tensor_copy(idx, p.idx[:, :]))
                dve.tensor_tensor(p.small[:, 48:49], top[:, 1:2], top[:, 0:1], ALU.subtract).then_inc(diff.sem, 1)
                dve.wait_ge(*ex(t + 1))
                chain(dve.tensor_scalar(p.small[:, 50:51], p.small[:, 49:50], 1.0, None, ALU.add))
                chain(dve.reciprocal(p.small[:, 50:51], p.small[:, 50:51]))
                chain(dve.tensor_tensor(p.small[:, 51:52], p.small[:, 50:51], p.small[:, 49:50], ALU.mult))
                chain(dve.tensor_scalar(gates[:, t, :], iota, idx[:, 0:1], p.small[:, 50:51], ALU.is_equal, ALU.mult))
                chain(dve.tensor_scalar(p.small[:, 52:60], iota, idx[:, 1:2], p.small[:, 51:52], ALU.is_equal, ALU.mult))
                chain(dve.tensor_tensor(gates[:, t, :], gates[:, t, :], p.small[:, 52:60], ALU.add))
            dve.sem_inc(gated.sem, 1)
            dve.wait_ge(*turned(1))
            dve.tensor_copy(gT, p.ps[1][0:NE, 0:T]).then_inc(gT_kept.sem, 1)
            for j in range(4):
                dve.wait_ge(*spread(j + 1))
                dve.tensor_copy(wide[:, 2 * j:2 * j + 2, :].rearrange("p e t -> p (e t)"),
                                p.ps[2 + j][:, :]).then_inc(spread_kept.sem, 1)
    for s, k in ((logit, 1), (kept, 0), (diff, 2), (ex, 2), (gated, 1), (turned, 1), (gT_kept, 1), (spread, 4),
                 (spread_kept, 4)):
        s.passed(k)
    return wide


def odd_layer(p):
    norm_to_hT(p, p.x, p.col("od_mix"))
    linear(p, p.hT, 7, out=p.proj[:, :, 0:O_COLS])
    w1 = p.gates[:].rearrange("p a b d -> p (a b d)")[0:HD, :].rearrange("p (k i j) -> p k i j", k=2, i=32)
    ctx = p.ctx[:].rearrange("p t d -> p (t d)")
    w2 = p.oT[:].rearrange("p k t -> p (k t)")[0:HD, 0:128].rearrange("p (k j) -> p k j", k=2)
    w_uq = p.oT[:].rearrange("p k t -> p (k t)")[:, 512:2048].rearrange("p (k c) -> p k c", k=2)
    w_ukv = ctx[:, 0:1024]
    load_small(p, [(w1, p.ap["cmp_w1"]), (w2, p.ap["cmp_w2"]), (w_uq, p.ap["w_uq"]), (w_ukv, p.ap["w_ukv"]),
                   (p.side[:], p.ap["router"])])
    nsa(p, w1, w2)
    o = mla(p, w_uq, w_ukv)
    turn(p, o_groups(p, [(k, (lambda k: lambda t: p.proj[:, t, k * P:k * P + P])(k)) for k in range(4)])
         + o_groups(p, [(4 + k, (lambda k: lambda t: o[:, t, k * P:k * P + P])(k)) for k in range(4)]))
    linear(p, p.oT, 4, residual=p.x)
    norm_to_hT(p, p.x, p.col("od_ffn"))
    weight = route(p)
    ffn(p, p.x, experts=NE, weight=weight)


def build(nc, ap, dbg=None, upto=None):
    p = Program(nc, ap)
    dense = SLOT
    p.streams = [
        Stream("w_ada0", 16, KT * AC), Stream("w_in0", 6, KT * PC), Stream("w_in0", 6, KT * PC),
        Stream("w_out0", 4, KT * PC), Stream("ffn0", FC, dense),
        Stream("w_out0", 4, KT * PC), Stream("ffn0", FC, dense),
        Stream("w_ada1", 16, KT * AC), Stream("w_in1", 6, KT * PC), Stream("w_in1", 6, KT * PC),
        Stream("w_out1", 4, KT * PC), Stream("ffn1", FC, dense),
        Stream("ev_in", 12, KT * PC), Stream("ev_out", 4, KT * PC), Stream("ffn_ev", FC, dense),
        Stream("od_in", 7, KT * PC), Stream("od_out", 4, KT * PC), Stream("moe", NE * FC, dense),
    ]
    load_small(p, [(p.x[:], ap["x"].rearrange("(t p) d -> p t d", p=P)),
                   (p.ctx[:], ap["ctx"].rearrange("(t p) d -> p t d", p=P)),
                   (p.cols[:], ap["cols"]), (p.ident[:], ap["ident"]), (p.side[:], ap["w_dt"]),
                   (p.con[:, 0:N_CON1], ap["con1"]),
                   (p.rows[:, 0:N_ROWS1], ap["rows1"].broadcast_to([P, N_ROWS1]))])
    block1(p)
    load_small(p, [(p.con[:, 0:N_CON2], ap["con2"]),
                   (p.rows[:, 0:N_ROWS2], ap["rows2"].broadcast_to([P, N_ROWS2]))])
    even_layer(p)
    odd_layer(p)
    stored = p.sig("stored")
    with nc.Block(no_gpsimd_drain=True) as block:
        @block.sync
        def _(sp):
            sp.dma_start(ap["out"].rearrange("(t p) d -> p t d", p=P), p.x[:]).then_inc(stored.sem, 16)
            sp.wait_ge(*stored(16))
    return p


def constants():
    f = np.float32
    q = np.arange(T)
    tile = lambda m: np.ascontiguousarray(m.reshape(NT, P, -1).transpose(1, 0, 2).reshape(P, -1)).astype(f)
    window = np.concatenate([np.zeros((T, T)), np.where(np.abs(q[None] - q[:, None]) <= 128, 0.0, NEG)], 1)
    ang = 2 * np.pi * (np.outer(q, q) % T) / T
    dft_seq = np.concatenate([np.cos(ang), np.sin(ang)], 1) / 16.0
    ch = np.arange(HD)
    a2 = 2 * np.pi * (np.outer(ch, ch) % HD) / HD
    two = np.eye(2)
    dft_cos, dft_sin = np.kron(two, np.cos(a2)) / 8.0, -np.kron(two, np.sin(a2)) / 8.0

    def tables(ang):
        c, s = np.cos(ang), np.sin(ang)
        return np.concatenate([c, c], 1), np.concatenate([-s, s], 1)
    inv1 = (f(10000.0) ** (-np.arange(0, 32, 2, dtype=f) / f(32))).astype(f)
    row, colp = (q // 64).astype(f), (q % 64).astype(f)
    c1, s1 = tables(np.concatenate([row[:, None] * inv1, colp[:, None] * inv1], 1).astype(f).astype(np.float64))
    inv2 = (f(1.0) / (f(10000.0) ** (np.arange(0, 64, 2, dtype=f) / f(64)))).astype(f)
    c2, s2 = tables((q.astype(f)[:, None] * inv2[None]).astype(f).astype(np.float64))
    end = np.arange(N_CMP) * 16 + 31
    pad = lambda m: np.concatenate([m, np.zeros((P - len(m), m.shape[1]))], 0).astype(f)
    valid = end[None] <= q[:, None]
    sel2 = pad(np.repeat(np.eye(2), P, 1))
    sel8 = pad(np.repeat(np.eye(NE), P, 1))
    tri = (q[:, None] <= q[None]).astype(f)
    con1 = np.concatenate([tile(window), tile(dft_seq), dft_cos.astype(f), dft_sin.astype(f), tile(c1), tile(s1),
                           sel2], 1)
    con2 = np.concatenate([tile(np.where(q[None] <= q[:, None], 0.0, NEG)), tile(tri), tile(np.where(tri > 0, 0.0, NEG)),
                           tile(c2), tile(s2), pad(c2[end]), pad(s2[end]), tile(np.where(valid, 0.0, NEG)),
                           tile(valid.astype(f)), np.tile(np.arange(NE, dtype=f), (P, 1)), sel8], 1)
    assert con1.shape[1] == N_CON1 and con2.shape[1] == N_CON2
    return con1, con2


def kernel(**inputs):
    import concourse.bacc as bacc
    from concourse.bass_utils import run_bass_kernel_spmd

    a = {k: np.asarray(v) for k, v in inputs.items()}
    arrays = {}

    def feature_columns(v):
        return v.reshape(-1, P).T

    def chunks(w, width):
        n = -(-w.shape[1] // width)
        if n * width != w.shape[1]:
            w = np.concatenate([w, np.zeros((w.shape[0], n * width - w.shape[1]), w.dtype)], 1)
        return np.ascontiguousarray(w.reshape(KT, P, n, width).transpose(2, 1, 0, 3).reshape(n, P, KT * width))

    def ffn_chunks(gate, up, down):
        n = gate.shape[-1] // P
        out = np.empty((n, P, 3, KT * P), gate.dtype)
        for i, w in enumerate((gate, up)):
            out[:, :, i].reshape(n, P, KT, P)[:] = w.reshape(KT, P, n, P).transpose(2, 1, 0, 3)
        out[:, :, 2] = down.reshape(n, P, D)
        return out.reshape(n, P, SLOT)

    arrays["x"] = a["x"].reshape(T, D)
    arrays["ctx"] = a["ctx"].reshape(T, D)
    arrays["b_ada"] = a["b_ada"]
    for l in range(2):
        arrays[f"w_ada{l}"] = chunks(a["w_ada"][l], AC)
        arrays[f"w_in{l}"] = chunks(a["w_in"][l], PC)
        arrays[f"w_out{l}"] = chunks(a["w_out"][l], PC)
        arrays[f"ffn{l}"] = ffn_chunks(a["w_gate"][l], a["w_up"][l], a["w_down"][l])
    ev = a["ev_w_in_2"][0]
    arrays["ev_in"] = chunks(ev[:, 0:3072], PC)
    arrays["w_dt"] = np.ascontiguousarray(ev[:, 3072:3080].reshape(KT, P, 8).transpose(1, 0, 2))
    arrays["ev_out"] = chunks(a["ev_w_out_2"][0], PC)
    arrays["ffn_ev"] = ffn_chunks(a["ffn_w_gate_2"][0], a["ffn_w_up_2"][0], a["ffn_w_down_2"][0])
    arrays["od_in"] = chunks(a["od_w_in_2"][0], PC)
    arrays["od_out"] = chunks(a["od_w_out_2"][0], PC)
    arrays["moe"] = np.concatenate([ffn_chunks(a["moe_w_gate_2"][0, e], a["moe_w_up_2"][0, e], a["moe_w_down_2"][0, e])
                                    for e in range(NE)])
    arrays["router"] = np.ascontiguousarray(a["moe_router_2"][0].reshape(KT, P, NE).transpose(1, 0, 2))
    arrays["cmp_w1"] = np.ascontiguousarray(a["nsa_cmp_w1_2"][0].reshape(2, 32, HD, HD).transpose(2, 0, 1, 3))
    arrays["cmp_w2"] = np.ascontiguousarray(a["nsa_cmp_w2_2"][0].transpose(1, 0, 2))
    arrays["w_uq"] = np.ascontiguousarray(a["mla_w_uq_2"][0].reshape(2, P, 768).transpose(1, 0, 2))
    arrays["w_ukv"] = a["mla_w_ukv_2"][0]
    pos = a["nsa_cmp_pos_2"][0].transpose(2, 0, 1).reshape(HD, 64)
    arrays["cols"] = np.concatenate([
        feature_columns(a["g_mix"]), feature_columns(a["g_ffn"]), feature_columns(a["ev_norm_mix_2"][0]),
        feature_columns(a["ev_norm_ffn_2"][0]), feature_columns(a["od_norm_mix_2"][0]),
        feature_columns(a["od_norm_ffn_2"][0]),
        np.stack([a["c"][0].reshape(KT, P), a["c_ctx"].reshape(KT, P)], -1).transpose(1, 0, 2).reshape(P, 16),
        a["ssm_conv_w_2"][0].reshape(4, KT, P).transpose(2, 1, 0).reshape(P, 32),
        feature_columns(a["ssm_conv_b_2"][0]), np.concatenate([pos, np.zeros_like(pos)], 0)], 1)
    arrays["rows1"] = np.concatenate([a[k].reshape(-1) for k in ("q_norm", "k_norm", "sink", "g_final")])[None]
    arrays["rows2"] = np.concatenate([a[k + "_2"].reshape(-1) for k in (
        "da_q_gain", "da_k_gain", "da_lambda", "da_subln_gain", "ssm_dt_bias", "ssm_a_log", "ssm_d",
        "ssm_norm_gain", "nsa_q_gain", "nsa_k_gain", "mla_cq_gain", "mla_ckv_gain", "mla_qn_gain", "mla_qr_gain",
        "mla_kn_gain", "mla_kr_gain")])[None]
    arrays["con1"], arrays["con2"] = constants()
    arrays["ident"] = np.eye(P, dtype=np.float32)

    nc = bacc.Bacc("TRN2", target_bir_lowering=False, num_devices=1)
    ap, maps = {}, {}
    for name, v in arrays.items():
        v = np.ascontiguousarray(v)
        maps[f"in_{name}"] = v
        ap[name] = nc.dram_tensor(f"in_{name}", v.shape, F32, kind="ExternalInput").ap()
    ap["out"] = nc.dram_tensor("out_x", (T, D), F32, kind="ExternalOutput").ap()
    build(nc, ap)
    r = run_bass_kernel_spmd(nc, [maps], core_ids=[0])
    return r.results[0]["out_x"].reshape(1, T, D)
```

```python
import math

import numpy as np

import concourse.bass as bass
from concourse import mybir

F32 = mybir.dt.float32
F32R = mybir.dt.float32r
U32 = mybir.dt.uint32
ALU = mybir.AluOpType
ACT = mybir.ActivationFunctionType
AX_X = mybir.AxisListType.X

P = 128
T = 256
NT = T // P
D = 1024
KT = D // P
HD = 64
F = 2816
FC = F // P
NE = 8
EPS = 1e-6
NEG = -1e30

RING = 4
SLOT = 3 * KT * P
PIECE = KT * P
PC = 256
AC = 384

A_COLS = 1536
E_COLS = 3080
O_COLS = 1752
SSM_H = 8
N_CMP = T // 16 - 1
LAM_INIT = 0.8 - 0.6 * math.exp(-0.3 * 0)


def pack(fields):
    at, where = 0, {}
    for name, n in fields:
        where[name] = (at, at + n)
        at += n
    return where, at


COLS, N_COLS = pack([("g_mix", 16), ("g_ffn", 16), ("ev_mix", 8), ("ev_ffn", 8), ("od_mix", 8),
                     ("od_ffn", 8), ("c", 16), ("conv_w", 32), ("conv_b", 8), ("cmp_pos", 64)])
ROWS1, N_ROWS1 = pack([("q_norm", 2 * HD), ("k_norm", 2 * HD), ("sink", 12), ("g_final", D)])
ROWS2, N_ROWS2 = pack([("da_q", HD), ("da_k", HD), ("da_lam", 4 * HD), ("subln", 128), ("dt_bias", 8),
                       ("a_log", 8), ("ssm_d", 8), ("nsa_q", HD), ("nsa_k", 3 * HD),
                       ("cq", 256), ("ckv", 128), ("qn", 128), ("qr", HD), ("kn", 128), ("kr", HD)])
N_ROWS = max(N_ROWS1, N_ROWS2)
CON1, N_CON1 = pack([("window", NT * 2 * T), ("dft_seq", NT * 2 * T), ("dft_cos", P), ("dft_sin", P),
                     ("rope_c", NT * HD), ("rope_s", NT * HD)])
CON2, N_CON2 = pack([("causal", NT * T), ("tri", NT * T), ("tri_mask", NT * T), ("rope_c", NT * HD),
                     ("rope_s", NT * HD), ("cmp_c", HD), ("cmp_s", HD), ("cmp_mask", NT * N_CMP),
                     ("cmp_valid", NT * N_CMP), ("iota", P)])
N_CON = max(N_CON1, N_CON2)


class Signal:

    def __init__(self, nc, name):
        self.sem, self.base = nc.alloc_semaphore(name), 0

    def __call__(self, n):
        return self.sem, self.base + n

    def passed(self, n):
        self.base += n


class Chain:

    def __init__(self, eng, steps):
        self.eng, self.steps = eng, steps

    def __call__(self, ins):
        ins.then_inc(self.steps.sem, 1)
        self.steps.passed(1)
        self.eng.wait_ge(*self.steps(0))


class Stream:

    def __init__(self, src, n, width):
        self.src, self.n, self.width = src, n, width


class Program:
    def __init__(self, nc, ap):
        self.nc, self.ap = nc, ap

        def sb(name, *shape):
            return nc.alloc_sbuf_tensor(name, [P, *shape], F32)

        self.ring = sb("ring", RING, SLOT)
        self.x = sb("x_res", NT, D)
        self.ctx = sb("ctx_res", NT, D)
        self.oT = sb("oT", KT, T)
        self.proj = sb("proj", NT, 2056)
        self.projc = sb("projc", NT, A_COLS)
        self.big = sb("big", 24 * T)
        self.srcH = nc.alloc_sbuf_tensor("src_hi", [P, KT, T], F32R)
        self.srcL = nc.alloc_sbuf_tensor("src_lo", [P, KT, T], F32R)
        self.actH = nc.alloc_sbuf_tensor("act_hi", [P, T], F32R)
        self.actL = nc.alloc_sbuf_tensor("act_lo", [P, T], F32R)
        self.sideH = nc.alloc_sbuf_tensor("side_hi", [P, KT, NE], F32R)
        self.sideL = nc.alloc_sbuf_tensor("side_lo", [P, KT, NE], F32R)
        self.wH = nc.alloc_sbuf_tensor("w_hi", [P, 3, PIECE], F32R)
        self.wL = nc.alloc_sbuf_tensor("w_lo", [P, 3, PIECE], F32R)
        self.work = sb("work", 3072)
        self.gates = sb("gates", 2, D)
        self.cols = sb("cols", N_COLS)
        self.rows = sb("rows", N_ROWS)
        self.con = sb("con", N_CON)
        self.xn = self.big[:, 4096:6144].rearrange("p (t d) -> p t d", t=NT)
        self.mod_rows = nc.dram_tensor("mod_rows", (2, 6 * D), F32, kind="Internal").ap()
        self.ident = sb("ident", P)
        self.mod = sb("mod", 32, 2)
        self.scl = sb("scl", 2, 2, KT)
        self.small = sb("small", 256)
        self.neg_half = sb("neg_half", 8)
        self.slot = sb("slot", NT, 2 * NE + 2)
        self.weight = sb("weight", NT, 2 * NE + 2)
        self.stat = sb("stat", 4, 4)
        self.side = sb("side", KT, NE)
        self.trip = nc.alloc_sbuf_tensor("trip", [P, 1], mybir.dt.int32)
        self.idx = nc.alloc_sbuf_tensor("idx", [P, 8], U32)
        self.ps = [nc.alloc_psum_tensor(f"bank{i}", [P, 512], F32) for i in range(8)]

        self.slot_loaded = [Signal(nc, f"slot_loaded{i}") for i in range(RING)]
        self.slot_free = Signal(nc, "slot_free")
        self.w_hi = [Signal(nc, f"w_hi{i}") for i in range(3)]
        self.w_lo = [Signal(nc, f"w_lo{i}") for i in range(3)]
        self.w_used = [Signal(nc, f"w_used{i}") for i in range(3)]
        self.names = {}
        self.meansq, self.rstd, self.roots = Signal(nc, "meansq_ready"), Signal(nc, "rstd_ready"), 0
        self.streams, self.stream_at = [], 0
        self.used = 0
        self.preloaded = 0

    def sig(self, name):
        if name not in self.names:
            self.names[name] = Signal(self.nc, name)
        return self.names[name]

    def con_at(self, where, name, *shape):
        a, b = where[name]
        v = self.con[:, a:b]
        return v if not shape else v.rearrange("p (a b) -> p a b", a=shape[0])

    def row(self, where, name, i=0, n=None):
        a, b = where[name]
        n = n or b - a
        return self.rows[:, a + i * n:a + i * n + n]

    def col(self, name, i=0, n=KT):
        a = COLS[name][0]
        return self.cols[:, a + i * n:a + i * n + n]

    def load_chunk(self, sp, stream, c, g, turn=0, wait=True):
        slot = g % RING
        if wait:
            sp.wait_ge(self.slot_free.sem, turn * RING + (g - RING + 1))
        src = self.ap[stream.src]
        src = src[c] if isinstance(c, int) else src[bass.ds(c, 1)].rearrange("o p f -> (o p) f")
        sp.dma_start(self.ring[:, slot, 0:stream.width], src).then_inc(self.slot_loaded[slot].sem, 16)

    def load_stream(self, sp):
        s = self.streams[self.stream_at]
        g0, c = self.used, self.preloaded
        while g0 + c < RING:
            self.load_chunk(sp, s, c, g0 + c, wait=False)
            c += 1
        turns = (s.n - c) // RING
        if turns > 1:
            with sp.Fori(0, turns) as i:
                for r in range(RING):
                    self.load_chunk(sp, s, i * RING + (c + r), g0 + c + r, i)
            c += turns * RING
        for c in range(c, s.n):
            self.load_chunk(sp, s, c, g0 + c)
        self.preloaded = 0
        if self.stream_at + 1 < len(self.streams):
            after = self.streams[self.stream_at + 1]
            self.preloaded = min(RING, after.n)
            for c in range(self.preloaded):
                self.load_chunk(sp, after, c, g0 + s.n + c)

    def end_stream(self):
        s = self.streams[self.stream_at]
        self.used += s.n
        self.stream_at += 1

    def wait_chunk(self, pe, g, turn=0):
        pe.wait_ge(self.slot_loaded[g % RING].sem, 16 * turn + 16 * (g // RING + 1))


def load_small(p, jobs):
    done = p.sig("small_loaded")
    with p.nc.Block(no_gpsimd_drain=True) as block:
        @block.scalar
        def _(act):
            for dst, src in jobs:
                act.dma_start(dst, src).then_inc(done.sem, 16)
            act.wait_ge(*done(16 * len(jobs)))

        @block.vector
        def _(dve):
            chain = Chain(dve, p.sig("dve_chain"))
            chain(dve.memset(p.neg_half[:], -0.5))
    done.passed(16 * len(jobs))


def start_gates(p, act, row):
    for i, a in enumerate((2 * D, 5 * D)):
        act.dma_start(p.gates[:, i, :], p.mod_rows[row:row + 1, a:a + D].broadcast_to([P, D])
                      ).then_inc(p.sig("gates_loaded").sem, 16)


def load_gates(p, row):
    with p.nc.Block(no_gpsimd_drain=True) as block:
        @block.scalar
        def _(act):
            start_gates(p, act, row)
            act.wait_ge(*p.sig("gates_loaded")(32))
    p.sig("gates_loaded").passed(32)


def adaln(p, l):
    nc = p.nc
    mrow = p.big[0:2, 0:6 * D]
    cT = p.col("c", 0, 16).rearrange("p (k v) -> p k v", v=2)
    scT = p.small[:, 0:16].rearrange("p (k v) -> p k v", v=2)
    bias_in, silu_e, silu_done = p.sig("ada_bias_loaded"), p.sig("silu_exp"), p.sig("ada_silu")
    ready, added = p.sig("ada_chunk_ready"), p.sig("ada_chunk_added")
    turned, rows_out = p.sig("ada_turned"), p.sig("mod_rows_out")
    n = 6 * D // AC
    g0 = p.used
    wanted = [8 * b + k for b in (0, 1, 3, 4) for k in range(8)]
    with nc.Block(no_gpsimd_drain=True) as block:
        @block.sync
        def _(sp):
            p.load_stream(sp)

        @block.scalar
        def _(act):
            act.dma_start(mrow, p.ap["b_ada"][l:l + 1, :].broadcast_to([2, 6 * D])).then_inc(bias_in.sem, 16)
            act.activation(p.small[:, 16:32], p.col("c", 0, 16), ACT.Exp, scale=-1.0).then_inc(silu_e.sem, 1)
            act.wait_ge(*added(n))
            act.dma_start(p.mod_rows, mrow).then_inc(rows_out.sem, 16)
            act.wait_ge(*rows_out(16))
            start_gates(p, act, 0)
            act.wait_ge(*p.sig("gates_loaded")(32))

        @block.tensor
        def _(pe):
            pe.wait_ge(*silu_done(1))
            for c in range(n):
                p.wait_chunk(pe, g0 + c)
                if c >= 2:
                    pe.wait_ge(*added(c - 1))
                w = p.ring[:, (g0 + c) % RING, 0:KT * AC].rearrange("p (k n) -> p k n", k=KT)
                for k in range(KT):
                    mm = pe.matmul(p.ps[c % 2][0:2, 0:AC], scT[:, k, :], w[:, k, :], start=k == 0, stop=k == KT - 1)
                mm.then_inc(ready.sem, 1)
                pe.wait_ge(*ready(c + 1))
                pe.sem_inc(p.slot_free.sem, 1)
            pe.wait_ge(*added(n))
            for j, f in enumerate(wanted):
                mm = pe.transpose(p.ps[2][:, 2 * j:2 * j + 2], mrow[:, f * P:f * P + P], p.ident[0:2, 0:2])
            mm.then_inc(turned.sem, 1)

        @block.vector
        def _(dve):
            chain = Chain(dve, p.sig("dve_chain"))
            dve.wait_ge(*silu_e(1))
            chain(dve.tensor_scalar(p.small[:, 16:32], p.small[:, 16:32], 1.0, None, ALU.add))
            chain(dve.reciprocal(p.small[:, 32:48], p.small[:, 16:32]))
            dve.tensor_tensor(p.small[:, 0:16], p.col("c", 0, 16), p.small[:, 32:48],
                              ALU.mult).then_inc(silu_done.sem, 1)
            dve.wait_ge(*bias_in(16))
            for c in range(n):
                dve.wait_ge(*ready(c + 1))
                m = mrow[:, c * AC:c * AC + AC]
                dve.tensor_tensor(m, m, p.ps[c % 2][0:2, 0:AC], ALU.add).then_inc(added.sem, 1)
            dve.wait_ge(*turned(1))
            mod = p.mod[:].rearrange("p f v -> p (f v)")
            chain(dve.tensor_copy(mod, p.ps[2][:, 0:64]))
            for i, name in enumerate(("g_mix", "g_ffn")):
                for r in range(2):
                    chain(dve.scalar_tensor_tensor(out=p.scl[:, i, r, :], in0=p.mod[:, 16 * i + 8:16 * i + 16, r],
                                                   scalar=1.0, in1=p.col(name, l), op0=ALU.add, op1=ALU.mult))
    for s, k in ((bias_in, 16), (silu_e, 1), (silu_done, 1), (ready, n), (added, n), (turned, 1), (rows_out, 16),
                 (p.sig("gates_loaded"), 32)):
        s.passed(k)
    p.slot_free.passed(n)
    p.end_stream()


def rsqrt(p, dve, st):
    p.meansq.passed(1)
    p.rstd.passed(1)
    dve.wait_ge(*p.rstd(0))


def rsqrts(p, pool, widths, parts=P):
    for w in widths:
        p.roots += 1
        pool.wait_ge(p.meansq.sem, p.roots)
        v = p.small[0:parts, 0:w]
        pool.tensor_tensor(v, v, p.neg_half[0:parts, 0:w], ALU.pow).then_inc(p.rstd.sem, 1)


def rstd_of(p, chain, dve, src, n, junk, out):
    heads = src.shape[1]
    sq = junk[:, 0:heads * n].rearrange("p (h d) -> p h d", h=heads)
    chain(dve.tensor_tensor(sq, src, src, ALU.mult))
    chain(dve.tensor_reduce(out, sq, AX_X, ALU.add))
    dve.tensor_scalar(out, out, 1.0 / n, EPS, ALU.mult, ALU.add).then_inc(p.meansq.sem, 1)
    rsqrt(p, dve, out)


def head_norm(p, chain, dve, src, gain, junk, stat):
    parts, heads, n = src.shape
    st = stat[:, 0:heads]
    rstd_of(p, chain, dve, src, n, junk, st)
    chain(dve.tensor_tensor(src, src, st.unsqueeze(2).broadcast_to([parts, heads, n]), ALU.mult))
    chain(dve.tensor_tensor(src, src, gain.unsqueeze(1).broadcast_to([parts, heads, n]), ALU.mult))


def rope(chain, dve, src, cos, sin, tmp):
    parts, heads, n = src.shape
    h = n // 2
    a = tmp[:, 0:heads * n].rearrange("p (h d) -> p h d", h=heads)
    b = tmp[:, heads * n:2 * heads * n].rearrange("p (h d) -> p h d", h=heads)

    def wide(t, k):
        return t.unsqueeze(1).broadcast_to([parts, heads, k])
    dve.tensor_tensor(b[:, :, 0:h], src[:, :, h:n], wide(sin[:, 0:h], h), ALU.mult)
    dve.tensor_tensor(b[:, :, h:n], src[:, :, 0:h], wide(sin[:, h:n], h), ALU.mult)
    chain(dve.tensor_tensor(a, src, wide(cos, n), ALU.mult))
    chain(dve.tensor_tensor(src, a, b, ALU.add))


def norm_src(p, src, scale, bias=None):
    nc = p.nc
    xn, h = p.xn, p.work[:, 0:KT * T].rearrange("p (k t) -> p k t", k=KT)
    normed, turned, kept, hi, lo = (p.sig("x_normed"), p.sig("x_turned"), p.sig("h_kept"), p.sig("src_hi_ready"),
                                    p.sig("src_ready"))
    with nc.Block(no_gpsimd_drain=True) as block:
        @block.vector
        def _(dve):
            chain = Chain(dve, p.sig("dve_chain"))
            st = p.small[:, 0:NT]
            chain(dve.tensor_tensor_reduce(out=p.work[:, 0:D], in0=src[:, 0, :], in1=src[:, 0, :], scale=1.0,
                                           scalar=0.0, op0=ALU.mult, op1=ALU.add, accum_out=st[:, 0:1]))
            dve.wait_ge(*p.sig("square_sum")(1))
            dve.tensor_scalar(st, st, 1.0 / D, EPS, ALU.mult, ALU.add).then_inc(p.meansq.sem, 1)
            rsqrt(p, dve, st)
            dve.tensor_scalar(xn[:, 0, :], src[:, 0, :], st[:, 0:1], None, ALU.mult).then_inc(normed.sem, 1)

            def low(k):
                dve.wait_ge(*hi(k + 1))
                dve.tensor_tensor(p.srcL[:, k, :], h[:, k, :], p.srcH[:, k, :].bitcast(F32),
                                  ALU.subtract).then_inc(lo.sem, 1)
            for k in range(KT):
                dve.wait_ge(*turned(k + 1))
                dve.tensor_scalar(h[:, k, :], p.ps[k][:, 0:T], scale[:, k:k + 1],
                                  0.0 if bias is None else bias[:, k:k + 1], ALU.mult, ALU.add).then_inc(kept.sem, 1)
                if k:
                    low(k - 1)
            low(KT - 1)

        @block.gpsimd
        def _(pool):
            rsqrts(p, pool, [NT])

        @block.scalar
        def _(act):
            act.activation(p.work[:, D:2 * D], src[:, 1, :], ACT.Square,
                           accum_out=p.small[:, 1:2]).then_inc(p.sig("square_sum").sem, 1)
            act.wait_ge(*p.rstd(0))
            act.activation(xn[:, 1, :], src[:, 1, :], ACT.Identity, scale=p.small[:, 1:2]).then_inc(normed.sem, 1)
            for k in range(KT):
                act.wait_ge(*kept(k + 1))
                act.activation(p.srcH[:, k, :], h[:, k, :], ACT.Copy).then_inc(hi.sem, 1)

        @block.tensor
        def _(pe):
            pe.wait_ge(*normed(NT))
            for k in range(KT):
                for t in range(NT):
                    mm = pe.transpose(p.ps[k][:, t * P:t * P + P], xn[:, t, k * P:k * P + P], p.ident[:, :])
                mm.then_inc(turned.sem, 1)
    normed.passed(NT)
    p.sig("square_sum").passed(1)
    for s in (turned, kept, hi, lo):
        s.passed(KT)


def turn(p, groups):
    turned, kept_v, kept_a = p.sig("group_turned"), p.sig("group_kept_dve"), p.sig("group_kept_act")
    n = len(groups)
    with p.nc.Block(no_gpsimd_drain=True) as block:
        @block.tensor
        def _(pe):
            for j, (sources, _) in enumerate(groups):
                if j >= 4:
                    pe.wait_ge(*(kept_a if j % 2 else kept_v)((j - 4) // 2 + 1))
                for i, s in enumerate(sources):
                    parts, w = s.shape
                    mm = pe.transpose(p.ps[j % 4][0:w, i * P:i * P + parts], s, p.ident[0:parts, 0:parts])
                mm.then_inc(turned.sem, 1)

        @block.vector
        def _(dve):
            for j in range(0, n, 2):
                sources, dst = groups[j]
                dve.wait_ge(*turned(j + 1))
                dve.tensor_copy(dst, p.ps[j % 4][0:sources[0].shape[1], 0:dst.shape[1]]).then_inc(kept_v.sem, 1)

        @block.scalar
        def _(act):
            for j in range(1, n, 2):
                sources, dst = groups[j]
                act.wait_ge(*turned(j + 1))
                act.activation(dst, p.ps[j % 4][0:sources[0].shape[1], 0:dst.shape[1]],
                               ACT.Copy).then_inc(kept_a.sem, 1)
    turned.passed(n)
    kept_v.passed((n + 1) // 2)
    kept_a.passed(n // 2)


def products(pe, out, pairs, start, stop):
    n = len(pairs)
    for i, ((ah, al), (bh, bl)) in enumerate(pairs):
        pe.matmul(out, ah, bh, start=start and i == 0, stop=False, skip_group_check=True)
        pe.matmul(out, ah, bl, start=False, stop=False, skip_group_check=True)
        mm = pe.matmul(out, al, bh, start=False, stop=stop and i == n - 1, skip_group_check=True)
    return mm


def split_src_hi(p, act, src):
    for h in range(2):
        act.activation(p.srcH[:, 4 * h:4 * h + 4, :], src[:, 4 * h:4 * h + 4, :],
                       ACT.Copy).then_inc(p.sig("src_hi_ready").sem, 1)


def split_src_lo(p, dve, src):
    for h in range(2):
        dve.wait_ge(*p.sig("src_hi_ready")(h + 1))
        k = slice(4 * h, 4 * h + 4)
        dve.tensor_tensor(p.srcL[:, k, :], src[:, k, :], p.srcH[:, k, :].bitcast(F32),
                          ALU.subtract).then_inc(p.sig("src_ready").sem, 1)


def split_side(p):
    hi = p.sig("side_hi")
    with p.nc.Block(no_gpsimd_drain=True) as block:
        @block.scalar
        def _(act):
            act.activation(p.sideH[:], p.side[:], ACT.Copy).then_inc(hi.sem, 1)

        @block.vector
        def _(dve):
            chain = Chain(dve, p.sig("dve_chain"))
            dve.wait_ge(*hi(1))
            chain(dve.tensor_tensor(p.sideL[:], p.side[:], p.sideH[:].bitcast(F32), ALU.subtract))
    hi.passed(1)


def side_product(p, pe):
    for m in range(NT):
        ms = slice(m * P, m * P + P)
        mm = products(pe, p.ps[0][:, m * NE:m * NE + NE],
                      [((p.srcH[:, k, ms], p.srcL[:, k, ms]), (p.sideH[:, k, :], p.sideL[:, k, :]))
                       for k in range(KT)], True, True)
    return mm


def linear(p, src, n_tok, n_feat=0, out=None, out_feat=None, residual=None, gate=None, side=None):
    nc = p.nc
    ready, taken, src_ready = p.sig("chunk_ready"), p.sig("chunk_taken"), p.sig("src_ready")
    n, g0 = n_tok + n_feat, p.used
    total = n + (1 if side is not None else 0)

    def parts(t, k):
        return t[0][:, k, :], t[1][:, k, :]

    with nc.Block(no_gpsimd_drain=True) as block:
        @block.sync
        def _(sp):
            p.load_stream(sp)

        @block.scalar
        def _(act):
            if src is not None:
                split_src_hi(p, act, src)
            for q in range(2 * n):
                g, b = g0 + q // 2, q % 3
                if q % 2 == 0:
                    p.wait_chunk(act, g)
                if q >= 3:
                    act.wait_ge(*p.w_used[b](q // 3))
                act.activation(p.wH[:, b, :], p.ring[:, g % RING, (q % 2) * PIECE:(q % 2 + 1) * PIECE],
                               ACT.Copy).then_inc(p.w_hi[b].sem, 1)

        @block.tensor
        def _(pe):
            for q in range(2 * n):
                c, h, b = q // 2, q % 2, q % 3
                if q < 2 and src is not None:
                    pe.wait_ge(*src_ready(q + 1))
                pe.wait_ge(*p.w_lo[b](q // 3 + 1))
                if h == 0 and c >= 4:
                    pe.wait_ge(*taken(c - 3))
                w = [v[:, b, :].rearrange("p (k n) -> p k n", k=4) for v in (p.wH, p.wL)]
                for m in range(2):
                    bank = p.ps[2 * (c % 4) + m][:, 0:PC]
                    ms = slice(m * P, m * P + P)
                    pairs = []
                    for k in range(4):
                        s = (p.srcH[:, 4 * h + k, :], p.srcL[:, 4 * h + k, :])
                        wk = (w[0][:, k, :], w[1][:, k, :])
                        if c < n_tok:
                            pairs.append(((s[0][:, ms], s[1][:, ms]), wk))
                        else:
                            pairs.append(((wk[0][:, ms], wk[1][:, ms]), s))
                    mm = products(pe, bank, pairs, h == 0, h == 1)
                mm.then_inc(p.w_used[b].sem, 1)
                if h:
                    pe.wait_ge(*p.w_used[b](q // 3 + 1))
                    pe.sem_inc(ready.sem, 1)
            if side is not None:
                pe.wait_ge(*taken(n))
                side_product(p, pe).then_inc(ready.sem, 1)

        @block.vector
        def _(dve):
            chain = Chain(dve, p.sig("dve_chain"))
            if src is not None:
                split_src_lo(p, dve, src)

            def split(q):
                g, b = g0 + q // 2, q % 3
                dve.wait_ge(*p.w_hi[b](q // 3 + 1))
                ins = dve.tensor_tensor(p.wL[:, b, :], p.ring[:, g % RING, (q % 2) * PIECE:(q % 2 + 1) * PIECE],
                                        p.wH[:, b, :].bitcast(F32), ALU.subtract)
                ins.then_inc(p.w_lo[b].sem, 1)
                if q % 2:
                    dve.wait_ge(*p.w_lo[b](q // 3 + 1))
                    dve.sem_inc(p.slot_free.sem, 1)

            for q in range(min(4, 2 * n)):
                split(q)
            for c in range(n):
                for q in (2 * c + 4, 2 * c + 5):
                    if q < 2 * n and q % 2 == 0:
                        split(q)
                dve.wait_ge(*ready(c + 1))
                for m in range(2):
                    bank = p.ps[2 * (c % 4) + m][:, 0:PC]
                    cut = slice(c * PC, c * PC + PC)
                    if c >= n_tok:
                        ins = dve.tensor_copy(out_feat[:, 2 * (c - n_tok) + m, :], bank)
                    elif residual is None:
                        w = min(PC, out.shape[2] - c * PC)
                        ins = dve.tensor_copy(out[:, m, c * PC:c * PC + w], bank[:, 0:w])
                    elif gate is None:
                        ins = dve.tensor_tensor(residual[:, m, cut], residual[:, m, cut], bank, ALU.add)
                    else:
                        y = p.work[:, m * PC:m * PC + PC]
                        chain(dve.tensor_tensor(y, bank, gate[:, cut], ALU.mult))
                        ins = dve.tensor_tensor(residual[:, m, cut], residual[:, m, cut], y, ALU.add)
                ins.then_inc(taken.sem, 1)
                if 2 * c + 5 < 2 * n:
                    split(2 * c + 5)
            if side is not None:
                dve.wait_ge(*ready(n + 1))
                dve.tensor_copy(side, p.ps[0][:, 0:NT * NE].rearrange("p (m n) -> p m n", m=NT)).then_inc(taken.sem, 1)
    ready.passed(total)
    taken.passed(total)
    if src is not None:
        src_ready.passed(2)
        p.sig("src_hi_ready").passed(2)
    for b in range(3):
        k = len(range(b, 2 * n, 3))
        for s in (p.w_hi[b], p.w_lo[b], p.w_used[b]):
            s.passed(k)
    p.slot_free.passed(n)
    p.end_stream()


def ffn(p, residual, gate=None):
    nc = p.nc
    n, g0 = FC, p.used
    GATE, UP, DOWN = 0, 1, 2
    exp_ready, half_ready, act_hi, act_ready = (p.sig("ffn_exp_ready"), p.sig("ffn_half_ready"),
                                                p.sig("ffn_act_hi"), p.sig("ffn_act_ready"))
    a_ready, step_done, y_zero, y_ready = (p.sig("ffn_a_ready"), p.sig("ffn_dve_step"), p.sig("ffn_zero"),
                                           p.sig("ffn_y_ready"))
    ex = p.work[:, 0:512].rearrange("p (b t) -> p b t", b=2)
    rc = p.work[:, 512:1024].rearrange("p (b t) -> p b t", b=2)
    aT = p.work[:, 1024:1536].rearrange("p (b t) -> p b t", b=2)
    zeros = p.work[:, 1536:2560]
    turns = (n - 2) // RING
    assert 2 + turns * RING == n

    def loop(eng, step):
        step(0, 0)
        step(1, 0)
        with eng.Fori(0, turns) as i:
            for r in range(RING):
                step(2 + r, i)
        step(n, 0)

    def at(signal, turn, k):
        return signal.sem, turn * RING + (signal.base + k)

    def piece(c, kind):
        return p.ring[:, (g0 + c) % RING, kind * PIECE:(kind + 1) * PIECE]

    with nc.Block(no_gpsimd_drain=True) as block:
        @block.sync
        def _(sp):
            p.load_stream(sp)

        @block.scalar
        def _(act):
            def hi(c, turn, kind):
                act.wait_ge(*at(p.w_used[kind], turn, c))
                act.activation(p.wH[:, kind, :], piece(c, kind), ACT.Copy).then_inc(p.w_hi[kind].sem, 1)

            def step(c, turn):
                if c < n:
                    p.wait_chunk(act, g0 + c, turn)
                    hi(c, turn, GATE)
                if c:
                    act.wait_ge(*at(p.w_used[GATE], turn, c))
                    if c >= 3:
                        act.wait_ge(*at(half_ready, turn, c - 2))
                    act.activation(ex[:, (c - 1) % 2, :], p.ps[4 + (c - 1) % 2][:, 0:T], ACT.Exp,
                                   scale=-1.0).then_inc(exp_ready.sem, 1)
                if c < n:
                    hi(c, turn, UP)
                if c:
                    hi(c - 1, turn, DOWN)
                    act.wait_ge(*at(a_ready, turn, c))
                    act.activation(p.actH[:, :], aT[:, (c - 1) % 2, :], ACT.Copy).then_inc(act_hi.sem, 1)
            loop(act, step)

        @block.tensor
        def _(pe):
            pe.wait_ge(*y_zero(1))
            for b in range(4):
                pe.matmul(p.ps[b][:, :], zeros[:, 0:P], zeros[:, 0:512], start=True, stop=False,
                          skip_group_check=True)

            def step(c, turn):
                if c < n:
                    if c >= 2:
                        pe.wait_ge(*at(a_ready, turn, c - 1))
                    for kind in (GATE, UP):
                        w = [v[:, kind, :].rearrange("p (k f) -> p k f", k=KT) for v in (p.wH, p.wL)]
                        pe.wait_ge(*at(p.w_lo[kind], turn, c + 1))
                        out = p.ps[4 + 2 * kind + c % 2][:, 0:T]
                        for h in range(2):
                            mm = products(pe, out, [((w[0][:, k, :], w[1][:, k, :]), (p.srcH[:, k, :], p.srcL[:, k, :]))
                                                    for k in range(4 * h, 4 * h + 4)], h == 0, h == 1)
                        mm.then_inc(p.w_used[kind].sem, 1)
                if c:
                    pe.wait_ge(*at(act_ready, turn, c))
                    pe.wait_ge(*at(p.w_lo[DOWN], turn, c))
                    for b in range(4):
                        t, hf = slice((b // 2) * P, (b // 2) * P + P), slice((b % 2) * 512, (b % 2) * 512 + 512)
                        mm = products(pe, p.ps[b][:, :], [((p.actH[:, t], p.actL[:, t]),
                                                           (p.wH[:, DOWN, hf], p.wL[:, DOWN, hf]))], False, False)
                    mm.then_inc(p.w_used[DOWN].sem, 1)
            loop(pe, step)
            for b in range(4):
                mm = pe.matmul(p.ps[b][:, :], zeros[:, 0:P], zeros[:, 0:512], start=False, stop=True,
                               skip_group_check=True)
            mm.then_inc(y_ready.sem, 1)

        @block.vector
        def _(dve):
            dve.memset(zeros, 0.0).then_inc(y_zero.sem, 1)
            def lo(c, turn, kind):
                dve.wait_ge(*at(p.w_hi[kind], turn, c + 1))
                dve.tensor_tensor(p.wL[:, kind, :], piece(c, kind), p.wH[:, kind, :].bitcast(F32),
                                  ALU.subtract).then_inc(p.w_lo[kind].sem, 1)

            def step(c, turn):
                a = (c - 1) % 2
                e, r = ex[:, a, :], rc[:, a, :]
                if c < n:
                    lo(c, turn, GATE)
                if c:
                    dve.wait_ge(*at(exp_ready, turn, c))
                    dve.tensor_scalar(e, e, 1.0, None, ALU.add).then_inc(step_done.sem, 1)
                    dve.wait_ge(step_done.sem, turn * (2 * RING) + (step_done.base + 2 * c - 1))
                    dve.reciprocal(r, e).then_inc(step_done.sem, 1)
                    dve.wait_ge(step_done.sem, turn * (2 * RING) + (step_done.base + 2 * c))
                    dve.tensor_tensor(r, r, p.ps[4 + a][:, 0:T], ALU.mult).then_inc(half_ready.sem, 1)
                if c < n:
                    lo(c, turn, UP)
                if c:
                    dve.wait_ge(*at(p.w_used[UP], turn, c))
                    dve.wait_ge(*at(half_ready, turn, c))
                    dve.tensor_tensor(aT[:, a, :], r, p.ps[6 + a][:, 0:T], ALU.mult).then_inc(a_ready.sem, 1)
                    dve.wait_ge(*at(act_hi, turn, c))
                    dve.tensor_tensor(p.actL[:, :], aT[:, a, :], p.actH[:, :].bitcast(F32),
                                      ALU.subtract).then_inc(act_ready.sem, 1)
                    lo(c - 1, turn, DOWN)
                    dve.wait_ge(*at(p.w_lo[DOWN], turn, c))
                    dve.sem_inc(p.slot_free.sem, 1)
            loop(dve, step)
            chain = Chain(dve, p.sig("dve_chain"))
            dve.wait_ge(*y_ready(1))
            for b in range(4):
                r = residual[:, b // 2, (b % 2) * 512:(b % 2) * 512 + 512]
                if gate is None:
                    chain(dve.tensor_tensor(r, r, p.ps[b][:, :], ALU.add))
                else:
                    y = p.work[:, (b % 2) * 512:(b % 2) * 512 + 512]
                    chain(dve.tensor_tensor(y, p.ps[b][:, :], gate[:, (b % 2) * 512:(b % 2) * 512 + 512], ALU.mult))
                    chain(dve.tensor_tensor(r, r, y, ALU.add))
    step_done.passed(2 * n)
    for s, k in ((exp_ready, n), (half_ready, n), (act_hi, n), (act_ready, n), (a_ready, n), (y_zero, 1),
                 (y_ready, 1)):
        s.passed(k)
    for b in range(3):
        for s in (p.w_hi[b], p.w_lo[b], p.w_used[b]):
            s.passed(n)
    p.slot_free.passed(n)
    p.end_stream()


def attention(p, items):
    n = len(items)
    scores, negmax, probs = p.sig("scores_ready"), p.sig("negmax_ready"), p.sig("probs_ready")
    masked, sunk = p.sig("probs_masked"), p.sig("sink_ready")
    pt_ready, pt_kept, pv, done = p.sig("pt_ready"), p.sig("pt_kept"), p.sig("pv_ready"), p.sig("attn_out")
    S = p.work[:, 0:1024].rearrange("p (b n) -> p b n", b=2)
    E = p.work[:, 1024:2048].rearrange("p (b n) -> p b n", b=2)
    PT = p.work[:, 2048:3072].rearrange("p (b n) -> p b n", b=2)
    has_valid = any(it.get("valid") is not None for it in items)
    has_sink = any(it.get("sink") is not None for it in items)

    def nk(i):
        return items[i]["qk"][0][1].shape[1]

    def blocks(i):
        return [min(P, nk(i) - b) for b in range(0, nk(i), P)]

    with p.nc.Block(no_gpsimd_drain=True) as block:
        @block.tensor
        def _(pe):
            for i in range(n + 2):
                if i < n:
                    if i >= 2:
                        pe.wait_ge(*probs(i - 1))
                    qk = items[i]["qk"]
                    for j, (q, k) in enumerate(qk):
                        mm = pe.matmul(p.ps[i % 2][:, 0:nk(i)], q, k, start=j == 0, stop=j == len(qk) - 1)
                    mm.then_inc(scores.sem, 1)
                if 1 <= i <= n:
                    j = i - 1
                    pe.wait_ge(*(masked if has_valid else probs)(j + 1))
                    if j >= 2:
                        pe.wait_ge(*pt_kept(j - 1))
                    for b, w in enumerate(blocks(j)):
                        mm = pe.transpose(p.ps[2 + j % 2][0:w, b * P:b * P + P], E[:, j % 2, b * P:b * P + w],
                                          p.ident[:, :])
                    mm.then_inc(pt_ready.sem, 1)
                if i >= 2:
                    j = i - 2
                    pe.wait_ge(*pt_kept(j + 1))
                    if j >= 2:
                        pe.wait_ge(*done(j - 1))
                    bl, v = blocks(j), items[j]["v"]
                    for b, w in enumerate(bl):
                        mm = pe.matmul(p.ps[4 + j % 2][:, 0:v[b].shape[1]], PT[0:w, j % 2, b * P:b * P + P], v[b],
                                       start=b == 0, stop=b == len(bl) - 1)
                    mm.then_inc(pv.sem, 1)

        @block.vector
        def _(dve):
            chain = Chain(dve, p.sig("dve_chain"))
            for i in range(n + 2):
                if i < n:
                    it, st = items[i], p.stat[:, i % 4, :]
                    dve.wait_ge(*scores(i + 1))
                    s = p.ps[i % 2][:, 0:nk(i)]
                    if it.get("mask") is not None:
                        if i >= 2:
                            dve.wait_ge(*probs(i - 1))
                        chain(dve.tensor_tensor(S[:, i % 2, 0:nk(i)], s, it["mask"], ALU.add))
                        s = S[:, i % 2, 0:nk(i)]
                    chain(dve.tensor_reduce(st[:, 0:1], s, AX_X, ALU.max))
                    if it.get("sink") is not None:
                        chain(dve.tensor_scalar(st[:, 0:1], st[:, 0:1], it["scale"], it["sink"], ALU.mult, ALU.max))
                        dve.tensor_scalar(st[:, 1:2], st[:, 0:1], -1.0, None, ALU.mult).then_inc(negmax.sem, 1)
                    else:
                        dve.tensor_scalar(st[:, 1:2], st[:, 0:1], -it["scale"], None, ALU.mult).then_inc(negmax.sem, 1)
                    if has_valid:
                        dve.wait_ge(*probs(i + 1))
                        e = E[:, i % 2, 0:nk(i)]
                        dve.tensor_tensor(e, e, it["valid"], ALU.mult).then_inc(masked.sem, 1)
                if i >= 2:
                    it, st = items[i - 2], p.stat[:, (i - 2) % 4, :]
                    dve.wait_ge(*pv(i - 1))
                    if it.get("sink") is not None:
                        dve.wait_ge(*sunk(i - 1))
                        chain(dve.tensor_tensor(st[:, 2:3], st[:, 2:3], st[:, 3:4], ALU.add))
                    chain(dve.reciprocal(st[:, 0:1], st[:, 2:3]))
                    dve.tensor_scalar(it["out"], p.ps[4 + i % 2][:, 0:it["out"].shape[1]], st[:, 0:1], None,
                                      ALU.mult).then_inc(done.sem, 1)

        @block.scalar
        def _(act):
            for i in range(n + 1):
                if i < n:
                    it, st = items[i], p.stat[:, i % 4, :]
                    act.wait_ge(*negmax(i + 1))
                    if has_sink:
                        act.activation(st[:, 3:4], it["sink"], ACT.Exp, bias=st[:, 1:2]).then_inc(sunk.sem, 1)
                    if i >= 2:
                        act.wait_ge(*pt_ready(i - 1))
                    s = p.ps[i % 2][:, 0:nk(i)] if it.get("mask") is None else S[:, i % 2, 0:nk(i)]
                    act.activation(E[:, i % 2, 0:nk(i)], s, ACT.Exp, bias=st[:, 1:2], scale=it["scale"],
                                   accum_out=st[:, 2:3]).then_inc(probs.sem, 1)
                if i >= 1:
                    j = i - 1
                    act.wait_ge(*pt_ready(j + 1))
                    if j >= 2:
                        act.wait_ge(*pv(j - 1))
                    w = blocks(j)
                    act.activation(PT[0:w[0], j % 2, 0:len(w) * P], p.ps[2 + j % 2][0:w[0], 0:len(w) * P],
                                   ACT.Copy).then_inc(pt_kept.sem, 1)
    for s in (scores, negmax, probs, pt_ready, pt_kept, pv, done):
        s.passed(n)
    if has_valid:
        masked.passed(n)
    if has_sink:
        sunk.passed(n)


def heads_to_T(src, first, count, dst, d=HD, at=None):
    groups = []
    for h in range(0, count, 2):
        hs = range(h, min(h + 2, count))
        groups.append(([src[:, t, first + a * d:first + a * d + d] for a in hs for t in range(NT)],
                       dst(h, len(hs))))
    return groups


def qk_rope1(p, proj, l, rotate):
    with p.nc.Block(no_gpsimd_drain=True) as block:
        @block.gpsimd
        def _(pool):
            rsqrts(p, pool, [6, 2] * NT)

        @block.vector
        def _(dve):
            chain = Chain(dve, p.sig("dve_chain"))
            for t in range(NT):
                def heads(a, n):
                    return proj[:, t, a:a + n * HD].rearrange("p (h d) -> p h d", h=n)
                head_norm(p, chain, dve, heads(0, 6), p.row(ROWS1, "q_norm", l, HD), p.work[:], p.small[:])
                head_norm(p, chain, dve, heads(384, 2), p.row(ROWS1, "k_norm", l, HD), p.work[:], p.small[:])
                if rotate:
                    c = p.con_at(CON1, "rope_c", NT)[:, t, :]
                    s = p.con_at(CON1, "rope_s", NT)[:, t, :]
                    rope(chain, dve, heads(0, 8), c, s, p.work[:])
                    rope(chain, dve, heads(896, 8), c, s, p.work[:])


def fourier(p, proj):
    seq_done, seq_kept, out_done, out_kept = (p.sig("dft_seq"), p.sig("dft_seq_kept"), p.sig("dft_out"),
                                              p.sig("dft_out_kept"))
    dft = p.con_at(CON1, "dft_seq", NT)
    A = p.work[:, 0:1024].rearrange("p (c n) -> p c n", c=2)
    with p.nc.Block(no_gpsimd_drain=True) as block:
        @block.tensor
        def _(pe):
            for c in range(2):
                for t in range(NT):
                    mm = pe.matmul(p.ps[c][:, :], proj[:, t, 640 + c * P:640 + c * P + P], dft[:, t, :],
                                   start=t == 0, stop=t == NT - 1)
                mm.then_inc(seq_done.sem, 1)
            for c in range(2):
                pe.wait_ge(*seq_kept(c + 1))
                pe.matmul(p.ps[2 + c][:, 0:T], p.con_at(CON1, "dft_cos"), A[:, c, 0:T], start=True, stop=False)
                pe.matmul(p.ps[2 + c][:, 0:T], p.con_at(CON1, "dft_sin"), A[:, c, T:2 * T], start=False,
                          stop=True).then_inc(out_done.sem, 1)

        @block.vector
        def _(dve):
            for c in range(2):
                dve.wait_ge(*seq_done(c + 1))
                dve.tensor_copy(A[:, c, :], p.ps[c][:, :]).then_inc(seq_kept.sem, 1)
            for c in range(2):
                dve.wait_ge(*out_done(c + 1))
                dve.tensor_copy(p.oT[:, 3 + c, :], p.ps[2 + c][:, 0:T]).then_inc(out_kept.sem, 1)
    for s in (seq_done, seq_kept, out_done, out_kept):
        s.passed(2)


def o_groups(p, cuts):
    out = []
    for i in range(0, len(cuts), 2):
        two = cuts[i:i + 2]
        assert len(two) == 1 or two[1][0] == two[0][0] + 1
        out.append(([f(t) for _, f in two for t in range(NT)],
                    p.oT[:, two[0][0]:two[0][0] + len(two), :].rearrange("p k t -> p (k t)")))
    return out


def block1_attention(p, proj, l, x_tokens, both):
    kT = p.big[:, 0:8 * T].rearrange("p (h n) -> p h n", h=4)
    qT = p.big[:, 8 * T:20 * T].rearrange("p (h n) -> p h n", h=12)

    def q_dst(first):
        return lambda h, m: qT[0:HD, first + h:first + h + m, :].rearrange("p h t -> p (h t)")
    turn(p, heads_to_T(proj, 0, 6, q_dst(0)) + heads_to_T(proj, 896, 6, q_dst(6)))
    items = []
    for h in range(12):
        for t in range(NT):
            kv, window = h // 3, h >= 6
            v_at = 512 + 64 * kv if kv < 2 else 1408 + 64 * (kv - 2)
            q_at = h * HD if not window else 896 + (h - 6) * HD
            v = [p.projc[:, b, v_at:v_at + HD] for b in range(NT)]
            if x_tokens:
                v += [p.proj[:, b, v_at:v_at + HD] for b in range(NT)]
            it = dict(qk=[(qT[0:HD, h, t * P:t * P + P], kT[0:HD, kv, 0:len(v) * P])], v=v, scale=HD ** -0.5,
                      out=proj[:, t, q_at:q_at + HD])
            if window:
                it["sink"] = p.row(ROWS1, "sink")[:, l * 6 + h - 6:l * 6 + h - 5]
                if x_tokens:
                    it["mask"] = p.con_at(CON1, "window", NT)[:, t, :]
            items.append(it)
    attention(p, items[:12])
    attention(p, items[12:])


def block1_keys(p, proj, at):
    kT = p.big[:, 0:8 * T].rearrange("p (h n) -> p h n", h=4)
    groups = []
    for g, first in enumerate((384, 1280)):
        for h in range(2):
            groups.append(([proj[:, t, first + h * HD:first + h * HD + HD] for t in range(NT)],
                           kT[0:HD, 2 * g + h, at:at + T]))
    turn(p, groups)


def block1_mix_out(p, proj, residual, gate):
    def cut(a):
        return lambda t: proj[:, t, a:a + P]
    turn(p, o_groups(p, [(0, cut(0)), (1, cut(P))]) + o_groups(p, [(2, cut(2 * P))])
         + o_groups(p, [(5, cut(896)), (6, cut(896 + P))]) + o_groups(p, [(7, cut(896 + 2 * P))]))
    linear(p, p.oT, 4, residual=residual, gate=gate)


def block1(p):
    x, ctx = p.x, p.ctx
    px = p.proj[:, :, 0:A_COLS]
    pc = p.projc[:]
    for l in range(2):
        adaln(p, l)
        norm_src(p, x, p.scl[:, 0, 0, :], p.mod[:, 0:8, 0])
        linear(p, None, 6, out=px)
        norm_src(p, ctx, p.scl[:, 0, 1, :], p.mod[:, 0:8, 1])
        linear(p, None, 6, out=pc)
        qk_rope1(p, px, l, True)
        qk_rope1(p, pc, l, False)
        block1_keys(p, pc, 0)
        block1_keys(p, px, T)
        block1_attention(p, px, l, True, True)
        fourier(p, px)
        block1_mix_out(p, px, x, p.gates[:, 0, :])
        norm_src(p, x, p.scl[:, 1, 0, :], p.mod[:, 16:24, 0])
        ffn(p, x, p.gates[:, 1, :])
        if l == 0:
            load_gates(p, 1)
            block1_attention(p, pc, l, False, True)
            fourier(p, pc)
            block1_mix_out(p, pc, ctx, p.gates[:, 0, :])
            norm_src(p, ctx, p.scl[:, 1, 1, :], p.mod[:, 16:24, 1])
            ffn(p, ctx, p.gates[:, 1, :])
    with p.nc.Block(no_gpsimd_drain=True) as block:
        @block.gpsimd
        def _(pool):
            rsqrts(p, pool, [1] * NT)

        @block.vector
        def _(dve):
            chain = Chain(dve, p.sig("dve_chain"))
            for t in range(NT):
                head_norm(p, chain, dve, x[:, t:t + 1, :], p.row(ROWS1, "g_final"), p.work[:], p.small[:])


def silu_by_parts(p, jobs):
    e = p.sig("silu_exp")
    with p.nc.Block(no_gpsimd_drain=True) as block:
        @block.scalar
        def _(act):
            for v, s in jobs:
                act.activation(s, v, ACT.Exp, scale=-1.0).then_inc(e.sem, 1)

        @block.vector
        def _(dve):
            chain = Chain(dve, p.sig("dve_chain"))
            for i, (v, s) in enumerate(jobs):
                dve.wait_ge(*e(i + 1))
                chain(dve.tensor_scalar(s, s, 1.0, None, ALU.add))
                chain(dve.reciprocal(s, s))
                chain(dve.tensor_tensor(v, v, s, ALU.mult))
    e.passed(len(jobs))


def rope_tables2(p, t):
    return p.con_at(CON2, "rope_c", NT)[:, t, :], p.con_at(CON2, "rope_s", NT)[:, t, :]


def diff_attention(p):
    proj = p.proj
    lam = p.small[:, 40:41]
    exp_ready = p.sig("lam_exp")
    dots_ready = p.sig("lam_dots")
    with p.nc.Block(no_gpsimd_drain=True) as block:
        @block.gpsimd
        def _(pool):
            rsqrts(p, pool, [8, 8] * NT)

        @block.vector
        def _(dve):
            chain = Chain(dve, p.sig("dve_chain"))
            lr = p.row(ROWS2, "da_lam").rearrange("p (a b d) -> p a b d", a=2, b=2)
            prod = p.work[:, 0:128].rearrange("p (a d) -> p a d", a=2)
            chain(dve.tensor_tensor(prod, lr[:, :, 0, :], lr[:, :, 1, :], ALU.mult))
            dve.tensor_reduce(p.small[:, 36:38], prod, AX_X, ALU.add).then_inc(dots_ready.sem, 1)
            dve.wait_ge(*dots_ready(1))
            for t in range(NT):
                def heads(a, n):
                    return proj[:, t, a:a + n * HD].rearrange("p (h d) -> p h d", h=n)
                head_norm(p, chain, dve, heads(0, 8), p.row(ROWS2, "da_q"), p.work[:], p.small[:])
                head_norm(p, chain, dve, heads(512, 8), p.row(ROWS2, "da_k"), p.work[:], p.small[:])
                rope(chain, dve, heads(0, 16), *rope_tables2(p, t), p.work[:])
            dve.wait_ge(*exp_ready(1))
            chain(dve.tensor_tensor(lam, p.small[:, 38:39], p.small[:, 39:40], ALU.subtract))
            chain(dve.tensor_scalar(lam, lam, LAM_INIT, None, ALU.add))

        @block.scalar
        def _(act):
            act.wait_ge(*dots_ready(1))
            act.activation(p.small[:, 38:40], p.small[:, 36:38], ACT.Exp).then_inc(exp_ready.sem, 1)
    exp_ready.passed(1)
    dots_ready.passed(1)
    qT = p.big[:, 0:8 * T].rearrange("p (h n) -> p h n", h=8)
    kT = p.big[:, 12 * T:20 * T].rearrange("p (h n) -> p h n", h=8)

    def to(dst):
        return lambda h, m: dst[0:HD, h:h + m, :].rearrange("p h t -> p (h t)")
    turn(p, heads_to_T(proj, 0, 8, to(qT)) + heads_to_T(proj, 512, 8, to(kT)))
    items = []
    for h in range(4):
        for c in range(2):
            for t in range(NT):
                n = (t + 1) * P
                items.append(dict(qk=[(qT[0:HD, 2 * h + c, t * P:t * P + P], kT[0:HD, 2 * h + c, 0:n])],
                                  v=[proj[:, b, 1024 + h * P:1024 + h * P + P] for b in range(t + 1)],
                                  mask=p.con_at(CON2, "causal", NT)[:, t, 0:n], scale=HD ** -0.5,
                                  out=proj[:, t, (2 * h + c) * P:(2 * h + c) * P + P]))
    attention(p, items)
    with p.nc.Block(no_gpsimd_drain=True) as block:
        @block.gpsimd
        def _(pool):
            rsqrts(p, pool, [4] * NT)

        @block.vector
        def _(dve):
            chain = Chain(dve, p.sig("dve_chain"))
            for t in range(NT):
                o = proj[:, t, 0:1024].rearrange("p (h c d) -> p h c d", h=4, c=2)
                w = p.work[:, 1024:1536].rearrange("p (h d) -> p h d", h=4)
                chain(dve.tensor_scalar(w, o[:, :, 1, :], lam, None, ALU.mult))
                chain(dve.tensor_tensor(w, o[:, :, 0, :], w, ALU.subtract))
                head_norm(p, chain, dve, w, p.row(ROWS2, "subln"), p.work[:], p.small[:])
                chain(dve.tensor_scalar(proj[:, t, 0:512].rearrange("p (h d) -> p h d", h=4), w, 1.0 - LAM_INIT, None,
                                        ALU.mult))


def mamba(p):
    nc = p.nc
    raw = p.projc[:].rearrange("p t c -> p (t c)")[:, 0:KT * T].rearrange("p (k t) -> p k t", k=KT)
    cv = p.oT
    xs = p.projc[:].rearrange("p t c -> p (t c)")[:, 2048:3072].rearrange("p (t c) -> p t c", t=NT)
    dt = p.small[:, 48:64].rearrange("p (t h) -> p t h", t=NT)
    tiny = [p.small[:, 64 + 16 * i:80 + 16 * i].rearrange("p (t h) -> p t h", t=NT) for i in range(8)]
    ad, ncs, u, z, z2, acc, neg_a, ex = tiny
    conv_w = p.col("conv_w", 0, 32).rearrange("p (k j) -> p k j", j=4)
    dt_u, dt_e = p.sig("dt_abs"), p.sig("dt_exp")
    with nc.Block(no_gpsimd_drain=True) as block:
        @block.vector
        def _(dve):
            chain = Chain(dve, p.sig("dve_chain"))
            bias = p.row(ROWS2, "dt_bias").unsqueeze(1).broadcast_to([P, NT, 8])
            chain(dve.tensor_tensor(dt, p.proj[:, :, 2048:2056], bias, ALU.add))
            chain(dve.tensor_scalar(u, dt, -1.0, None, ALU.mult))
            dve.tensor_tensor(u, u, dt, ALU.min).then_inc(dt_u.sem, 1)
            for k in range(KT):
                a, b = raw[:, k, :], cv[:, k, :]
                chain(dve.tensor_scalar(b, a, conv_w[:, k, 3:4], p.col("conv_b")[:, k:k + 1], ALU.mult, ALU.add))
                for j in range(1, 4):
                    chain(dve.scalar_tensor_tensor(out=b[:, j:T], in0=a[:, 0:T - j], scalar=conv_w[:, k, 3 - j:4 - j],
                                                   in1=b[:, j:T], op0=ALU.mult, op1=ALU.add))
            dve.wait_ge(*dt_e(2))
            chain(dve.tensor_scalar(z, ex, 2.0, None, ALU.add))
            chain(dve.reciprocal(z, z))
            chain(dve.tensor_tensor(z, z, ex, ALU.mult))
            chain(dve.tensor_tensor(z2, z, z, ALU.mult))
            chain(dve.tensor_scalar(acc, z2, 2.0 / 17, 2.0 / 15, ALU.mult, ALU.add))
            for m in (13, 11, 9, 7, 5, 3, 1):
                chain(dve.tensor_tensor(acc, acc, z2, ALU.mult))
                chain(dve.tensor_scalar(acc, acc, 2.0 / m, None, ALU.add))
            chain(dve.tensor_tensor(acc, acc, z, ALU.mult))
            chain(dve.tensor_scalar(dt, dt, 0.0, None, ALU.max))
            chain(dve.tensor_tensor(dt, dt, acc, ALU.add))
            chain(dve.tensor_tensor(ad, dt, neg_a[:, 0:1, :].broadcast_to([P, NT, 8]), ALU.mult))
            chain(dve.tensor_scalar(ad, ad, -1.0, None, ALU.mult))

        @block.scalar
        def _(act):
            act.wait_ge(*dt_u(1))
            act.activation(ex, u, ACT.Exp).then_inc(dt_e.sem, 1)
            act.activation(neg_a[:, 0, :], p.row(ROWS2, "a_log"), ACT.Exp).then_inc(dt_e.sem, 1)
    dt_u.passed(1)
    dt_e.passed(2)
    silu_by_parts(p, [(cv[:, 2 * k:2 * k + 2, :], raw[:, 2 * k:2 * k + 2, :]) for k in range(4)])
    turn(p, [([cv[:, k, t * P:t * P + P] for k in range(4)], xs[:, t, :]) for t in range(NT)])

    xdt = p.big[:, 0:1024].rearrange("p (t c) -> p t c", t=NT)
    y = p.big[:, 1024:2048].rearrange("p (t c) -> p t c", t=NT)
    adw = p.big[:, 2048:2048 + 2048].rearrange("p (t h m) -> p t h m", t=NT, h=8)
    dec = p.work[:, 0:512].rearrange("p (b n) -> p b n", b=2)
    MT = p.work[:, 1024:2048].rearrange("p (b s n) -> p b s n", b=2, s=2)
    tri = p.con_at(CON2, "tri", NT)
    mask = p.con_at(CON2, "tri_mask", NT)
    wide, sums, ncs_ready = p.sig("ad_wide"), p.sig("ssm_sums"), p.sig("ncs_ready")
    shifted, decayed, mt_ready, y_ready = (p.sig("decay_in"), p.sig("decay_out"), p.sig("mt_ready"), p.sig("ssm_y"))
    with nc.Block(no_gpsimd_drain=True) as block:
        @block.vector
        def _(dve):
            chain = Chain(dve, p.sig("dve_chain"))
            for t in range(NT):
                dve.tensor_copy(adw[:, t, :, :], ad[:, t, :].unsqueeze(2).broadcast_to([P, 8, P])).then_inc(wide.sem, 1)
            chain(dve.tensor_tensor(xdt[:].rearrange("p t (h d) -> p t h d", h=8),
                                    xs.rearrange("p t (h d) -> p t h d", h=8),
                                    dt.unsqueeze(3).broadcast_to([P, NT, 8, HD]), ALU.mult))
            dve.wait_ge(*sums(3))
            dve.tensor_scalar(ncs, p.ps[4][:, 0:16].rearrange("p (t h) -> p t h", t=NT), -1.0, None,
                              ALU.mult).then_inc(ncs_ready.sem, 1)

            def shift(i):
                h, s = i // 2, i % 2
                if i >= 2:
                    dve.wait_ge(*decayed(i - 1))
                dve.tensor_tensor(dec[:, s, :], p.ps[h // 2][:, (h % 2) * T:(h % 2) * T + T], mask[:, s, :],
                                  ALU.add).then_inc(shifted.sem, 1)
            shift(0)
            for i in range(16):
                if i + 1 < 16:
                    shift(i + 1)
                h, s = i // 2, i % 2
                dve.wait_ge(*decayed(i + 1))
                if h >= 2:
                    dve.wait_ge(*y_ready(h - 1))
                q = (h // 4) * 2 + s
                m = MT[:, h % 2, s, :]
                dve.tensor_tensor(m, m, p.ps[5 + q // 2][:, (q % 2) * T:(q % 2) * T + T],
                                  ALU.mult).then_inc(mt_ready.sem, 1)
            dve.wait_ge(*y_ready(8))
            for t in range(NT):
                h8 = [P, 8, HD]
                w = p.big[:, 4096:4608].rearrange("p (h d) -> p h d", h=8)
                chain(dve.tensor_tensor(w, xs[:, t, :].rearrange("p (h d) -> p h d", h=8),
                                        p.row(ROWS2, "ssm_d").unsqueeze(2).broadcast_to(h8), ALU.mult))
                chain(dve.tensor_tensor(y[:, t, :], p.big[:, 4096:4608], p.ps[7 if t == 0 else 4][:, :], ALU.add))

        @block.tensor
        def _(pe):
            pe.wait_ge(*wide(NT))
            for h in range(8):
                for t in range(NT):
                    mm = pe.matmul(p.ps[h // 2][:, (h % 2) * T:(h % 2) * T + T], adw[:, t, h, :], tri[:, t, :],
                                   start=t == 0, stop=t == NT - 1)
            mm.then_inc(sums.sem, 1)
            for q in range(4):
                g, s = q // 2, q % 2
                mm = pe.matmul(p.ps[5 + q // 2][:, (q % 2) * T:(q % 2) * T + T], cv[:, 4 + g, s * P:s * P + P],
                               cv[:, 6 + g, :], start=True, stop=True)
            mm.then_inc(sums.sem, 1)
            for lt in range(NT):
                for t in range(NT):
                    mm = pe.matmul(p.ps[4][:, lt * 8:lt * 8 + 8], tri[:, t, lt * P:lt * P + P], ad[:, t, :],
                                   start=t == 0, stop=t == NT - 1)
            mm.then_inc(sums.sem, 1)
            pe.wait_ge(*ncs_ready(1))
            for h in range(8):
                pe.wait_ge(*mt_ready(2 * h + 2))
                for lt in range(NT):
                    for s in range(NT):
                        mm = pe.matmul(p.ps[7 if lt == 0 else 4][:, h * HD:h * HD + HD],
                                       MT[:, h % 2, s, lt * P:lt * P + P], xdt[:, s, h * HD:h * HD + HD],
                                       start=s == 0, stop=s == NT - 1)
                mm.then_inc(y_ready.sem, 1)

        @block.scalar
        def _(act):
            act.wait_ge(*ncs_ready(1))
            for i in range(16):
                h, s = i // 2, i % 2
                act.wait_ge(*shifted(i + 1))
                if h >= 2:
                    act.wait_ge(*y_ready(h - 1))
                act.activation(MT[:, h % 2, s, :], dec[:, s, :], ACT.Exp,
                               bias=ncs[:, s, h:h + 1]).then_inc(decayed.sem, 1)
    for s, k in ((wide, NT), (sums, 3), (ncs_ready, 1), (shifted, 16), (decayed, 16), (mt_ready, 16), (y_ready, 8)):
        s.passed(k)
    silu_by_parts(p, [(p.proj[:, t, 1536:2048], p.work[:, t * 512:t * 512 + 512]) for t in range(NT)])
    with nc.Block(no_gpsimd_drain=True) as block:
        @block.gpsimd
        def _(pool):
            rsqrts(p, pool, [2] * NT)

        @block.vector
        def _(dve):
            chain = Chain(dve, p.sig("dve_chain"))
            for t in range(NT):
                chain(dve.tensor_tensor(y[:, t, :], y[:, t, :], p.proj[:, t, 1536:2048], ALU.mult))
                yg = y[:, t, :].rearrange("p (g d) -> p g d", g=2)
                rstd_of(p, chain, dve, yg, 256, p.work[:], p.small[:, 0:2])
                chain(dve.tensor_tensor(yg, yg, p.small[:, 0:2].unsqueeze(2).broadcast_to([P, 2, 256]), ALU.mult))
                chain(dve.tensor_tensor(y[:, t, :], y[:, t, :], p.gates[:, 0, 0:512], ALU.mult))
    return y


def even_layer(p):
    norm_src(p, p.x, p.col("ev_mix"))
    raw = p.projc[:].rearrange("p t c -> p (t c)")[:, 0:KT * T].rearrange("p (k t) -> p k t", k=KT)
    linear(p, None, 8, 4, out=p.proj[:, :, 0:2048], out_feat=raw, side=p.proj[:, :, 2048:2056])
    diff_attention(p)
    y = mamba(p)
    turn(p, o_groups(p, [(k, (lambda k: lambda t: p.proj[:, t, k * P:k * P + P])(k)) for k in range(4)])
         + o_groups(p, [(4 + k, (lambda k: lambda t: y[:, t, k * P:k * P + P])(k)) for k in range(4)]))
    linear(p, p.oT, 4, residual=p.x)
    norm_src(p, p.x, p.col("ev_ffn"))
    ffn(p, p.x)


def nsa_compress(p, w1, w2):
    nc = p.nc
    kcT = p.big[0:HD, 2048:2048 + 4 * T].rearrange("p (k n) -> p k n", k=4)
    turn(p, heads_to_T(p.proj, 512, 4, lambda h, m: kcT[:, h:h + m, :].rearrange("p h t -> p (h t)")))
    flat = p.work[0:HD, 0:32 * 2 * N_CMP].rearrange("p (i g n) -> p i g n", i=32, g=2)
    posed, hid, act_exp, act_done = p.sig("cmp_posed"), p.sig("cmp_hidden"), p.sig("cmp_exp"), p.sig("cmp_act")
    out_ready, kept = p.sig("cmp_out"), p.sig("cmp_kept")
    hsb = p.work[0:HD, 1024:1024 + 3 * 2 * N_CMP].rearrange("p (a n) -> p a n", a=3)
    ckv = p.work[0:N_CMP, 1280:1280 + 4 * HD].rearrange("p (k g d) -> p k g d", k=2, g=2)
    ck_keep = p.big[0:N_CMP, 5120:5120 + 4 * HD].rearrange("p (k g d) -> p k g d", k=2, g=2)
    with nc.Block(no_gpsimd_drain=True) as block:
        @block.gpsimd
        def _(pool):
            rsqrts(p, pool, [2], parts=N_CMP)

        @block.vector
        def _(dve):
            chain = Chain(dve, p.sig("dve_chain"))
            for kind in range(2):
                pos = p.col("cmp_pos", kind, 32)[0:HD, :]
                if kind:
                    dve.wait_ge(*hid(1))
                for g in range(2):
                    for half in range(2):
                        src = kcT[:, 2 * kind + g, 16 * half:16 * half + 16 * N_CMP]\
                            .rearrange("p (n i) -> p i n", i=16)
                        dve.tensor_tensor(flat[:, 16 * half:16 * half + 16, g, :], src,
                                          pos[:, 16 * half:16 * half + 16].unsqueeze(2)
                                          .broadcast_to([HD, 16, N_CMP]), ALU.add).then_inc(posed.sem, 1)
                dve.wait_ge(*act_exp(kind + 1))
                chain(dve.tensor_scalar(hsb[:, 0, :], hsb[:, 0, :], 1.0, None, ALU.add))
                chain(dve.reciprocal(hsb[:, 1, :], hsb[:, 0, :]))
                dve.tensor_tensor(hsb[:, 2, :], hsb[:, 1, :], p.ps[0][0:HD, 0:2 * N_CMP],
                                  ALU.mult).then_inc(act_done.sem, 1)
                dve.wait_ge(*out_ready(kind + 1))
                chain(dve.tensor_copy(ck_keep[:, kind, :, :],
                                      p.ps[1][0:N_CMP, 0:2 * HD].rearrange("p (g d) -> p g d", g=2)))
                dve.sem_inc(kept.sem, 1)
            keys = ck_keep[:, 0, :, :]
            head_norm(p, chain, dve, keys, p.row(ROWS2, "nsa_k", 0, HD)[0:N_CMP, :], p.work[0:N_CMP, :],
                      p.small[0:N_CMP, :])
            rope(chain, dve, keys, p.con_at(CON2, "cmp_c")[0:N_CMP, :], p.con_at(CON2, "cmp_s")[0:N_CMP, :],
                 p.work[0:N_CMP, :])

        @block.tensor
        def _(pe):
            for kind in range(2):
                pe.wait_ge(*posed(4 * kind + 4))
                for i in range(32):
                    mm = pe.matmul(p.ps[0][0:HD, 0:2 * N_CMP], w1[kind][:, i, :],
                                   flat[:, i, :, :].rearrange("p g n -> p (g n)"), start=i == 0, stop=i == 31)
                mm.then_inc(hid.sem, 1)
                pe.wait_ge(*act_done(kind + 1))
                if kind:
                    pe.wait_ge(*kept(1))
                for g in range(2):
                    mm = pe.matmul(p.ps[1][0:N_CMP, g * HD:g * HD + HD], hsb[:, 2, g * N_CMP:g * N_CMP + N_CMP],
                                   w2[:, kind, :], start=True, stop=True)
                mm.then_inc(out_ready.sem, 1)

        @block.scalar
        def _(act):
            for kind in range(2):
                act.wait_ge(*hid(kind + 1))
                act.activation(hsb[:, 0, :], p.ps[0][0:HD, 0:2 * N_CMP], ACT.Exp, scale=-1.0).then_inc(act_exp.sem, 1)
    for s, k in ((posed, 8), (hid, 2), (act_exp, 2), (act_done, 2), (out_ready, 2), (kept, 2)):
        s.passed(k)
    ckT = p.big[0:HD, 5376:5376 + 256]
    turn(p, [([ck_keep[:, 0, g, :]], ckT[:, g * P:g * P + N_CMP]) for g in range(2)])
    return ck_keep, ckT


def nsa(p, w1, w2):
    proj = p.proj
    ck, ckT = nsa_compress(p, w1, w2)
    with p.nc.Block(no_gpsimd_drain=True) as block:
        @block.gpsimd
        def _(pool):
            rsqrts(p, pool, [8, 2, 2] * NT)

        @block.vector
        def _(dve):
            chain = Chain(dve, p.sig("dve_chain"))
            for t in range(NT):
                def heads(a, n):
                    return proj[:, t, a:a + n * HD].rearrange("p (h d) -> p h d", h=n)
                for a, n, gain in ((0, 8, p.row(ROWS2, "nsa_q")), (768, 2, p.row(ROWS2, "nsa_k", 1, HD)),
                                   (1024, 2, p.row(ROWS2, "nsa_k", 2, HD))):
                    head_norm(p, chain, dve, heads(a, n), gain, p.work[:], p.small[:])
                    rope(chain, dve, heads(a, n), *rope_tables2(p, t), p.work[:])
    qT = p.big[:, 0:8 * T].rearrange("p (h n) -> p h n", h=8)
    kT = p.big[:, 3072:3072 + 4 * T].rearrange("p (h n) -> p h n", h=4)

    def to(dst, first):
        return lambda h, m: dst[0:HD, first + h:first + h + m, :].rearrange("p h t -> p (h t)")
    turn(p, heads_to_T(proj, 0, 8, to(qT, 0)) + heads_to_T(proj, 768, 2, to(kT, 0))
         + heads_to_T(proj, 1024, 2, to(kT, 2)))
    ow = p.projc[:].rearrange("p t c -> p (t c)")[:, 0:2048].rearrange("p (w t c) -> p w t c", w=2, t=NT)
    items = []
    for h in range(8):
        for t in range(NT):
            g = h // 4
            items.append(dict(qk=[(qT[0:HD, h, t * P:t * P + P], ckT[:, g * P:g * P + N_CMP])],
                              v=[ck[:, 1, g, :]], mask=p.con_at(CON2, "cmp_mask", NT)[:, t, :],
                              valid=p.con_at(CON2, "cmp_valid", NT)[:, t, :], scale=HD ** -0.5,
                              out=proj[:, t, h * HD:h * HD + HD]))
    attention(p, items)
    items = []
    for w in range(2):
        for h in range(8):
            for t in range(NT):
                g, n = h // 4, (t + 1) * P
                a = 896 + 256 * w + g * HD
                items.append(dict(qk=[(qT[0:HD, h, t * P:t * P + P], kT[0:HD, 2 * w + g, 0:n])],
                                  v=[proj[:, b, a:a + HD] for b in range(t + 1)],
                                  mask=p.con_at(CON2, "causal", NT)[:, t, 0:n], scale=HD ** -0.5,
                                  out=ow[:, w, t, h * HD:h * HD + HD]))
    attention(p, items)
    gate_exp = p.sig("nsa_gate_exp")
    gx = p.small[:, 0:48].rearrange("p (t g) -> p t g", t=NT)
    with p.nc.Block(no_gpsimd_drain=True) as block:
        @block.scalar
        def _(act):
            act.activation(gx, proj[:, :, 1280:1304], ACT.Exp, scale=-1.0).then_inc(gate_exp.sem, 1)

        @block.vector
        def _(dve):
            chain = Chain(dve, p.sig("dve_chain"))
            dve.wait_ge(*gate_exp(1))
            chain(dve.tensor_scalar(gx, gx, 1.0, None, ALU.add))
            chain(dve.reciprocal(gx, gx))
            for t in range(NT):
                g3 = gx[:, t, :].rearrange("p (h c) -> p h c", c=3)
                outs = [v.rearrange("p (h d) -> p h d", h=8) for v in (proj[:, t, 0:512], ow[:, 0, t, :], ow[:, 1, t, :])]
                for c in range(3):
                    chain(dve.tensor_tensor(outs[c], outs[c], g3[:, :, c:c + 1].broadcast_to([P, 8, HD]), ALU.mult))
                chain(dve.tensor_tensor(outs[0], outs[0], outs[1], ALU.add))
                chain(dve.tensor_tensor(outs[0], outs[0], outs[2], ALU.add))
    gate_exp.passed(1)


def mla(p, w_uq, w_ukv):
    nc = p.nc
    proj = p.proj
    q = p.gates[:].rearrange("p a d -> p (a d)")[:, 0:1536].rearrange("p (t c) -> p t c", t=NT)
    flat = p.projc[:].rearrange("p t c -> p (t c)")
    kv = flat[:, 0:2048].rearrange("p (t c) -> p t c", t=NT)
    o = flat[:, 2048:3072].rearrange("p (t c) -> p t c", t=NT)
    big = p.big
    cT = big[:, 5120:5888].rearrange("p (k t) -> p k t", k=3)
    with nc.Block(no_gpsimd_drain=True) as block:
        @block.gpsimd
        def _(pool):
            rsqrts(p, pool, [1, 1, 1] * NT)

        @block.vector
        def _(dve):
            chain = Chain(dve, p.sig("dve_chain"))
            for t in range(NT):
                head_norm(p, chain, dve, proj[:, t:t + 1, 1304:1560], p.row(ROWS2, "cq"), p.work[:], p.small[:])
                head_norm(p, chain, dve, proj[:, t:t + 1, 1560:1688], p.row(ROWS2, "ckv"), p.work[:], p.small[:])
                head_norm(p, chain, dve, proj[:, t:t + 1, 1688:1752], p.row(ROWS2, "kr"), p.work[:], p.small[:])
                rope(chain, dve, proj[:, t:t + 1, 1688:1752], *rope_tables2(p, t), p.work[:])
    turn(p, [([proj[:, t, 1304 + k * P:1304 + k * P + P] for t in range(NT)], cT[:, k, :]) for k in range(3)])
    up, kept = p.sig("mla_up"), p.sig("mla_kept")
    jobs = []
    for t in range(NT):
        for c in range(2):
            jobs.append((q[:, t, c * 384:c * 384 + 384],
                         [(cT[:, k, t * P:t * P + P], w_uq[:, k, c * 384:c * 384 + 384]) for k in range(2)]))
            jobs.append((kv[:, t, c * 512:c * 512 + 512],
                         [(cT[:, 2, t * P:t * P + P], w_ukv[:, c * 512:c * 512 + 512])]))
    with nc.Block(no_gpsimd_drain=True) as block:
        @block.gpsimd
        def _(pool):
            rsqrts(p, pool, [4, 4, 4] * NT)

        @block.tensor
        def _(pe):
            for j, (dst, pairs) in enumerate(jobs):
                for i, (a, b) in enumerate(pairs):
                    mm = pe.matmul(p.ps[j][:, 0:dst.shape[1]], a, b, start=i == 0, stop=i == len(pairs) - 1)
                mm.then_inc(up.sem, 1)

        @block.vector
        def _(dve):
            chain = Chain(dve, p.sig("dve_chain"))
            for j, (dst, _) in enumerate(jobs):
                dve.wait_ge(*up(j + 1))
                chain(dve.tensor_copy(dst, p.ps[j][:, 0:dst.shape[1]]))
            for t in range(NT):
                qh = q[:, t, :].rearrange("p (h d) -> p h d", h=4)
                kh = kv[:, t, :].rearrange("p (h d) -> p h d", h=4)
                head_norm(p, chain, dve, qh[:, :, 0:128], p.row(ROWS2, "qn"), p.work[:], p.small[:])
                head_norm(p, chain, dve, qh[:, :, 128:192], p.row(ROWS2, "qr"), p.work[:], p.small[:])
                rope(chain, dve, qh[:, :, 128:192], *rope_tables2(p, t), p.work[:])
                head_norm(p, chain, dve, kh[:, :, 0:128], p.row(ROWS2, "kn"), p.work[:], p.small[:])
    up.passed(len(jobs))
    qn = big[:, 0:4 * T].rearrange("p (h n) -> p h n", h=4)
    kn = big[:, 4 * T:8 * T].rearrange("p (h n) -> p h n", h=4)
    qr = big[:, 8 * T:12 * T].rearrange("p (h n) -> p h n", h=4)
    kr = big[:, 12 * T:13 * T]

    def tiles(src, a, w):
        return [src[:, t, a:a + w] for t in range(NT)]
    turn(p, [(tiles(q, h * 192, 128), qn[:, h, :]) for h in range(4)]
         + [(tiles(kv, h * 256, 128), kn[:, h, :]) for h in range(4)]
         + [(tiles(q, h * 192 + 128, 64), qr[0:HD, h, :]) for h in range(4)]
         + [(tiles(proj, 1688, 64), kr[0:HD, :])])
    items = []
    for h in range(4):
        for t in range(NT):
            n = (t + 1) * P
            items.append(dict(qk=[(qn[:, h, t * P:t * P + P], kn[:, h, 0:n]),
                                  (qr[0:HD, h, t * P:t * P + P], kr[0:HD, 0:n])],
                              v=[kv[:, b, h * 256 + 128:h * 256 + 256] for b in range(t + 1)],
                              mask=p.con_at(CON2, "causal", NT)[:, t, 0:n], scale=192 ** -0.5,
                              out=o[:, t, h * P:h * P + P]))
    attention(p, items)
    return o


def route(p):
    nc = p.nc
    slot, weight = p.slot, p.weight
    logits = p.small[:, 0:16].rearrange("p (t e) -> p t e", t=NT)
    top = p.small[:, 16:24]
    idx = p.small[:, 24:32]
    hot = p.small[:, 64:80].rearrange("p (t e) -> p t e", t=NT)
    iota = p.con_at(CON2, "iota")[:, 0:NE]
    tri = p.con_at(CON2, "tri", NT)
    logit, diff, ex, chosen, counted, routed = (p.sig("logits"), p.sig("top_diff"), p.sig("top_exp"),
                                                p.sig("tokens_chosen"), p.sig("tokens_counted"), p.sig("routed"))
    with nc.Block(no_gpsimd_drain=True) as block:
        @block.tensor
        def _(pe):
            side_product(p, pe).then_inc(logit.sem, 1)
            pe.wait_ge(*chosen(1))
            for lt in range(NT):
                for t in range(NT):
                    pe.matmul(p.ps[1][:, lt * NE:lt * NE + NE], tri[:, t, lt * P:lt * P + P], hot[:, t, :],
                              start=t == 0, stop=t == NT - 1)
            for t in range(NT):
                mm = pe.matmul(p.ps[1][:, 2 * NE:3 * NE], tri[:, 0, P:2 * P], hot[:, t, :], start=t == 0,
                               stop=t == NT - 1)
            mm.then_inc(counted.sem, 1)

        @block.scalar
        def _(act):
            for t in range(NT):
                act.wait_ge(*diff(t + 1))
                act.activation(p.small[:, 49:50], p.small[:, 48:49], ACT.Exp).then_inc(ex.sem, 1)

        @block.vector
        def _(dve):
            chain = Chain(dve, p.sig("dve_chain"))
            chain(dve.memset(slot[:], -1.0))
            chain(dve.memset(weight[:], 0.0))
            dve.wait_ge(*logit(1))
            chain(dve.tensor_copy(logits, p.ps[0][:, 0:16].rearrange("p (t e) -> p t e", t=NT)))
            for t in range(NT):
                chain(dve.max(top, logits[:, t, :]))
                chain(dve.max_index(p.idx[:, :], top, logits[:, t, :]))
                chain(dve.tensor_copy(idx, p.idx[:, :]))
                dve.tensor_tensor(p.small[:, 48:49], top[:, 1:2], top[:, 0:1], ALU.subtract).then_inc(diff.sem, 1)
                first, second = p.small[:, 52:60], p.small[:, 80:88]
                chain(dve.tensor_scalar(first, iota, idx[:, 0:1], None, ALU.is_equal))
                chain(dve.tensor_scalar(second, iota, idx[:, 1:2], None, ALU.is_equal))
                chain(dve.tensor_tensor(hot[:, t, :], first, second, ALU.add))
                dve.wait_ge(*ex(t + 1))
                chain(dve.tensor_scalar(p.small[:, 50:51], p.small[:, 49:50], 1.0, None, ALU.add))
                chain(dve.reciprocal(p.small[:, 50:51], p.small[:, 50:51]))
                chain(dve.tensor_tensor(p.small[:, 51:52], p.small[:, 50:51], p.small[:, 49:50], ALU.mult))
                chain(dve.tensor_scalar(first, first, p.small[:, 50:51], None, ALU.mult))
                chain(dve.tensor_scalar(second, second, p.small[:, 51:52], None, ALU.mult))
                for half in range(2):
                    chain(dve.tensor_tensor(weight[:, t, half * NE:half * NE + NE], first, second, ALU.add))
            dve.sem_inc(chosen.sem, 1)
            dve.wait_ge(*counted(1))
            cum = p.ps[1][:, 0:16].rearrange("p (t e) -> p t e", t=NT)
            chain(dve.tensor_tensor(slot[:, :, 0:NE], cum, hot[:], ALU.mult))
            chain(dve.tensor_scalar(slot[:, :, 0:NE], slot[:, :, 0:NE], -1.0, None, ALU.add))
            chain(dve.tensor_scalar(slot[:, :, NE:2 * NE], slot[:, :, 0:NE], -float(P), None, ALU.add))
            most = p.small[:, 49:50]
            chain(dve.tensor_reduce(most, p.ps[1][:, 2 * NE:3 * NE], AX_X, ALU.max))
            chain(dve.tensor_scalar(most, most, float(P), 4.0, ALU.is_gt, ALU.mult))
            chain(dve.tensor_scalar(most, most, 4.0, None, ALU.add))
            dve.tensor_copy(p.trip[:, :], most).then_inc(routed.sem, 1)
    for s, k in ((logit, 1), (diff, 2), (ex, 2), (chosen, 1), (counted, 1), (routed, 1)):
        s.passed(k)


def moe(p, gain):
    nc = p.nc
    g0 = p.used
    xn = p.xn
    hJ = p.projc[:].rearrange("p t c -> p (t c)")[:, 0:2048].rearrange("p (b k s) -> p b k s", b=2, k=KT)
    big = p.big
    pick = big[:, 0:512].rearrange("p (b t s) -> p b t s", b=2, t=NT)
    pickw = big[:, 512:1024].rearrange("p (b t s) -> p b t s", b=2, t=NT)
    WT = big[:, 1024:1536].rearrange("p (b n) -> p b n", b=2)
    yS = big[:, 1536:2560]
    ex = p.work[:, 0:256].rearrange("p (b t) -> p b t", b=2)
    rc = p.work[:, 256:512].rearrange("p (b t) -> p b t", b=2)
    aJ = p.work[:, 512:768].rearrange("p (b t) -> p b t", b=2)
    gu_ready, exp_ready, act_ready = p.sig("gate_up_ready"), p.sig("ffn_exp_ready"), p.sig("ffn_act_ready")
    dve_step = p.sig("ffn_dve_step")
    picked, gathered, hJ_ready = p.sig("pick_ready"), p.sig("tokens_gathered"), p.sig("hJ_ready")
    wt_turned, wt_kept = p.sig("wt_turned"), p.sig("wt_kept")
    y_kept, scattered, added = p.sig("job_y_kept"), p.sig("scattered"), p.sig("y_added")
    pair_rounds = 2 * FC // RING
    inner = (FC - 2) // RING

    def at(signal, i, per_pair, turn, per_turn, n):
        return signal.sem, i * per_pair + turn * per_turn + (signal.base + n)

    def chunks(eng, b, step):
        for c in range(2):
            step(0, b * FC + c)
        with eng.Fori(0, inner) as turn:
            for r in range(RING):
                step(turn, b * FC + 2 + r)

    with nc.Block(no_gpsimd_drain=True) as block:
        @block.sync
        def _(sp):
            pairs = sp.value_load(p.trip[0:1, 0:1], min_val=4, max_val=8)
            with sp.Fori(1, pairs * pair_rounds) as rnd:
                for r in range(RING):
                    g = g0 + r
                    sp.wait_ge(p.slot_free.sem, rnd * RING + (g - RING + 1))
                    chunk = (rnd % (4 * pair_rounds)) * RING + r
                    sp.dma_start(p.ring[:, g % RING, :],
                                 p.ap["moe"][bass.ds(chunk, 1)].rearrange("o p f -> (o p) f")
                                 ).then_inc(p.slot_loaded[g % RING].sem, 16)

        @block.tensor
        def _(pe):
            pairs = pe.value_load(p.trip[0:1, 0:1], min_val=4, max_val=8)

            def gather(i, j, part):
                if part == 0:
                    pe.wait_ge(*at(picked, i, 2, 0, 0, j + 1))
                    pe.wait_ge(*at(added, i, 8, 0, 0, 4 * j))
                for k in range(4 * part, 4 * part + 4):
                    for t in range(NT):
                        mm = pe.matmul(p.ps[6 + part][:, (k % 4) * P:(k % 4) * P + P], xn[:, t, k * P:k * P + P],
                                       pick[:, j % 2, t, :], start=t == 0, stop=t == NT - 1)
                mm.then_inc(gathered.sem, 1)

            def turn_weights(j):
                for t in range(NT):
                    mm = pe.transpose(p.ps[4][:, t * P:t * P + P], pickw[:, j % 2, t, :], p.ident[:, :])
                mm.then_inc(wt_turned.sem, 1)

            def down(i, turn, k):
                pe.wait_ge(*at(act_ready, i, 2 * FC, turn, RING, k + 1))
                w = p.ring[:, (g0 + k) % RING, 2 * KT * P:3 * KT * P]
                first, last = k % FC == 0, k % FC == FC - 1
                for hf in range(2):
                    mm = pe.matmul(p.ps[hf][:, :], aJ[:, k % 2, :], w[:, hf * 512:hf * 512 + 512],
                                   start=first, stop=last, skip_group_check=True)
                mm.then_inc(p.slot_free.sem, 1)

            def up(i, turn, k):
                g = g0 + k
                pe.wait_ge(p.slot_loaded[g % RING].sem, i * (16 * pair_rounds) + turn * 16 + 16 * (g // RING + 1))
                pe.wait_ge(*at(act_ready, i, 2 * FC, turn, RING, k - 1))
                w = p.ring[:, g % RING, 0:2 * KT * P].rearrange("p (u k f) -> p u k f", u=2, k=KT)
                for u in range(2):
                    for kt in range(KT):
                        mm = pe.matmul(p.ps[2 + k % 2][:, u * P:u * P + P], w[:, u, kt, :],
                                       hJ[:, k // FC, kt, :], start=kt == 0, stop=kt == KT - 1)
                mm.then_inc(gu_ready.sem, 1)

            gather(0, 0, 0)
            gather(0, 0, 1)
            turn_weights(0)
            with pe.Fori(0, pairs) as i:
                for b in range(2):
                    k0 = b * FC
                    pe.wait_ge(*at(hJ_ready, i, 2, 0, 0, b + 1))
                    up(i, 0, k0)
                    up(i, 0, k0 + 1)
                    down(i, 0, k0)
                    with pe.Fori(0, inner) as turn:
                        for r in range(RING):
                            up(i, turn, k0 + 2 + r)
                            down(i, turn, k0 + 1 + r)
                    gather(i, b + 1, 0)
                    down(i, 0, k0 + FC - 1)
                    gather(i, b + 1, 1)
                    turn_weights(b + 1)
                    pe.wait_ge(*at(y_kept, i, 2, 0, 0, b + 1))
                    pe.wait_ge(*at(wt_kept, i, 2, 0, 0, b + 2))
                    pe.wait_ge(*at(hJ_ready, i, 2, 0, 0, b + 2))
                    for q in range(4):
                        t, hf = q // 2, q % 2
                        pe.matmul(p.ps[4 + q][:, :], WT[:, b, t * P:t * P + P], yS[:, hf * 512:hf * 512 + 512],
                                  start=True, stop=True).then_inc(scattered.sem, 1)

        @block.scalar
        def _(act):
            pairs = act.value_load(p.trip[0:1, 0:1], min_val=4, max_val=8)

            def keep_weights(i, j):
                act.wait_ge(*at(wt_turned, i, 2, 0, 0, j + 1))
                act.activation(WT[:, j % 2, :], p.ps[4][:, 0:T], ACT.Copy).then_inc(wt_kept.sem, 1)

            keep_weights(0, 0)
            with act.Fori(0, pairs) as i:
                for b in range(2):
                    def step(turn, k):
                        act.wait_ge(*at(gu_ready, i, 2 * FC, turn, RING, k + 1))
                        act.wait_ge(*at(act_ready, i, 2 * FC, turn, RING, k - 1))
                        act.activation(ex[:, k % 2, :], p.ps[2 + k % 2][:, 0:P], ACT.Exp,
                                       scale=-1.0).then_inc(exp_ready.sem, 1)
                    chunks(act, b, step)
                    act.wait_ge(p.slot_free.sem, i * (2 * FC) + (g0 + (b + 1) * FC))
                    act.activation(yS[:, 0:512], p.ps[0][:, :], ACT.Copy)
                    act.activation(yS[:, 512:1024], p.ps[1][:, :], ACT.Copy).then_inc(y_kept.sem, 1)
                    keep_weights(i, b + 1)

        @block.vector
        def _(dve):
            pairs = dve.value_load(p.trip[0:1, 0:1], min_val=4, max_val=8)
            iota = p.con_at(CON2, "iota")
            dve.sem_inc(added.sem, 4)

            def make_pick(i, j):
                for t in range(NT):
                    job = slice(0, 1) if isinstance(i, int) else bass.ds(i * 2 + j, 1)
                    sl, wt = p.slot[:, t, job], p.weight[:, t, job]
                    dve.tensor_scalar(pick[:, j % 2, t, :], iota, sl, None, ALU.is_equal)
                    ins = dve.tensor_scalar(pickw[:, j % 2, t, :], iota, sl, wt, ALU.is_equal, ALU.mult)
                ins.then_inc(picked.sem, 1)

            def keep_gathered(i, j):
                for part in range(2):
                    dve.wait_ge(*at(gathered, i, 4, 0, 0, 2 * j + part + 1))
                    ins = dve.tensor_tensor(hJ[:, j % 2, 4 * part:4 * part + 4, :],
                                            p.ps[6 + part][:, :].rearrange("p (k s) -> p k s", k=4),
                                            gain[:, 4 * part:4 * part + 4].unsqueeze(2).broadcast_to([P, 4, P]),
                                            ALU.mult)
                ins.then_inc(hJ_ready.sem, 1)

            make_pick(0, 0)
            keep_gathered(0, 0)
            with dve.Fori(0, pairs) as i:
                for b in range(2):
                    make_pick(i, b + 1)

                    def step(turn, k):
                        e, r, a = ex[:, k % 2, :], rc[:, k % 2, :], aJ[:, k % 2, :]
                        bank = p.ps[2 + k % 2]
                        dve.wait_ge(*at(exp_ready, i, 2 * FC, turn, RING, k + 1))
                        dve.tensor_scalar(e, e, 1.0, None, ALU.add).then_inc(dve_step.sem, 1)
                        dve.wait_ge(*at(dve_step, i, 6 * FC, turn, 3 * RING, 3 * k + 1))
                        dve.reciprocal(r, e).then_inc(dve_step.sem, 1)
                        dve.wait_ge(*at(dve_step, i, 6 * FC, turn, 3 * RING, 3 * k + 2))
                        dve.tensor_tensor(r, r, bank[:, 0:P], ALU.mult).then_inc(dve_step.sem, 1)
                        dve.wait_ge(*at(dve_step, i, 6 * FC, turn, 3 * RING, 3 * k + 3))
                        dve.wait_ge(p.slot_free.sem, i * (2 * FC) + turn * RING + (g0 + k - 1))
                        dve.tensor_tensor(a, r, bank[:, P:2 * P], ALU.mult).then_inc(act_ready.sem, 1)
                    chunks(dve, b, step)
                    keep_gathered(i, b + 1)
                    for q in range(4):
                        t, hf = q // 2, q % 2
                        x = p.x[:, t, hf * 512:hf * 512 + 512]
                        dve.wait_ge(*at(scattered, i, 8, 0, 0, 4 * b + q + 1))
                        dve.tensor_tensor(x, x, p.ps[4 + q][:, :], ALU.add).then_inc(added.sem, 1)
    p.end_stream()


def odd_layer(p):
    norm_src(p, p.x, p.col("od_mix"))
    linear(p, None, 7, out=p.proj[:, :, 0:O_COLS])
    w1 = [v.rearrange("p a d -> p (a d)")[0:HD, :].rearrange("p (i j) -> p i j", i=32) for v in (p.gates[:], p.ctx[:])]
    free = p.oT[:].rearrange("p k t -> p (k t)")
    w2 = free[0:HD, 1536:1664].rearrange("p (k j) -> p k j", k=2)
    w_uq = free[:, 0:1536].rearrange("p (k c) -> p k c", k=2)
    w_ukv = p.projc[:].rearrange("p t c -> p (t c)")[:, 2048:3072]
    load_small(p, [(w1[0], p.ap["cmp_w1"][:, 0]), (w1[1], p.ap["cmp_w1"][:, 1]), (w2, p.ap["cmp_w2"]),
                   (w_uq, p.ap["w_uq"]), (w_ukv, p.ap["w_ukv"]), (p.side[:], p.ap["router"])])
    split_side(p)
    nsa(p, w1, w2)
    o = mla(p, w_uq, w_ukv)
    turn(p, o_groups(p, [(k, (lambda k: lambda t: p.proj[:, t, k * P:k * P + P])(k)) for k in range(4)])
         + o_groups(p, [(4 + k, (lambda k: lambda t: o[:, t, k * P:k * P + P])(k)) for k in range(4)]))
    linear(p, p.oT, 4, residual=p.x)
    norm_src(p, p.x, p.col("od_ffn"))
    route(p)
    moe(p, p.col("od_ffn"))


def build(nc, ap, dbg=None, upto=None):
    p = Program(nc, ap)
    dense = SLOT
    p.streams = [
        Stream("w_ada0", 16, KT * AC), Stream("w_in0", 6, KT * PC), Stream("w_in0", 6, KT * PC),
        Stream("w_out0", 4, KT * PC), Stream("ffn0", FC, dense),
        Stream("w_out0", 4, KT * PC), Stream("ffn0", FC, dense),
        Stream("w_ada1", 16, KT * AC), Stream("w_in1", 6, KT * PC), Stream("w_in1", 6, KT * PC),
        Stream("w_out1", 4, KT * PC), Stream("ffn1", FC, dense),
        Stream("ev_in", 12, KT * PC), Stream("ev_out", 4, KT * PC), Stream("ffn_ev", FC, dense),
        Stream("od_in", 7, KT * PC), Stream("od_out", 4, KT * PC), Stream("moe", NE * FC, dense),
    ]
    load_small(p, [(p.x[:], ap["x"].rearrange("(t p) d -> p t d", p=P)),
                   (p.ctx[:], ap["ctx"].rearrange("(t p) d -> p t d", p=P)),
                   (p.cols[:], ap["cols"]), (p.ident[:], ap["ident"]), (p.side[:], ap["w_dt"]),
                   (p.con[:, 0:N_CON1], ap["con1"]),
                   (p.rows[:, 0:N_ROWS1], ap["rows1"].broadcast_to([P, N_ROWS1]))])
    split_side(p)
    block1(p)
    load_small(p, [(p.con[:, 0:N_CON2], ap["con2"]),
                   (p.rows[:, 0:N_ROWS2], ap["rows2"].broadcast_to([P, N_ROWS2])),
                   (p.gates[:, 0, 0:512], ap["ssm_norm"].broadcast_to([P, 512]))])
    even_layer(p)
    odd_layer(p)
    stored = p.sig("stored")
    with nc.Block(no_gpsimd_drain=True) as block:
        @block.sync
        def _(sp):
            sp.dma_start(ap["out"].rearrange("(t p) d -> p t d", p=P), p.x[:]).then_inc(stored.sem, 16)
            sp.wait_ge(*stored(16))
    return p


def constants():
    f = np.float32
    q = np.arange(T)
    tile = lambda m: np.ascontiguousarray(m.reshape(NT, P, -1).transpose(1, 0, 2).reshape(P, -1)).astype(f)
    window = np.concatenate([np.zeros((T, T)), np.where(np.abs(q[None] - q[:, None]) <= 128, 0.0, NEG)], 1)
    ang = 2 * np.pi * (np.outer(q, q) % T) / T
    dft_seq = np.concatenate([np.cos(ang), np.sin(ang)], 1) / 16.0
    ch = np.arange(HD)
    a2 = 2 * np.pi * (np.outer(ch, ch) % HD) / HD
    two = np.eye(2)
    dft_cos, dft_sin = np.kron(two, np.cos(a2)) / 8.0, -np.kron(two, np.sin(a2)) / 8.0

    def tables(ang):
        c, s = np.cos(ang), np.sin(ang)
        return np.concatenate([c, c], 1), np.concatenate([-s, s], 1)
    inv1 = (f(10000.0) ** (-np.arange(0, 32, 2, dtype=f) / f(32))).astype(f)
    row, colp = (q // 64).astype(f), (q % 64).astype(f)
    c1, s1 = tables(np.concatenate([row[:, None] * inv1, colp[:, None] * inv1], 1).astype(f).astype(np.float64))
    inv2 = (f(1.0) / (f(10000.0) ** (np.arange(0, 64, 2, dtype=f) / f(64)))).astype(f)
    c2, s2 = tables((q.astype(f)[:, None] * inv2[None]).astype(f).astype(np.float64))
    end = np.arange(N_CMP) * 16 + 31
    pad = lambda m: np.concatenate([m, np.zeros((P - len(m), m.shape[1]))], 0).astype(f)
    valid = end[None] <= q[:, None]
    tri = (q[:, None] <= q[None]).astype(f)
    con1 = np.concatenate([tile(window), tile(dft_seq), dft_cos.astype(f), dft_sin.astype(f), tile(c1), tile(s1)], 1)
    con2 = np.concatenate([tile(np.where(q[None] <= q[:, None], 0.0, NEG)), tile(tri), tile(np.where(tri > 0, 0.0, NEG)),
                           tile(c2), tile(s2), pad(c2[end]), pad(s2[end]), tile(np.where(valid, 0.0, NEG)),
                           tile(valid.astype(f)), np.tile(np.arange(P, dtype=f), (P, 1))], 1)
    assert con1.shape[1] == N_CON1 and con2.shape[1] == N_CON2
    return con1, con2


def kernel(**inputs):
    import concourse.bacc as bacc
    from concourse.bass_utils import run_bass_kernel_spmd

    a = {k: np.asarray(v) for k, v in inputs.items()}
    arrays = {}

    def feature_columns(v):
        return v.reshape(-1, P).T

    def chunks(w, width):
        n = -(-w.shape[1] // width)
        if n * width != w.shape[1]:
            w = np.concatenate([w, np.zeros((w.shape[0], n * width - w.shape[1]), w.dtype)], 1)
        return np.ascontiguousarray(w.reshape(KT, P, n, width).transpose(2, 1, 0, 3).reshape(n, P, KT * width))

    def ffn_chunks(gate, up, down):
        n = gate.shape[-1] // P
        out = np.empty((n, P, 3, KT * P), gate.dtype)
        for i, w in enumerate((gate, up)):
            out[:, :, i].reshape(n, P, KT, P)[:] = w.reshape(KT, P, n, P).transpose(2, 1, 0, 3)
        out[:, :, 2] = down.reshape(n, P, D)
        return out.reshape(n, P, SLOT)

    arrays["x"] = a["x"].reshape(T, D)
    arrays["ctx"] = a["ctx"].reshape(T, D)
    arrays["b_ada"] = a["b_ada"]
    for l in range(2):
        arrays[f"w_ada{l}"] = chunks(a["w_ada"][l], AC)
        arrays[f"w_in{l}"] = chunks(a["w_in"][l], PC)
        arrays[f"w_out{l}"] = chunks(a["w_out"][l], PC)
        arrays[f"ffn{l}"] = ffn_chunks(a["w_gate"][l], a["w_up"][l], a["w_down"][l])
    ev = a["ev_w_in_2"][0]
    arrays["ev_in"] = chunks(ev[:, 0:3072], PC)
    arrays["w_dt"] = np.ascontiguousarray(ev[:, 3072:3080].reshape(KT, P, 8).transpose(1, 0, 2))
    arrays["ev_out"] = chunks(a["ev_w_out_2"][0], PC)
    arrays["ffn_ev"] = ffn_chunks(a["ffn_w_gate_2"][0], a["ffn_w_up_2"][0], a["ffn_w_down_2"][0])
    arrays["od_in"] = chunks(a["od_w_in_2"][0], PC)
    arrays["od_out"] = chunks(a["od_w_out_2"][0], PC)
    arrays["moe"] = np.concatenate([ffn_chunks(a["moe_w_gate_2"][0, e], a["moe_w_up_2"][0, e], a["moe_w_down_2"][0, e])
                                    for e in range(NE)])
    arrays["router"] = np.ascontiguousarray(a["moe_router_2"][0].reshape(KT, P, NE).transpose(1, 0, 2))
    arrays["cmp_w1"] = np.ascontiguousarray(a["nsa_cmp_w1_2"][0].reshape(2, 32, HD, HD).transpose(2, 0, 1, 3))
    arrays["cmp_w2"] = np.ascontiguousarray(a["nsa_cmp_w2_2"][0].transpose(1, 0, 2))
    arrays["w_uq"] = np.ascontiguousarray(a["mla_w_uq_2"][0].reshape(2, P, 768).transpose(1, 0, 2))
    arrays["w_ukv"] = a["mla_w_ukv_2"][0]
    pos = a["nsa_cmp_pos_2"][0].transpose(2, 0, 1).reshape(HD, 64)
    arrays["cols"] = np.concatenate([
        feature_columns(a["g_mix"]), feature_columns(a["g_ffn"]), feature_columns(a["ev_norm_mix_2"][0]),
        feature_columns(a["ev_norm_ffn_2"][0]), feature_columns(a["od_norm_mix_2"][0]),
        feature_columns(a["od_norm_ffn_2"][0]),
        np.stack([a["c"][0].reshape(KT, P), a["c_ctx"].reshape(KT, P)], -1).transpose(1, 0, 2).reshape(P, 16),
        a["ssm_conv_w_2"][0].reshape(4, KT, P).transpose(2, 1, 0).reshape(P, 32),
        feature_columns(a["ssm_conv_b_2"][0]), np.concatenate([pos, np.zeros_like(pos)], 0)], 1)
    arrays["rows1"] = np.concatenate([a[k].reshape(-1) for k in ("q_norm", "k_norm", "sink", "g_final")])[None]
    arrays["rows2"] = np.concatenate([a[k + "_2"].reshape(-1) for k in (
        "da_q_gain", "da_k_gain", "da_lambda", "da_subln_gain", "ssm_dt_bias", "ssm_a_log", "ssm_d",
        "nsa_q_gain", "nsa_k_gain", "mla_cq_gain", "mla_ckv_gain", "mla_qn_gain", "mla_qr_gain",
        "mla_kn_gain", "mla_kr_gain")])[None]
    arrays["ssm_norm"] = a["ssm_norm_gain_2"].reshape(1, 512)
    arrays["con1"], arrays["con2"] = constants()
    arrays["ident"] = np.eye(P, dtype=np.float32)

    nc = bacc.Bacc("TRN2", target_bir_lowering=False, num_devices=1)
    ap, maps = {}, {}
    for name, v in arrays.items():
        v = np.ascontiguousarray(v)
        maps[f"in_{name}"] = v
        ap[name] = nc.dram_tensor(f"in_{name}", v.shape, F32, kind="ExternalInput").ap()
    ap["out"] = nc.dram_tensor("out_x", (T, D), F32, kind="ExternalOutput").ap()
    build(nc, ap)
    r = run_bass_kernel_spmd(nc, [maps], core_ids=[0])
    return r.results[0]["out_x"].reshape(1, T, D)
```

```python
import math

import numpy as np

import concourse.bass as bass
from concourse import mybir

F32 = mybir.dt.float32
F32R = mybir.dt.float32r
U32 = mybir.dt.uint32
ALU = mybir.AluOpType
ACT = mybir.ActivationFunctionType
AX_X = mybir.AxisListType.X

P = 128
T = 256
NT = T // P
D = 1024
KT = D // P
HD = 64
F = 2816
FC = F // P
NE = 8
EPS = 1e-6
NEG = -1e30

RING = 4
SLOT = 3 * KT * P
PIECE = KT * P
PC = 256

A_COLS = 1536
O_COLS = 1752
SSM_H = 8
N_CMP = T // 16 - 1
LAM_INIT = 0.8 - 0.6 * math.exp(-0.3 * 0)


def pack(fields):
    at, where = 0, {}
    for name, n in fields:
        where[name] = (at, at + n)
        at += n
    return where, at


COLS, N_COLS = pack([("g_mix", 16), ("g_ffn", 16), ("ev_mix", 8), ("ev_ffn", 8), ("od_mix", 8),
                     ("od_ffn", 8), ("c", 16), ("conv_w", 32), ("conv_b", 8), ("cmp_pos", 64)])
ROWS1, N_ROWS1 = pack([("q_norm", 2 * HD), ("k_norm", 2 * HD), ("sink", 12), ("g_final", D)])
ROWS2, N_ROWS2 = pack([("da_q", HD), ("da_k", HD), ("da_lam", 4 * HD), ("subln", 128), ("dt_bias", 8),
                       ("a_log", 8), ("ssm_d", 8), ("nsa_q", HD), ("nsa_k", 3 * HD),
                       ("cq", 256), ("ckv", 128), ("qn", 128), ("qr", HD), ("kn", 128), ("kr", HD)])
N_ROWS = max(N_ROWS1, N_ROWS2)
CON1, N_CON1 = pack([("window", NT * 2 * T), ("dft_seq", NT * 2 * T), ("dft_cos", P), ("dft_sin", P),
                     ("rope_c", NT * HD), ("rope_s", NT * HD)])
CON2, N_CON2 = pack([("causal", NT * T), ("tri", NT * T), ("tri_mask", NT * T), ("rope_c", NT * HD),
                     ("rope_s", NT * HD), ("cmp_c", HD), ("cmp_s", HD), ("cmp_mask", NT * N_CMP),
                     ("cmp_valid", NT * N_CMP), ("iota", P)])
N_CON = max(N_CON1, N_CON2)


class Signal:

    def __init__(self, nc, name):
        self.sem, self.base = nc.alloc_semaphore(name), 0

    def __call__(self, n):
        return self.sem, self.base + n

    def passed(self, n):
        self.base += n


class Chain:

    def __init__(self, eng, steps):
        self.eng, self.steps = eng, steps

    def __call__(self, ins):
        ins.then_inc(self.steps.sem, 1)
        self.steps.passed(1)
        self.eng.wait_ge(*self.steps(0))


class Stream:

    def __init__(self, src, n, width):
        self.src, self.n, self.width = src, n, width


class Program:
    def __init__(self, nc, ap):
        self.nc, self.ap = nc, ap

        def sb(name, *shape):
            return nc.alloc_sbuf_tensor(name, [P, *shape], F32)

        self.ring = sb("ring", RING, SLOT)
        self.x = sb("x_res", NT, D)
        self.ctx = sb("ctx_res", NT, D)
        self.oT = sb("oT", KT, T)
        self.proj = sb("proj", NT, 2056)
        self.projc = sb("projc", NT, A_COLS)
        self.big = sb("big", 24 * T)
        self.srcH = nc.alloc_sbuf_tensor("src_hi", [P, KT, T], F32R)
        self.srcL = nc.alloc_sbuf_tensor("src_lo", [P, KT, T], F32R)
        self.actH = nc.alloc_sbuf_tensor("act_hi", [P, T], F32R)
        self.actL = nc.alloc_sbuf_tensor("act_lo", [P, T], F32R)
        self.sideH = nc.alloc_sbuf_tensor("side_hi", [P, KT, NE], F32R)
        self.sideL = nc.alloc_sbuf_tensor("side_lo", [P, KT, NE], F32R)
        self.wH = nc.alloc_sbuf_tensor("w_hi", [P, 3, PIECE], F32R)
        self.wL = nc.alloc_sbuf_tensor("w_lo", [P, 3, PIECE], F32R)
        self.work = sb("work", 3072)
        self.gates = sb("gates", 2, D)
        self.cols = sb("cols", N_COLS)
        self.rows = sb("rows", N_ROWS)
        self.con = sb("con", N_CON)
        self.xn = self.big[:, 4096:6144].rearrange("p (t d) -> p t d", t=NT)
        self.mod_rows = nc.dram_tensor("mod_rows", (2, 6 * D), F32, kind="Internal").ap()
        self.ident = sb("ident", P)
        self.mod = sb("mod", 4 * KT, 2)
        self.scl = sb("scl", 2, 2, KT)
        self.small = sb("small", 256)
        self.neg_half = sb("neg_half", 4 * SSM_H)
        self.slot = sb("slot", NT, 2 * NE + 2)
        self.weight = sb("weight", NT, 2 * NE + 2)
        self.stat = sb("stat", 4, 4)
        self.side = sb("side", KT, NE)
        self.trip = nc.alloc_sbuf_tensor("trip", [P, 1], mybir.dt.int32)
        self.idx = nc.alloc_sbuf_tensor("idx", [P, 8], U32)
        self.ps = [nc.alloc_psum_tensor(f"bank{i}", [P, 512], F32) for i in range(8)]

        self.slot_loaded = [Signal(nc, f"slot_loaded{i}") for i in range(RING)]
        self.slot_free = Signal(nc, "slot_free")
        self.w_hi = [Signal(nc, f"w_hi{i}") for i in range(3)]
        self.w_lo = [Signal(nc, f"w_lo{i}") for i in range(3)]
        self.w_used = [Signal(nc, f"w_used{i}") for i in range(3)]
        self.names = {}
        self.meansq, self.rstd, self.roots = Signal(nc, "meansq_ready"), Signal(nc, "rstd_ready"), 0
        self.streams, self.stream_at = [], 0
        self.used = 0
        self.preloaded = 0

    def sig(self, name):
        if name not in self.names:
            self.names[name] = Signal(self.nc, name)
        return self.names[name]

    def con_at(self, where, name, *shape):
        a, b = where[name]
        v = self.con[:, a:b]
        return v if not shape else v.rearrange("p (a b) -> p a b", a=shape[0])

    def row(self, where, name, i=0, n=None):
        a, b = where[name]
        n = n or b - a
        return self.rows[:, a + i * n:a + i * n + n]

    def col(self, name, i=0, n=KT):
        a = COLS[name][0]
        return self.cols[:, a + i * n:a + i * n + n]

    def load_chunk(self, sp, stream, c, g, turn=0, wait=True):
        slot = g % RING
        if wait:
            sp.wait_ge(self.slot_free.sem, turn * RING + (g - RING + 1))
        src = self.ap[stream.src]
        src = src[c] if isinstance(c, int) else src[bass.ds(c, 1)].rearrange("o p f -> (o p) f")
        sp.dma_start(self.ring[:, slot, 0:stream.width], src).then_inc(self.slot_loaded[slot].sem, 16)

    def load_stream(self, sp):
        s = self.streams[self.stream_at]
        g0, c = self.used, self.preloaded
        while g0 + c < RING:
            self.load_chunk(sp, s, c, g0 + c, wait=False)
            c += 1
        turns = (s.n - c) // RING
        if turns > 1:
            with sp.Fori(0, turns) as i:
                for r in range(RING):
                    self.load_chunk(sp, s, i * RING + (c + r), g0 + c + r, i)
            c += turns * RING
        for c in range(c, s.n):
            self.load_chunk(sp, s, c, g0 + c)
        self.preloaded = 0
        if self.stream_at + 1 < len(self.streams):
            after = self.streams[self.stream_at + 1]
            self.preloaded = min(RING, after.n)
            for c in range(self.preloaded):
                self.load_chunk(sp, after, c, g0 + s.n + c)

    def end_stream(self):
        s = self.streams[self.stream_at]
        self.used += s.n
        self.stream_at += 1

    def wait_chunk(self, pe, g, turn=0):
        pe.wait_ge(self.slot_loaded[g % RING].sem, 16 * turn + 16 * (g // RING + 1))


def load_small(p, jobs):
    done = p.sig("small_loaded")
    with p.nc.Block(no_gpsimd_drain=True) as block:
        @block.scalar
        def _(act):
            for dst, src in jobs:
                act.dma_start(dst, src).then_inc(done.sem, 16)
            act.wait_ge(*done(16 * len(jobs)))

        @block.vector
        def _(dve):
            chain = Chain(dve, p.sig("dve_chain"))
            chain(dve.memset(p.neg_half[:], -0.5))
    done.passed(16 * len(jobs))


def start_loads(p, act, loads):
    for dst, src in loads:
        act.dma_start(dst, src).then_inc(p.sig("small_loaded").sem, 16)


def end_loads(p, act, loads):
    p.sig("small_loaded").passed(16 * len(loads))
    if loads:
        act.wait_ge(*p.sig("small_loaded")(0))


def gate_load(p, i, row):
    a = (2 * D, 5 * D)[i]
    return p.gates[:, i, :], p.mod_rows[row:row + 1, a:a + D].broadcast_to([P, D])


def adaln(p, l, loads):
    nc = p.nc
    mrow = p.big[0:2, 0:6 * D]
    cT = p.col("c", 0, 16).rearrange("p (k v) -> p k v", v=2)
    scT = p.small[:, 0:16].rearrange("p (k v) -> p k v", v=2)
    bias_in, silu_e, silu_done = p.sig("ada_bias_loaded"), p.sig("silu_exp"), p.sig("ada_silu")
    ready, added = p.sig("ada_chunk_ready"), p.sig("ada_chunk_added")
    turned, rows_out = p.sig("ada_turned"), p.sig("mod_rows_out")
    n = 6 * D // PC
    scH, scL = [v[:].rearrange("p k n -> p (k n)")[:, 0:2 * KT].rearrange("p (k v) -> p k v", v=2)
                for v in (p.sideH, p.sideL)]
    sc_kept, sc_hi = p.sig("ada_sc_kept"), p.sig("ada_sc_hi")
    g0 = p.used
    wanted = [8 * b + k for b in (0, 1, 3, 4) for k in range(8)]
    with nc.Block(no_gpsimd_drain=True) as block:
        @block.sync
        def _(sp):
            p.load_stream(sp)

        @block.scalar
        def _(act):
            act.dma_start(mrow, p.ap["b_ada"][l:l + 1, :].broadcast_to([2, 6 * D])).then_inc(bias_in.sem, 16)
            act.activation(p.small[:, 16:32], p.col("c", 0, 16), ACT.Exp, scale=-1.0).then_inc(silu_e.sem, 1)
            act.wait_ge(*sc_kept(1))
            act.activation(scH, scT, ACT.Copy).then_inc(sc_hi.sem, 1)
            for q in range(2 * n):
                if q == 3:
                    start_loads(p, act, loads)
                g, b = g0 + q // 2, q % 3
                if q % 2 == 0:
                    p.wait_chunk(act, g)
                if q >= 3:
                    act.wait_ge(*p.w_used[b](q // 3))
                act.activation(p.wH[:, b, :], p.ring[:, g % RING, (q % 2) * PIECE:(q % 2 + 1) * PIECE],
                               ACT.Copy).then_inc(p.w_hi[b].sem, 1)
            act.wait_ge(*added(n))
            act.dma_start(p.mod_rows, mrow).then_inc(rows_out.sem, 16)
            act.wait_ge(*rows_out(16))
            end_loads(p, act, loads)

        @block.tensor
        def _(pe):
            pe.wait_ge(*silu_done(1))
            for q in range(2 * n):
                c, h, b = q // 2, q % 2, q % 3
                pe.wait_ge(*p.w_lo[b](q // 3 + 1))
                if h == 0 and c >= 2:
                    pe.wait_ge(*added(c - 1))
                w = [v[:, b, :].rearrange("p (k n) -> p k n", k=4) for v in (p.wH, p.wL)]
                mm = products(pe, p.ps[c % 2][0:2, 0:PC],
                              [((scH[:, 4 * h + k, :], scL[:, 4 * h + k, :]), (w[0][:, k, :], w[1][:, k, :]))
                               for k in range(4)], h == 0, h == 1)
                mm.then_inc(p.w_used[b].sem, 1)
                if h:
                    pe.wait_ge(*p.w_used[b](q // 3 + 1))
                    pe.sem_inc(ready.sem, 1)
            pe.wait_ge(*added(n))
            for j, f in enumerate(wanted):
                mm = pe.transpose(p.ps[2][:, 2 * j:2 * j + 2], mrow[:, f * P:f * P + P], p.ident[0:2, 0:2])
            mm.then_inc(turned.sem, 1)

        @block.vector
        def _(dve):
            chain = Chain(dve, p.sig("dve_chain"))
            dve.wait_ge(*silu_e(1))
            chain(dve.tensor_scalar(p.small[:, 16:32], p.small[:, 16:32], 1.0, None, ALU.add))
            chain(dve.reciprocal(p.small[:, 32:48], p.small[:, 16:32]))
            dve.tensor_tensor(p.small[:, 0:16], p.col("c", 0, 16), p.small[:, 32:48],
                              ALU.mult).then_inc(sc_kept.sem, 1)
            dve.wait_ge(*sc_hi(1))
            dve.wait_ge(*sc_kept(1))
            dve.tensor_tensor(scL, scT, scH.bitcast(F32), ALU.subtract).then_inc(silu_done.sem, 1)
            dve.wait_ge(*bias_in(16))

            def split(q):
                g, b = g0 + q // 2, q % 3
                dve.wait_ge(*p.w_hi[b](q // 3 + 1))
                dve.tensor_tensor(p.wL[:, b, :], p.ring[:, g % RING, (q % 2) * PIECE:(q % 2 + 1) * PIECE],
                                  p.wH[:, b, :].bitcast(F32), ALU.subtract).then_inc(p.w_lo[b].sem, 1)
                if q % 2:
                    dve.wait_ge(*p.w_lo[b](q // 3 + 1))
                    dve.sem_inc(p.slot_free.sem, 1)

            for c in range(n + 1):
                if c < n:
                    split(2 * c)
                    split(2 * c + 1)
                if c:
                    dve.wait_ge(*ready(c))
                    m = mrow[:, (c - 1) * PC:c * PC]
                    dve.tensor_tensor(m, m, p.ps[(c - 1) % 2][0:2, 0:PC], ALU.add).then_inc(added.sem, 1)
            dve.wait_ge(*turned(1))
            mod = p.mod[:].rearrange("p f v -> p (f v)")
            chain(dve.tensor_copy(mod, p.ps[2][:, 0:64]))
            for i, name in enumerate(("g_mix", "g_ffn")):
                for r in range(2):
                    chain(dve.scalar_tensor_tensor(out=p.scl[:, i, r, :], in0=p.mod[:, 16 * i + 8:16 * i + 16, r],
                                                   scalar=1.0, in1=p.col(name, l), op0=ALU.add, op1=ALU.mult))
    for s, k in ((bias_in, 16), (silu_e, 1), (silu_done, 1), (ready, n), (added, n), (turned, 1), (rows_out, 16),
                 (sc_kept, 1), (sc_hi, 1)):
        s.passed(k)
    for b in range(3):
        k = len(range(b, 2 * n, 3))
        for s in (p.w_hi[b], p.w_lo[b], p.w_used[b]):
            s.passed(k)
    p.slot_free.passed(n)
    p.end_stream()


def rsqrt(p, dve, st):
    p.meansq.passed(1)
    p.rstd.passed(1)
    dve.wait_ge(*p.rstd(0))


def rsqrts(p, pool, widths, parts=P):
    for w in widths:
        p.roots += 1
        pool.wait_ge(p.meansq.sem, p.roots)
        v = p.small[0:parts, 0:w]
        pool.tensor_tensor(v, v, p.neg_half[0:parts, 0:w], ALU.pow).then_inc(p.rstd.sem, 1)


def rstd_of(p, chain, dve, src, n, junk, out):
    heads = src.shape[1]
    sq = junk[:, 0:heads * n].rearrange("p (h d) -> p h d", h=heads)
    chain(dve.tensor_tensor(sq, src, src, ALU.mult))
    chain(dve.tensor_reduce(out, sq, AX_X, ALU.add))
    dve.tensor_scalar(out, out, 1.0 / n, EPS, ALU.mult, ALU.add).then_inc(p.meansq.sem, 1)
    rsqrt(p, dve, out)


def norm_rows(p, chain, eng, src, gains, junk, on_pool=False):
    parts, tiles, heads, n = src.shape
    first = 224 if on_pool else 0
    st = p.small[:, first:first + tiles * heads]
    st3 = st.rearrange("p (t h) -> p t h", t=tiles)
    sq = junk[:, 0:tiles * heads * n].rearrange("p (t h d) -> p t h d", t=tiles, h=heads)
    chain(eng.tensor_tensor(sq, src, src, ALU.mult))
    if on_pool:
        half = n // 2
        while half > 1:
            chain(eng.tensor_tensor(sq[:, :, :, 0:half], sq[:, :, :, 0:half], sq[:, :, :, half:2 * half], ALU.add))
            half //= 2
        chain(eng.tensor_tensor(st3.unsqueeze(3), sq[:, :, :, 0:1], sq[:, :, :, 1:2], ALU.add))
        chain(eng.tensor_scalar(st, st, 1.0 / n, EPS, ALU.mult, ALU.add))
        chain(eng.tensor_tensor(st, st, p.neg_half[:, 0:tiles * heads], ALU.pow))
    else:
        chain(eng.tensor_reduce(st3, sq, AX_X, ALU.add))
        eng.tensor_scalar(st, st, 1.0 / n, EPS, ALU.mult, ALU.add).then_inc(p.meansq.sem, 1)
        rsqrt(p, eng, st)
    chain(eng.tensor_tensor(src, src, st3.unsqueeze(3).broadcast_to([parts, tiles, heads, n]), ALU.mult))
    for a, k, gain in gains:
        v = src[:, :, a:a + k, :]
        chain(eng.tensor_tensor(v, v, gain.unsqueeze(1).unsqueeze(1).broadcast_to([parts, tiles, k, n]), ALU.mult))


def rope_rows(chain, eng, src, cos, sin, tmp):
    parts, tiles, heads, n = src.shape
    h, size = n // 2, tiles * heads * n
    a, b = [tmp[:, i * size:(i + 1) * size].rearrange("p (t h d) -> p t h d", t=tiles, h=heads) for i in range(2)]

    def wide(t):
        return t.unsqueeze(2).broadcast_to([parts, tiles, heads, t.shape[2]])
    eng.tensor_tensor(b[:, :, :, 0:h], src[:, :, :, h:n], wide(sin[:, :, 0:h]), ALU.mult)
    eng.tensor_tensor(b[:, :, :, h:n], src[:, :, :, 0:h], wide(sin[:, :, h:n]), ALU.mult)
    chain(eng.tensor_tensor(a, src, wide(cos), ALU.mult))
    chain(eng.tensor_tensor(src, a, b, ALU.add))


def heads_of(proj, a, n, d=HD):
    return proj[:, :, a:a + n * d].rearrange("p t (h d) -> p t h d", h=n)


def head_norm(p, chain, dve, src, gain, junk, stat):
    parts, heads, n = src.shape
    st = stat[:, 0:heads]
    rstd_of(p, chain, dve, src, n, junk, st)
    chain(dve.tensor_tensor(src, src, st.unsqueeze(2).broadcast_to([parts, heads, n]), ALU.mult))
    chain(dve.tensor_tensor(src, src, gain.unsqueeze(1).broadcast_to([parts, heads, n]), ALU.mult))


def rope(chain, dve, src, cos, sin, tmp):
    parts, heads, n = src.shape
    h = n // 2
    a = tmp[:, 0:heads * n].rearrange("p (h d) -> p h d", h=heads)
    b = tmp[:, heads * n:2 * heads * n].rearrange("p (h d) -> p h d", h=heads)

    def wide(t, k):
        return t.unsqueeze(1).broadcast_to([parts, heads, k])
    dve.tensor_tensor(b[:, :, 0:h], src[:, :, h:n], wide(sin[:, 0:h], h), ALU.mult)
    dve.tensor_tensor(b[:, :, h:n], src[:, :, 0:h], wide(sin[:, h:n], h), ALU.mult)
    chain(dve.tensor_tensor(a, src, wide(cos, n), ALU.mult))
    chain(dve.tensor_tensor(src, a, b, ALU.add))


def norm_src(p, src, scale, bias=None, loads=()):
    nc = p.nc
    xn, h = p.xn, p.work[:, 0:KT * T].rearrange("p (k t) -> p k t", k=KT)
    normed, turned, kept, hi, lo = (p.sig("x_normed"), p.sig("x_turned"), p.sig("h_kept"), p.sig("src_hi_ready"),
                                    p.sig("src_ready"))
    with nc.Block(no_gpsimd_drain=True) as block:
        @block.vector
        def _(dve):
            chain = Chain(dve, p.sig("dve_chain"))
            st = p.small[:, 0:NT]
            chain(dve.tensor_tensor_reduce(out=p.work[:, 0:D], in0=src[:, 0, :], in1=src[:, 0, :], scale=1.0,
                                           scalar=0.0, op0=ALU.mult, op1=ALU.add, accum_out=st[:, 0:1]))
            dve.wait_ge(*p.sig("square_sum")(1))
            dve.tensor_scalar(st, st, 1.0 / D, EPS, ALU.mult, ALU.add).then_inc(p.meansq.sem, 1)
            rsqrt(p, dve, st)
            dve.tensor_scalar(xn[:, 0, :], src[:, 0, :], st[:, 0:1], None, ALU.mult).then_inc(normed.sem, 1)

            def low(k):
                dve.wait_ge(*hi(k + 1))
                dve.tensor_tensor(p.srcL[:, k, :], h[:, k, :], p.srcH[:, k, :].bitcast(F32),
                                  ALU.subtract).then_inc(lo.sem, 1)
            for k in range(KT):
                dve.wait_ge(*turned(k + 1))
                dve.tensor_scalar(h[:, k, :], p.ps[k][:, 0:T], scale[:, k:k + 1],
                                  0.0 if bias is None else bias[:, k:k + 1], ALU.mult, ALU.add).then_inc(kept.sem, 1)
                if k:
                    low(k - 1)
            low(KT - 1)

        @block.gpsimd
        def _(pool):
            rsqrts(p, pool, [NT])

        @block.scalar
        def _(act):
            act.activation(p.work[:, D:2 * D], src[:, 1, :], ACT.Square,
                           accum_out=p.small[:, 1:2]).then_inc(p.sig("square_sum").sem, 1)
            start_loads(p, act, loads)
            act.wait_ge(*p.rstd(0))
            act.activation(xn[:, 1, :], src[:, 1, :], ACT.Identity, scale=p.small[:, 1:2]).then_inc(normed.sem, 1)
            for k in range(KT):
                act.wait_ge(*kept(k + 1))
                act.activation(p.srcH[:, k, :], h[:, k, :], ACT.Copy).then_inc(hi.sem, 1)
            end_loads(p, act, loads)

        @block.tensor
        def _(pe):
            pe.wait_ge(*normed(NT))
            for k in range(KT):
                for t in range(NT):
                    mm = pe.transpose(p.ps[k][:, t * P:t * P + P], xn[:, t, k * P:k * P + P], p.ident[:, :])
                mm.then_inc(turned.sem, 1)
    normed.passed(NT)
    p.sig("square_sum").passed(1)
    for s in (turned, kept, hi, lo):
        s.passed(KT)


def turn(p, groups):
    turned, kept_v, kept_a = p.sig("group_turned"), p.sig("group_kept_dve"), p.sig("group_kept_act")
    n = len(groups)
    with p.nc.Block(no_gpsimd_drain=True) as block:
        @block.tensor
        def _(pe):
            for j, (sources, _) in enumerate(groups):
                if j >= 4:
                    pe.wait_ge(*(kept_a if j % 2 else kept_v)((j - 4) // 2 + 1))
                for i, s in enumerate(sources):
                    parts, w = s.shape
                    mm = pe.transpose(p.ps[j % 4][0:w, i * P:i * P + parts], s, p.ident[0:parts, 0:parts])
                mm.then_inc(turned.sem, 1)

        @block.vector
        def _(dve):
            for j in range(0, n, 2):
                sources, dst = groups[j]
                dve.wait_ge(*turned(j + 1))
                dve.tensor_copy(dst, p.ps[j % 4][0:sources[0].shape[1], 0:dst.shape[1]]).then_inc(kept_v.sem, 1)

        @block.scalar
        def _(act):
            for j in range(1, n, 2):
                sources, dst = groups[j]
                act.wait_ge(*turned(j + 1))
                act.activation(dst, p.ps[j % 4][0:sources[0].shape[1], 0:dst.shape[1]],
                               ACT.Copy).then_inc(kept_a.sem, 1)
    turned.passed(n)
    kept_v.passed((n + 1) // 2)
    kept_a.passed(n // 2)


def products(pe, out, pairs, start, stop):
    n = len(pairs)
    for i, ((ah, al), (bh, bl)) in enumerate(pairs):
        pe.matmul(out, ah, bh, start=start and i == 0, stop=False, skip_group_check=True)
        pe.matmul(out, ah, bl, start=False, stop=False, skip_group_check=True)
        mm = pe.matmul(out, al, bh, start=False, stop=stop and i == n - 1, skip_group_check=True)
    return mm


def split_src_hi(p, act, src):
    for h in range(2):
        act.activation(p.srcH[:, 4 * h:4 * h + 4, :], src[:, 4 * h:4 * h + 4, :],
                       ACT.Copy).then_inc(p.sig("src_hi_ready").sem, 1)


def split_src_lo(p, dve, src):
    for h in range(2):
        dve.wait_ge(*p.sig("src_hi_ready")(h + 1))
        k = slice(4 * h, 4 * h + 4)
        dve.tensor_tensor(p.srcL[:, k, :], src[:, k, :], p.srcH[:, k, :].bitcast(F32),
                          ALU.subtract).then_inc(p.sig("src_ready").sem, 1)


def split_side(p):
    hi = p.sig("side_hi")
    with p.nc.Block(no_gpsimd_drain=True) as block:
        @block.scalar
        def _(act):
            act.activation(p.sideH[:], p.side[:], ACT.Copy).then_inc(hi.sem, 1)

        @block.vector
        def _(dve):
            chain = Chain(dve, p.sig("dve_chain"))
            dve.wait_ge(*hi(1))
            chain(dve.tensor_tensor(p.sideL[:], p.side[:], p.sideH[:].bitcast(F32), ALU.subtract))
    hi.passed(1)


def side_product(p, pe):
    for m in range(NT):
        ms = slice(m * P, m * P + P)
        mm = products(pe, p.ps[0][:, m * NE:m * NE + NE],
                      [((p.srcH[:, k, ms], p.srcL[:, k, ms]), (p.sideH[:, k, :], p.sideL[:, k, :]))
                       for k in range(KT)], True, True)
    return mm


def linear(p, src, n_tok, n_feat=0, out=None, out_feat=None, residual=None, gate=None, side=None,
           out_at=None, loads=(), beside=None):
    nc = p.nc
    ready, taken, src_ready = p.sig("chunk_ready"), p.sig("chunk_taken"), p.sig("src_ready")
    n, g0 = n_tok + n_feat, p.used
    total = n + (1 if side is not None else 0)
    out_at = out_at or [c * PC for c in range(n_tok)]

    def parts(t, k):
        return t[0][:, k, :], t[1][:, k, :]

    with nc.Block(no_gpsimd_drain=True) as block:
        @block.sync
        def _(sp):
            p.load_stream(sp)

        if beside is not None:
            @block.gpsimd
            def _(pool):
                beside(pool, taken)

        @block.scalar
        def _(act):
            if src is not None:
                split_src_hi(p, act, src)
            for q in range(2 * n):
                if q == 3:
                    start_loads(p, act, loads)
                g, b = g0 + q // 2, q % 3
                if q % 2 == 0:
                    p.wait_chunk(act, g)
                if q >= 3:
                    act.wait_ge(*p.w_used[b](q // 3))
                act.activation(p.wH[:, b, :], p.ring[:, g % RING, (q % 2) * PIECE:(q % 2 + 1) * PIECE],
                               ACT.Copy).then_inc(p.w_hi[b].sem, 1)
            end_loads(p, act, loads)

        @block.tensor
        def _(pe):
            for q in range(2 * n):
                c, h, b = q // 2, q % 2, q % 3
                if q < 2 and src is not None:
                    pe.wait_ge(*src_ready(q + 1))
                pe.wait_ge(*p.w_lo[b](q // 3 + 1))
                if h == 0 and c >= 4:
                    pe.wait_ge(*taken(c - 3))
                w = [v[:, b, :].rearrange("p (k n) -> p k n", k=4) for v in (p.wH, p.wL)]
                for m in range(2):
                    bank = p.ps[2 * (c % 4) + m][:, 0:PC]
                    ms = slice(m * P, m * P + P)
                    pairs = []
                    for k in range(4):
                        s = (p.srcH[:, 4 * h + k, :], p.srcL[:, 4 * h + k, :])
                        wk = (w[0][:, k, :], w[1][:, k, :])
                        if c < n_tok:
                            pairs.append(((s[0][:, ms], s[1][:, ms]), wk))
                        else:
                            pairs.append(((wk[0][:, ms], wk[1][:, ms]), s))
                    mm = products(pe, bank, pairs, h == 0, h == 1)
                mm.then_inc(p.w_used[b].sem, 1)
                if h:
                    pe.wait_ge(*p.w_used[b](q // 3 + 1))
                    pe.sem_inc(ready.sem, 1)
            if side is not None:
                pe.wait_ge(*taken(n))
                side_product(p, pe).then_inc(ready.sem, 1)

        @block.vector
        def _(dve):
            chain = Chain(dve, p.sig("dve_chain"))
            if src is not None:
                split_src_lo(p, dve, src)

            def split(q):
                g, b = g0 + q // 2, q % 3
                dve.wait_ge(*p.w_hi[b](q // 3 + 1))
                ins = dve.tensor_tensor(p.wL[:, b, :], p.ring[:, g % RING, (q % 2) * PIECE:(q % 2 + 1) * PIECE],
                                        p.wH[:, b, :].bitcast(F32), ALU.subtract)
                ins.then_inc(p.w_lo[b].sem, 1)
                if q % 2:
                    dve.wait_ge(*p.w_lo[b](q // 3 + 1))
                    dve.sem_inc(p.slot_free.sem, 1)

            for q in range(min(4, 2 * n)):
                split(q)
            for c in range(n):
                for q in (2 * c + 4, 2 * c + 5):
                    if q < 2 * n and q % 2 == 0:
                        split(q)
                dve.wait_ge(*ready(c + 1))
                for m in range(2):
                    bank = p.ps[2 * (c % 4) + m][:, 0:PC]
                    cut = slice(c * PC, c * PC + PC)
                    if c >= n_tok:
                        ins = dve.tensor_copy(out_feat[:, 2 * (c - n_tok) + m, :], bank)
                    elif residual is None:
                        w = min(PC, out.shape[2] - out_at[c])
                        ins = dve.tensor_copy(out[:, m, out_at[c]:out_at[c] + w], bank[:, 0:w])
                    elif gate is None:
                        ins = dve.tensor_tensor(residual[:, m, cut], residual[:, m, cut], bank, ALU.add)
                    else:
                        y = p.work[:, m * PC:m * PC + PC]
                        chain(dve.tensor_tensor(y, bank, gate[:, cut], ALU.mult))
                        ins = dve.tensor_tensor(residual[:, m, cut], residual[:, m, cut], y, ALU.add)
                ins.then_inc(taken.sem, 1)
                if 2 * c + 5 < 2 * n:
                    split(2 * c + 5)
            if side is not None:
                dve.wait_ge(*ready(n + 1))
                dve.tensor_copy(side, p.ps[0][:, 0:NT * NE].rearrange("p (m n) -> p m n", m=NT)).then_inc(taken.sem, 1)
    ready.passed(total)
    taken.passed(total)
    if src is not None:
        src_ready.passed(2)
        p.sig("src_hi_ready").passed(2)
    for b in range(3):
        k = len(range(b, 2 * n, 3))
        for s in (p.w_hi[b], p.w_lo[b], p.w_used[b]):
            s.passed(k)
    p.slot_free.passed(n)
    p.end_stream()


def ffn(p, residual, gate=None, loads=()):
    nc = p.nc
    n, g0 = FC, p.used
    GATE, UP, DOWN = 0, 1, 2
    exp_ready, half_ready, act_hi, act_ready = (p.sig("ffn_exp_ready"), p.sig("ffn_half_ready"),
                                                p.sig("ffn_act_hi"), p.sig("ffn_act_ready"))
    a_ready, step_done = p.sig("ffn_a_ready"), p.sig("ffn_dve_step")
    ex = p.work[:, 0:512].rearrange("p (b t) -> p b t", b=2)
    rc = p.work[:, 512:1024].rearrange("p (b t) -> p b t", b=2)
    aT = p.work[:, 1024:1536].rearrange("p (b t) -> p b t", b=2)
    turns = (n - 2) // RING
    assert 2 + turns * RING == n

    def loop(eng, step):
        step(0, 0)
        step(1, 0)
        with eng.Fori(0, turns) as i:
            for r in range(RING):
                step(2 + r, i)
        step(n, 0)

    def at(signal, turn, k):
        return signal.sem, turn * RING + (signal.base + k)

    def piece(c, kind):
        return p.ring[:, (g0 + c) % RING, kind * PIECE:(kind + 1) * PIECE]

    with nc.Block(no_gpsimd_drain=True) as block:
        @block.sync
        def _(sp):
            p.load_stream(sp)

        @block.scalar
        def _(act):
            def hi(c, turn, kind):
                act.wait_ge(*at(p.w_used[kind], turn, c))
                act.activation(p.wH[:, kind, :], piece(c, kind), ACT.Copy).then_inc(p.w_hi[kind].sem, 1)

            def step(c, turn):
                if c < n:
                    p.wait_chunk(act, g0 + c, turn)
                    hi(c, turn, GATE)
                if c:
                    act.wait_ge(*at(p.w_used[GATE], turn, c))
                    if c >= 3:
                        act.wait_ge(*at(half_ready, turn, c - 2))
                    act.activation(ex[:, (c - 1) % 2, :], p.ps[4 + (c - 1) % 2][:, 0:T], ACT.Exp,
                                   scale=-1.0).then_inc(exp_ready.sem, 1)
                if c < n:
                    hi(c, turn, UP)
                if c:
                    hi(c - 1, turn, DOWN)
                    act.wait_ge(*at(a_ready, turn, c))
                    act.activation(p.actH[:, :], aT[:, (c - 1) % 2, :], ACT.Copy).then_inc(act_hi.sem, 1)
            start_loads(p, act, loads)
            loop(act, step)
            end_loads(p, act, loads)

        @block.tensor
        def _(pe):
            def step(c, turn):
                if c < n:
                    if c >= 2:
                        pe.wait_ge(*at(a_ready, turn, c - 1))
                    for kind in (GATE, UP):
                        w = [v[:, kind, :].rearrange("p (k f) -> p k f", k=KT) for v in (p.wH, p.wL)]
                        pe.wait_ge(*at(p.w_lo[kind], turn, c + 1))
                        out = p.ps[4 + 2 * kind + c % 2][:, 0:T]
                        for h in range(2):
                            mm = products(pe, out, [((w[0][:, k, :], w[1][:, k, :]), (p.srcH[:, k, :], p.srcL[:, k, :]))
                                                    for k in range(4 * h, 4 * h + 4)], h == 0, h == 1)
                        mm.then_inc(p.w_used[kind].sem, 1)
                if c:
                    pe.wait_ge(*at(act_ready, turn, c))
                    pe.wait_ge(*at(p.w_lo[DOWN], turn, c))
                    for b in range(4):
                        t, hf = slice((b // 2) * P, (b // 2) * P + P), slice((b % 2) * 512, (b % 2) * 512 + 512)
                        mm = products(pe, p.ps[b][:, :], [((p.actH[:, t], p.actL[:, t]),
                                                           (p.wH[:, DOWN, hf], p.wL[:, DOWN, hf]))],
                                      c == 1, c == n)
                    mm.then_inc(p.w_used[DOWN].sem, 1)
            loop(pe, step)

        @block.vector
        def _(dve):
            def lo(c, turn, kind):
                dve.wait_ge(*at(p.w_hi[kind], turn, c + 1))
                dve.tensor_tensor(p.wL[:, kind, :], piece(c, kind), p.wH[:, kind, :].bitcast(F32),
                                  ALU.subtract).then_inc(p.w_lo[kind].sem, 1)

            def step(c, turn):
                a = (c - 1) % 2
                e, r = ex[:, a, :], rc[:, a, :]
                if c < n:
                    lo(c, turn, GATE)
                if c:
                    dve.wait_ge(*at(exp_ready, turn, c))
                    dve.tensor_scalar(e, e, 1.0, None, ALU.add).then_inc(step_done.sem, 1)
                    dve.wait_ge(step_done.sem, turn * (2 * RING) + (step_done.base + 2 * c - 1))
                    dve.reciprocal(r, e).then_inc(step_done.sem, 1)
                    dve.wait_ge(step_done.sem, turn * (2 * RING) + (step_done.base + 2 * c))
                    dve.tensor_tensor(r, r, p.ps[4 + a][:, 0:T], ALU.mult).then_inc(half_ready.sem, 1)
                if c < n:
                    lo(c, turn, UP)
                if c:
                    dve.wait_ge(*at(p.w_used[UP], turn, c))
                    dve.wait_ge(*at(half_ready, turn, c))
                    dve.tensor_tensor(aT[:, a, :], r, p.ps[6 + a][:, 0:T], ALU.mult).then_inc(a_ready.sem, 1)
                    dve.wait_ge(*at(act_hi, turn, c))
                    dve.tensor_tensor(p.actL[:, :], aT[:, a, :], p.actH[:, :].bitcast(F32),
                                      ALU.subtract).then_inc(act_ready.sem, 1)
                    lo(c - 1, turn, DOWN)
                    dve.wait_ge(*at(p.w_lo[DOWN], turn, c))
                    dve.sem_inc(p.slot_free.sem, 1)
            loop(dve, step)
            chain = Chain(dve, p.sig("dve_chain"))
            dve.wait_ge(*p.w_used[DOWN](n))
            for b in range(4):
                r = residual[:, b // 2, (b % 2) * 512:(b % 2) * 512 + 512]
                if gate is None:
                    chain(dve.tensor_tensor(r, r, p.ps[b][:, :], ALU.add))
                else:
                    y = p.work[:, (b % 2) * 512:(b % 2) * 512 + 512]
                    chain(dve.tensor_tensor(y, p.ps[b][:, :], gate[:, (b % 2) * 512:(b % 2) * 512 + 512], ALU.mult))
                    chain(dve.tensor_tensor(r, r, y, ALU.add))
    step_done.passed(2 * n)
    for s, k in ((exp_ready, n), (half_ready, n), (act_hi, n), (act_ready, n), (a_ready, n)):
        s.passed(k)
    for b in range(3):
        for s in (p.w_hi[b], p.w_lo[b], p.w_used[b]):
            s.passed(n)
    p.slot_free.passed(n)
    p.end_stream()


def attention(p, items):
    n = len(items)
    scores, negmax, probs = p.sig("scores_ready"), p.sig("negmax_ready"), p.sig("probs_ready")
    masked, sunk = p.sig("probs_masked"), p.sig("sink_ready")
    pt_ready, pt_kept, pv, done = p.sig("pt_ready"), p.sig("pt_kept"), p.sig("pv_ready"), p.sig("attn_out")
    S = p.work[:, 0:1024].rearrange("p (b n) -> p b n", b=2)
    E = p.work[:, 1024:2048].rearrange("p (b n) -> p b n", b=2)
    PT = p.work[:, 2048:3072].rearrange("p (b n) -> p b n", b=2)
    has_valid = any(it.get("valid") is not None for it in items)

    def sinks(n):
        return sum(it.get("sink") is not None for it in items[:n])

    def nk(i):
        return items[i]["qk"][0][1].shape[1]

    def blocks(i):
        return [min(P, nk(i) - b) for b in range(0, nk(i), P)]

    with p.nc.Block(no_gpsimd_drain=True) as block:
        @block.tensor
        def _(pe):
            for i in range(n + 2):
                if i < n:
                    if i >= 2:
                        pe.wait_ge(*probs(i - 1))
                    qk = items[i]["qk"]
                    for j, (q, k) in enumerate(qk):
                        mm = pe.matmul(p.ps[i % 2][:, 0:nk(i)], q, k, start=j == 0, stop=j == len(qk) - 1)
                    mm.then_inc(scores.sem, 1)
                if 1 <= i <= n:
                    j = i - 1
                    pe.wait_ge(*(masked if has_valid else probs)(j + 1))
                    if j >= 2:
                        pe.wait_ge(*pt_kept(j - 1))
                    for b, w in enumerate(blocks(j)):
                        mm = pe.transpose(p.ps[2 + j % 2][0:w, b * P:b * P + P], E[:, j % 2, b * P:b * P + w],
                                          p.ident[:, :])
                    mm.then_inc(pt_ready.sem, 1)
                if i >= 2:
                    j = i - 2
                    pe.wait_ge(*pt_kept(j + 1))
                    if j >= 2:
                        pe.wait_ge(*done(j - 1))
                    bl, v = blocks(j), items[j]["v"]
                    for b, w in enumerate(bl):
                        mm = pe.matmul(p.ps[4 + j % 2][:, 0:v[b].shape[1]], PT[0:w, j % 2, b * P:b * P + P], v[b],
                                       start=b == 0, stop=b == len(bl) - 1)
                    mm.then_inc(pv.sem, 1)

        @block.vector
        def _(dve):
            chain = Chain(dve, p.sig("dve_chain"))
            for i in range(n + 2):
                if i < n:
                    it, st = items[i], p.stat[:, i % 4, :]
                    dve.wait_ge(*scores(i + 1))
                    s = p.ps[i % 2][:, 0:nk(i)]
                    if it.get("mask") is not None:
                        if i >= 2:
                            dve.wait_ge(*probs(i - 1))
                        chain(dve.tensor_tensor(S[:, i % 2, 0:nk(i)], s, it["mask"], ALU.add))
                        s = S[:, i % 2, 0:nk(i)]
                    chain(dve.tensor_reduce(st[:, 0:1], s, AX_X, ALU.max))
                    if it.get("sink") is not None:
                        chain(dve.tensor_scalar(st[:, 0:1], st[:, 0:1], it["scale"], it["sink"], ALU.mult, ALU.max))
                        dve.tensor_scalar(st[:, 1:2], st[:, 0:1], -1.0, None, ALU.mult).then_inc(negmax.sem, 1)
                    else:
                        dve.tensor_scalar(st[:, 1:2], st[:, 0:1], -it["scale"], None, ALU.mult).then_inc(negmax.sem, 1)
                    if has_valid:
                        dve.wait_ge(*probs(i + 1))
                        e = E[:, i % 2, 0:nk(i)]
                        dve.tensor_tensor(e, e, it["valid"], ALU.mult).then_inc(masked.sem, 1)
                if i >= 2:
                    it, st = items[i - 2], p.stat[:, (i - 2) % 4, :]
                    dve.wait_ge(*pv(i - 1))
                    if it.get("sink") is not None:
                        dve.wait_ge(*sunk(sinks(i - 1)))
                        chain(dve.tensor_tensor(st[:, 2:3], st[:, 2:3], st[:, 3:4], ALU.add))
                    chain(dve.reciprocal(st[:, 0:1], st[:, 2:3]))
                    dve.tensor_scalar(it["out"], p.ps[4 + i % 2][:, 0:it["out"].shape[1]], st[:, 0:1], None,
                                      ALU.mult).then_inc(done.sem, 1)

        @block.scalar
        def _(act):
            for i in range(n + 1):
                if i < n:
                    it, st = items[i], p.stat[:, i % 4, :]
                    act.wait_ge(*negmax(i + 1))
                    if it.get("sink") is not None:
                        act.activation(st[:, 3:4], it["sink"], ACT.Exp, bias=st[:, 1:2]).then_inc(sunk.sem, 1)
                    if i >= 2:
                        act.wait_ge(*pt_ready(i - 1))
                    s = p.ps[i % 2][:, 0:nk(i)] if it.get("mask") is None else S[:, i % 2, 0:nk(i)]
                    act.activation(E[:, i % 2, 0:nk(i)], s, ACT.Exp, bias=st[:, 1:2], scale=it["scale"],
                                   accum_out=st[:, 2:3]).then_inc(probs.sem, 1)
                if i >= 1:
                    j = i - 1
                    act.wait_ge(*pt_ready(j + 1))
                    if j >= 2:
                        act.wait_ge(*pv(j - 1))
                    w = blocks(j)
                    act.activation(PT[0:w[0], j % 2, 0:len(w) * P], p.ps[2 + j % 2][0:w[0], 0:len(w) * P],
                                   ACT.Copy).then_inc(pt_kept.sem, 1)
    for s in (scores, negmax, probs, pt_ready, pt_kept, pv, done):
        s.passed(n)
    if has_valid:
        masked.passed(n)
    sunk.passed(sinks(n))


def heads_to_T(src, first, count, dst, d=HD):
    groups = []
    for h in range(0, count, 2):
        hs = range(h, min(h + 2, count))
        groups.append(([src[:, t, first + a * d:first + a * d + d] for a in hs for t in range(NT)],
                       dst(h, len(hs))))
    return groups


def pool_chain(p, pool):
    return Chain(pool, p.sig("pool_chain"))


def x_heads1(p, proj, l):
    def beside(pool, taken):
        chain, junk = pool_chain(p, pool), p.work[:, 1024:3072]
        norm_rows(p, chain, pool, heads_of(proj, 0, 8), [(0, 6, p.row(ROWS1, "q_norm", l, HD)),
                                                         (6, 2, p.row(ROWS1, "k_norm", l, HD))], junk, True)
        for a in (0, 896):
            rope_rows(chain, pool, heads_of(proj, a, 8), p.con_at(CON1, "rope_c", NT), p.con_at(CON1, "rope_s", NT),
                      junk)
    return beside


def ctx_heads1(p, proj, l, queries):
    gains = [(0, 6, p.row(ROWS1, "q_norm", l, HD)), (6, 2, p.row(ROWS1, "k_norm", l, HD))]
    src = heads_of(proj, 0, 8) if queries else heads_of(proj, 6 * HD, 2)
    with p.nc.Block(no_gpsimd_drain=True) as block:
        @block.gpsimd
        def _(pool):
            rsqrts(p, pool, [16 if queries else 4])

        @block.vector
        def _(dve):
            norm_rows(p, Chain(dve, p.sig("dve_chain")), dve, src,
                      gains if queries else [(0, 2, gains[1][2])], p.work[:])


def fourier(p, proj):
    seq_done, seq_kept, out_done, out_kept = (p.sig("dft_seq"), p.sig("dft_seq_kept"), p.sig("dft_out"),
                                              p.sig("dft_out_kept"))
    dft = p.con_at(CON1, "dft_seq", NT)
    A = p.work[:, 0:1024].rearrange("p (c n) -> p c n", c=2)
    with p.nc.Block(no_gpsimd_drain=True) as block:
        @block.tensor
        def _(pe):
            for c in range(2):
                for t in range(NT):
                    mm = pe.matmul(p.ps[c][:, :], proj[:, t, 640 + c * P:640 + c * P + P], dft[:, t, :],
                                   start=t == 0, stop=t == NT - 1)
                mm.then_inc(seq_done.sem, 1)
            for c in range(2):
                pe.wait_ge(*seq_kept(c + 1))
                pe.matmul(p.ps[2 + c][:, 0:T], p.con_at(CON1, "dft_cos"), A[:, c, 0:T], start=True, stop=False)
                pe.matmul(p.ps[2 + c][:, 0:T], p.con_at(CON1, "dft_sin"), A[:, c, T:2 * T], start=False,
                          stop=True).then_inc(out_done.sem, 1)

        @block.vector
        def _(dve):
            for c in range(2):
                dve.wait_ge(*seq_done(c + 1))
                dve.tensor_copy(A[:, c, :], p.ps[c][:, :]).then_inc(seq_kept.sem, 1)
            for c in range(2):
                dve.wait_ge(*out_done(c + 1))
                dve.tensor_copy(p.oT[:, 3 + c, :], p.ps[2 + c][:, 0:T]).then_inc(out_kept.sem, 1)
    for s in (seq_done, seq_kept, out_done, out_kept):
        s.passed(2)


def o_groups(p, cuts):
    out = []
    for i in range(0, len(cuts), 2):
        two = cuts[i:i + 2]
        assert len(two) == 1 or two[1][0] == two[0][0] + 1
        out.append(([f(t) for _, f in two for t in range(NT)],
                    p.oT[:, two[0][0]:two[0][0] + len(two), :].rearrange("p k t -> p (k t)")))
    return out


def block1_attention(p, proj, l, x_tokens):
    kT = p.big[:, 0:8 * T].rearrange("p (h n) -> p h n", h=4)
    qT = p.big[:, 8 * T:20 * T].rearrange("p (h n) -> p h n", h=12)

    def q_dst(first):
        return lambda h, m: qT[0:HD, first + h:first + h + m, :].rearrange("p h t -> p (h t)")
    turn(p, heads_to_T(proj, 0, 6, q_dst(0)) + heads_to_T(proj, 896, 6, q_dst(6)))
    items = []
    for h in range(12):
        for t in range(NT):
            kv, window = h // 3, h >= 6
            v_at = 512 + 64 * kv if kv < 2 else 1408 + 64 * (kv - 2)
            q_at = h * HD if not window else 896 + (h - 6) * HD
            v = [p.projc[:, b, v_at:v_at + HD] for b in range(NT)]
            if x_tokens:
                v += [p.proj[:, b, v_at:v_at + HD] for b in range(NT)]
            it = dict(qk=[(qT[0:HD, h, t * P:t * P + P], kT[0:HD, kv, 0:len(v) * P])], v=v, scale=HD ** -0.5,
                      out=proj[:, t, q_at:q_at + HD])
            if window:
                it["sink"] = p.row(ROWS1, "sink")[:, l * 6 + h - 6:l * 6 + h - 5]
                if x_tokens:
                    it["mask"] = p.con_at(CON1, "window", NT)[:, t, :]
            items.append(it)
    attention(p, items[:12])
    attention(p, items[12:])


def block1_keys(p, proj, at):
    kT = p.big[:, 0:8 * T].rearrange("p (h n) -> p h n", h=4)
    groups = []
    for g, first in enumerate((384, 1280)):
        for h in range(2):
            groups.append(([proj[:, t, first + h * HD:first + h * HD + HD] for t in range(NT)],
                           kT[0:HD, 2 * g + h, at:at + T]))
    turn(p, groups)


def block1_mix_out(p, proj, residual, gate, loads=()):
    def cut(a):
        return lambda t: proj[:, t, a:a + P]
    turn(p, o_groups(p, [(0, cut(0)), (1, cut(P))]) + o_groups(p, [(2, cut(2 * P))])
         + o_groups(p, [(5, cut(896)), (6, cut(896 + P))]) + o_groups(p, [(7, cut(896 + 2 * P))]))
    linear(p, p.oT, 4, residual=residual, gate=gate, loads=loads)


def block1(p, first_loads, last_loads):
    x, ctx = p.x, p.ctx
    px = p.proj[:, :, 0:A_COLS]
    pc = p.projc[:]
    for l in range(2):
        adaln(p, l, first_loads if l == 0 else ())
        norm_src(p, x, p.scl[:, 0, 0, :], p.mod[:, 0:8, 0])
        linear(p, None, 6, out=px, loads=[gate_load(p, 0, 0), gate_load(p, 1, 0)])
        norm_src(p, ctx, p.scl[:, 0, 1, :], p.mod[:, 0:8, 1])
        if l == 0:
            linear(p, None, 6, out=pc, beside=x_heads1(p, px, l))
        else:
            linear(p, None, 3, out=pc, out_at=[256, 512, 1280], beside=x_heads1(p, px, l))
        ctx_heads1(p, pc, l, l == 0)
        block1_keys(p, pc, 0)
        block1_keys(p, px, T)
        block1_attention(p, px, l, True)
        fourier(p, px)
        block1_mix_out(p, px, x, p.gates[:, 0, :])
        norm_src(p, x, p.scl[:, 1, 0, :], p.mod[:, 16:24, 0])
        ffn(p, x, p.gates[:, 1, :], loads=[gate_load(p, 0, 1)] if l == 0 else last_loads)
        if l == 0:
            block1_attention(p, pc, l, False)
            fourier(p, pc)
            block1_mix_out(p, pc, ctx, p.gates[:, 0, :], loads=[gate_load(p, 1, 1)])
            norm_src(p, ctx, p.scl[:, 1, 1, :], p.mod[:, 16:24, 1])
            ffn(p, ctx, p.gates[:, 1, :])
    with p.nc.Block(no_gpsimd_drain=True) as block:
        @block.gpsimd
        def _(pool):
            rsqrts(p, pool, [NT])

        @block.vector
        def _(dve):
            norm_rows(p, Chain(dve, p.sig("dve_chain")), dve, x[:].unsqueeze(2),
                      [(0, 1, p.row(ROWS1, "g_final"))], p.work[:])


def silu_rest(chain, dve, v, s):
    chain(dve.tensor_scalar(s, s, 1.0, None, ALU.add))
    chain(dve.reciprocal(s, s))
    chain(dve.tensor_tensor(v, v, s, ALU.mult))


def silu_by_parts(p, jobs):
    e = p.sig("silu_exp")
    with p.nc.Block(no_gpsimd_drain=True) as block:
        @block.scalar
        def _(act):
            for v, s in jobs:
                act.activation(s, v, ACT.Exp, scale=-1.0).then_inc(e.sem, 1)

        @block.vector
        def _(dve):
            chain = Chain(dve, p.sig("dve_chain"))
            for i, (v, s) in enumerate(jobs):
                dve.wait_ge(*e(i + 1))
                silu_rest(chain, dve, v, s)
    e.passed(len(jobs))


def da_heads(p):
    def beside(pool, taken):
        chain, junk = pool_chain(p, pool), p.work[:, 1024:3072]
        for i, name in enumerate(("da_q", "da_k")):
            pool.wait_ge(*taken(2 * i + 2))
            v = heads_of(p.proj, 512 * i, 8)
            norm_rows(p, chain, pool, v, [(0, 8, p.row(ROWS2, name))], junk, True)
            rope_rows(chain, pool, v, p.con_at(CON2, "rope_c", NT), p.con_at(CON2, "rope_s", NT), junk)
    return beside


def diff_attention(p):
    proj = p.proj
    lam = p.small[:, 40:41]
    exp_ready = p.sig("lam_exp")
    dots_ready = p.sig("lam_dots")
    with p.nc.Block(no_gpsimd_drain=True) as block:
        @block.vector
        def _(dve):
            chain = Chain(dve, p.sig("dve_chain"))
            lr = p.row(ROWS2, "da_lam").rearrange("p (a b d) -> p a b d", a=2, b=2)
            prod = p.work[:, 0:128].rearrange("p (a d) -> p a d", a=2)
            chain(dve.tensor_tensor(prod, lr[:, :, 0, :], lr[:, :, 1, :], ALU.mult))
            dve.tensor_reduce(p.small[:, 36:38], prod, AX_X, ALU.add).then_inc(dots_ready.sem, 1)
            dve.wait_ge(*dots_ready(1))
            dve.wait_ge(*exp_ready(1))
            chain(dve.tensor_tensor(lam, p.small[:, 38:39], p.small[:, 39:40], ALU.subtract))
            chain(dve.tensor_scalar(lam, lam, LAM_INIT, None, ALU.add))

        @block.scalar
        def _(act):
            act.wait_ge(*dots_ready(1))
            act.activation(p.small[:, 38:40], p.small[:, 36:38], ACT.Exp).then_inc(exp_ready.sem, 1)
    exp_ready.passed(1)
    dots_ready.passed(1)
    qT = p.big[:, 0:8 * T].rearrange("p (h n) -> p h n", h=8)
    kT = p.big[:, 12 * T:20 * T].rearrange("p (h n) -> p h n", h=8)

    def to(dst):
        return lambda h, m: dst[0:HD, h:h + m, :].rearrange("p h t -> p (h t)")
    turn(p, heads_to_T(proj, 0, 8, to(qT)) + heads_to_T(proj, 512, 8, to(kT)))
    items = []
    for h in range(4):
        for c in range(2):
            for t in range(NT):
                n = (t + 1) * P
                items.append(dict(qk=[(qT[0:HD, 2 * h + c, t * P:t * P + P], kT[0:HD, 2 * h + c, 0:n])],
                                  v=[proj[:, b, 1024 + h * P:1024 + h * P + P] for b in range(t + 1)],
                                  mask=p.con_at(CON2, "causal", NT)[:, t, 0:n], scale=HD ** -0.5,
                                  out=proj[:, t, (2 * h + c) * P:(2 * h + c) * P + P]))
    attention(p, items)
    with p.nc.Block(no_gpsimd_drain=True) as block:
        @block.gpsimd
        def _(pool):
            rsqrts(p, pool, [4 * NT])

        @block.vector
        def _(dve):
            chain = Chain(dve, p.sig("dve_chain"))
            w = p.work[:, 1024:2048].rearrange("p (t c) -> p t c", t=NT)
            for t in range(NT):
                o = proj[:, t, 0:1024].rearrange("p (h c d) -> p h c d", h=4, c=2)
                wt = w[:, t, :].rearrange("p (h d) -> p h d", h=4)
                chain(dve.tensor_scalar(wt, o[:, :, 1, :], lam, None, ALU.mult))
                chain(dve.tensor_tensor(wt, o[:, :, 0, :], wt, ALU.subtract))
            norm_rows(p, chain, dve, heads_of(w, 0, 4, P), [(0, 4, p.row(ROWS2, "subln"))], p.work[:])
            chain(dve.tensor_scalar(proj[:, :, 0:512], w, 1.0 - LAM_INIT, None, ALU.mult))


def mamba(p):
    nc = p.nc
    raw = p.projc[:].rearrange("p t c -> p (t c)")[:, 0:KT * T].rearrange("p (k t) -> p k t", k=KT)
    cv = p.oT
    xs = p.projc[:].rearrange("p t c -> p (t c)")[:, 2048:3072].rearrange("p (t c) -> p t c", t=NT)
    dt = p.small[:, 48:64].rearrange("p (t h) -> p t h", t=NT)
    tiny = [p.small[:, 64 + 16 * i:80 + 16 * i].rearrange("p (t h) -> p t h", t=NT) for i in range(8)]
    ad, ncs, u, z, z2, acc, neg_a, ex = tiny
    conv_w = p.col("conv_w", 0, 32).rearrange("p (k j) -> p k j", j=4)
    dt_u, dt_e = p.sig("dt_abs"), p.sig("dt_exp")

    def convolve(eng, chain, tiles, on_pool=False):
        for k in tiles:
            a, b = raw[:, k, :], cv[:, k, :]
            chain(eng.tensor_scalar(b, a, conv_w[:, k, 3:4], p.col("conv_b")[:, k:k + 1], ALU.mult, ALU.add))
            for j in range(1, 4):
                tap = conv_w[:, k, 3 - j:4 - j]
                if on_pool:
                    y = p.work[:, 0:T - j]
                    chain(eng.tensor_scalar(y, a[:, 0:T - j], tap, None, ALU.mult))
                    chain(eng.tensor_tensor(b[:, j:T], b[:, j:T], y, ALU.add))
                else:
                    chain(eng.scalar_tensor_tensor(out=b[:, j:T], in0=a[:, 0:T - j], scalar=tap, in1=b[:, j:T],
                                                   op0=ALU.mult, op1=ALU.add))

    with nc.Block(no_gpsimd_drain=True) as block:
        @block.vector
        def _(dve):
            chain = Chain(dve, p.sig("dve_chain"))
            bias = p.row(ROWS2, "dt_bias").unsqueeze(1).broadcast_to([P, NT, 8])
            chain(dve.tensor_tensor(dt, p.proj[:, :, 2048:2056], bias, ALU.add))
            chain(dve.tensor_scalar(u, dt, -1.0, None, ALU.mult))
            dve.tensor_tensor(u, u, dt, ALU.min).then_inc(dt_u.sem, 1)
            convolve(dve, chain, range(6))
            dve.wait_ge(*dt_e(2))
            chain(dve.tensor_scalar(z, ex, 2.0, None, ALU.add))
            chain(dve.reciprocal(z, z))
            chain(dve.tensor_tensor(z, z, ex, ALU.mult))
            chain(dve.tensor_tensor(z2, z, z, ALU.mult))
            chain(dve.tensor_scalar(acc, z2, 2.0 / 17, 2.0 / 15, ALU.mult, ALU.add))
            for m in (13, 11, 9, 7, 5, 3, 1):
                chain(dve.tensor_tensor(acc, acc, z2, ALU.mult))
                chain(dve.tensor_scalar(acc, acc, 2.0 / m, None, ALU.add))
            chain(dve.tensor_tensor(acc, acc, z, ALU.mult))
            chain(dve.tensor_scalar(dt, dt, 0.0, None, ALU.max))
            chain(dve.tensor_tensor(dt, dt, acc, ALU.add))
            chain(dve.tensor_tensor(ad, dt, neg_a[:, 0:1, :].broadcast_to([P, NT, 8]), ALU.mult))
            chain(dve.tensor_scalar(ad, ad, -1.0, None, ALU.mult))

        @block.gpsimd
        def _(pool):
            convolve(pool, pool_chain(p, pool), range(6, KT), True)

        @block.scalar
        def _(act):
            act.wait_ge(*dt_u(1))
            act.activation(ex, u, ACT.Exp).then_inc(dt_e.sem, 1)
            act.activation(neg_a[:, 0, :], p.row(ROWS2, "a_log"), ACT.Exp).then_inc(dt_e.sem, 1)
    dt_u.passed(1)
    dt_e.passed(2)
    silu_by_parts(p, [tuple(v[:, 2 * k:2 * k + 2, :].rearrange("p k t -> p (k t)") for v in (cv, raw))
                      for k in range(4)])
    turn(p, [([cv[:, k, t * P:t * P + P] for k in range(4)], xs[:, t, :]) for t in range(NT)])

    xdt = p.big[:, 0:1024].rearrange("p (t c) -> p t c", t=NT)
    y = p.big[:, 1024:2048].rearrange("p (t c) -> p t c", t=NT)
    adw = p.big[:, 2048:2048 + 2048].rearrange("p (t h m) -> p t h m", t=NT, h=8)
    dec = p.work[:, 0:512].rearrange("p (b n) -> p b n", b=2)
    MT = p.work[:, 1024:2048].rearrange("p (b s n) -> p b s n", b=2, s=2)
    z_sc, z_exp = p.work[:, 2048:3072].rearrange("p (t c) -> p t c", t=NT), p.sig("silu_exp")
    tri = p.con_at(CON2, "tri", NT)
    mask = p.con_at(CON2, "tri_mask", NT)
    wide, sums, ncs_ready = p.sig("ad_wide"), p.sig("ssm_sums"), p.sig("ncs_ready")
    shifted, decayed, mt_ready, y_ready = (p.sig("decay_in"), p.sig("decay_out"), p.sig("mt_ready"), p.sig("ssm_y"))
    with nc.Block(no_gpsimd_drain=True) as block:
        @block.vector
        def _(dve):
            chain = Chain(dve, p.sig("dve_chain"))
            for t in range(NT):
                dve.tensor_copy(adw[:, t, :, :], ad[:, t, :].unsqueeze(2).broadcast_to([P, 8, P])).then_inc(wide.sem, 1)
            chain(dve.tensor_tensor(xdt[:].rearrange("p t (h d) -> p t h d", h=8),
                                    xs.rearrange("p t (h d) -> p t h d", h=8),
                                    dt.unsqueeze(3).broadcast_to([P, NT, 8, HD]), ALU.mult))
            for t in range(NT):
                dve.wait_ge(*z_exp(t + 1))
                silu_rest(chain, dve, p.proj[:, t, 1536:2048], z_sc[:, t, :])
            dve.wait_ge(*sums(3))
            dve.tensor_scalar(ncs, p.ps[4][:, 0:16].rearrange("p (t h) -> p t h", t=NT), -1.0, None,
                              ALU.mult).then_inc(ncs_ready.sem, 1)

            def shift(i):
                h, s = i // 2, i % 2
                if i >= 2:
                    dve.wait_ge(*decayed(i - 1))
                dve.tensor_tensor(dec[:, s, :], p.ps[h // 2][:, (h % 2) * T:(h % 2) * T + T], mask[:, s, :],
                                  ALU.add).then_inc(shifted.sem, 1)
            shift(0)
            for i in range(16):
                if i + 1 < 16:
                    shift(i + 1)
                h, s = i // 2, i % 2
                dve.wait_ge(*decayed(i + 1))
                if h >= 2:
                    dve.wait_ge(*y_ready(h - 1))
                q = (h // 4) * 2 + s
                m = MT[:, h % 2, s, :]
                dve.tensor_tensor(m, m, p.ps[5 + q // 2][:, (q % 2) * T:(q % 2) * T + T],
                                  ALU.mult).then_inc(mt_ready.sem, 1)
            dve.wait_ge(*y_ready(8))
            for t in range(NT):
                h8 = [P, 8, HD]
                w = p.big[:, 4096:4608].rearrange("p (h d) -> p h d", h=8)
                chain(dve.tensor_tensor(w, xs[:, t, :].rearrange("p (h d) -> p h d", h=8),
                                        p.row(ROWS2, "ssm_d").unsqueeze(2).broadcast_to(h8), ALU.mult))
                chain(dve.tensor_tensor(y[:, t, :], p.big[:, 4096:4608], p.ps[7 if t == 0 else 4][:, :], ALU.add))

        @block.tensor
        def _(pe):
            pe.wait_ge(*wide(NT))
            for h in range(8):
                for t in range(NT):
                    mm = pe.matmul(p.ps[h // 2][:, (h % 2) * T:(h % 2) * T + T], adw[:, t, h, :], tri[:, t, :],
                                   start=t == 0, stop=t == NT - 1)
            mm.then_inc(sums.sem, 1)
            for q in range(4):
                g, s = q // 2, q % 2
                mm = pe.matmul(p.ps[5 + q // 2][:, (q % 2) * T:(q % 2) * T + T], cv[:, 4 + g, s * P:s * P + P],
                               cv[:, 6 + g, :], start=True, stop=True)
            mm.then_inc(sums.sem, 1)
            for lt in range(NT):
                for t in range(NT):
                    mm = pe.matmul(p.ps[4][:, lt * 8:lt * 8 + 8], tri[:, t, lt * P:lt * P + P], ad[:, t, :],
                                   start=t == 0, stop=t == NT - 1)
            mm.then_inc(sums.sem, 1)
            pe.wait_ge(*ncs_ready(1))
            for h in range(8):
                pe.wait_ge(*mt_ready(2 * h + 2))
                for lt in range(NT):
                    for s in range(NT):
                        mm = pe.matmul(p.ps[7 if lt == 0 else 4][:, h * HD:h * HD + HD],
                                       MT[:, h % 2, s, lt * P:lt * P + P], xdt[:, s, h * HD:h * HD + HD],
                                       start=s == 0, stop=s == NT - 1)
                mm.then_inc(y_ready.sem, 1)

        @block.scalar
        def _(act):
            for t in range(NT):
                act.activation(z_sc[:, t, :], p.proj[:, t, 1536:2048], ACT.Exp, scale=-1.0).then_inc(z_exp.sem, 1)
            act.wait_ge(*ncs_ready(1))
            for i in range(16):
                h, s = i // 2, i % 2
                act.wait_ge(*shifted(i + 1))
                if h >= 2:
                    act.wait_ge(*y_ready(h - 1))
                act.activation(MT[:, h % 2, s, :], dec[:, s, :], ACT.Exp,
                               bias=ncs[:, s, h:h + 1]).then_inc(decayed.sem, 1)
    for s, k in ((wide, NT), (sums, 3), (ncs_ready, 1), (shifted, 16), (decayed, 16), (mt_ready, 16), (y_ready, 8),
                 (z_exp, NT)):
        s.passed(k)
    with nc.Block(no_gpsimd_drain=True) as block:
        @block.gpsimd
        def _(pool):
            rsqrts(p, pool, [2 * NT])

        @block.vector
        def _(dve):
            chain = Chain(dve, p.sig("dve_chain"))
            chain(dve.tensor_tensor(y, y, p.proj[:, :, 1536:2048], ALU.mult))
            norm_rows(p, chain, dve, heads_of(y, 0, 2, 256), [], p.work[:])
            chain(dve.tensor_tensor(y, y, p.gates[:, 0:1, 0:512].broadcast_to([P, NT, 512]), ALU.mult))
    return y


def even_layer(p, loads):
    norm_src(p, p.x, p.col("ev_mix"), loads=loads)
    split_side(p)
    raw = p.projc[:].rearrange("p t c -> p (t c)")[:, 0:KT * T].rearrange("p (k t) -> p k t", k=KT)
    linear(p, None, 8, 4, out=p.proj[:, :, 0:2048], out_feat=raw, side=p.proj[:, :, 2048:2056],
           beside=da_heads(p))
    diff_attention(p)
    y = mamba(p)
    turn(p, o_groups(p, [(k, (lambda k: lambda t: p.proj[:, t, k * P:k * P + P])(k)) for k in range(4)])
         + o_groups(p, [(4 + k, (lambda k: lambda t: y[:, t, k * P:k * P + P])(k)) for k in range(4)]))
    linear(p, p.oT, 4, residual=p.x)
    norm_src(p, p.x, p.col("ev_ffn"))
    ffn(p, p.x)


def nsa_compress(p, w1, w2):
    nc = p.nc
    kcT = p.big[0:HD, 2048:2048 + 4 * T].rearrange("p (k n) -> p k n", k=4)
    turn(p, heads_to_T(p.proj, 512, 4, lambda h, m: kcT[:, h:h + m, :].rearrange("p h t -> p (h t)")))
    flat = p.work[0:HD, 0:32 * 2 * N_CMP].rearrange("p (i g n) -> p i g n", i=32, g=2)
    posed, hid, act_exp, act_done = p.sig("cmp_posed"), p.sig("cmp_hidden"), p.sig("cmp_exp"), p.sig("cmp_act")
    out_ready, kept = p.sig("cmp_out"), p.sig("cmp_kept")
    hsb = p.work[0:HD, 1024:1024 + 3 * 2 * N_CMP].rearrange("p (a n) -> p a n", a=3)
    ckv = p.work[0:N_CMP, 1280:1280 + 4 * HD].rearrange("p (k g d) -> p k g d", k=2, g=2)
    ck_keep = p.big[0:N_CMP, 5120:5120 + 4 * HD].rearrange("p (k g d) -> p k g d", k=2, g=2)
    with nc.Block(no_gpsimd_drain=True) as block:
        @block.gpsimd
        def _(pool):
            rsqrts(p, pool, [2], parts=N_CMP)

        @block.vector
        def _(dve):
            chain = Chain(dve, p.sig("dve_chain"))
            for kind in range(2):
                pos = p.col("cmp_pos", kind, 32)[0:HD, :]
                if kind:
                    dve.wait_ge(*hid(1))
                for g in range(2):
                    for half in range(2):
                        src = kcT[:, 2 * kind + g, 16 * half:16 * half + 16 * N_CMP]\
                            .rearrange("p (n i) -> p i n", i=16)
                        dve.tensor_tensor(flat[:, 16 * half:16 * half + 16, g, :], src,
                                          pos[:, 16 * half:16 * half + 16].unsqueeze(2)
                                          .broadcast_to([HD, 16, N_CMP]), ALU.add).then_inc(posed.sem, 1)
                dve.wait_ge(*act_exp(kind + 1))
                chain(dve.tensor_scalar(hsb[:, 0, :], hsb[:, 0, :], 1.0, None, ALU.add))
                chain(dve.reciprocal(hsb[:, 1, :], hsb[:, 0, :]))
                dve.tensor_tensor(hsb[:, 2, :], hsb[:, 1, :], p.ps[0][0:HD, 0:2 * N_CMP],
                                  ALU.mult).then_inc(act_done.sem, 1)
                dve.wait_ge(*out_ready(kind + 1))
                chain(dve.tensor_copy(ck_keep[:, kind, :, :],
                                      p.ps[1][0:N_CMP, 0:2 * HD].rearrange("p (g d) -> p g d", g=2)))
                dve.sem_inc(kept.sem, 1)
            keys = ck_keep[:, 0, :, :]
            head_norm(p, chain, dve, keys, p.row(ROWS2, "nsa_k", 0, HD)[0:N_CMP, :], p.work[0:N_CMP, :],
                      p.small[0:N_CMP, :])
            rope(chain, dve, keys, p.con_at(CON2, "cmp_c")[0:N_CMP, :], p.con_at(CON2, "cmp_s")[0:N_CMP, :],
                 p.work[0:N_CMP, :])

        @block.tensor
        def _(pe):
            for kind in range(2):
                pe.wait_ge(*posed(4 * kind + 4))
                for i in range(32):
                    mm = pe.matmul(p.ps[0][0:HD, 0:2 * N_CMP], w1[kind][:, i, :],
                                   flat[:, i, :, :].rearrange("p g n -> p (g n)"), start=i == 0, stop=i == 31)
                mm.then_inc(hid.sem, 1)
                pe.wait_ge(*act_done(kind + 1))
                if kind:
                    pe.wait_ge(*kept(1))
                for g in range(2):
                    mm = pe.matmul(p.ps[1][0:N_CMP, g * HD:g * HD + HD], hsb[:, 2, g * N_CMP:g * N_CMP + N_CMP],
                                   w2[:, kind, :], start=True, stop=True)
                mm.then_inc(out_ready.sem, 1)

        @block.scalar
        def _(act):
            for kind in range(2):
                act.wait_ge(*hid(kind + 1))
                act.activation(hsb[:, 0, :], p.ps[0][0:HD, 0:2 * N_CMP], ACT.Exp, scale=-1.0).then_inc(act_exp.sem, 1)
    for s, k in ((posed, 8), (hid, 2), (act_exp, 2), (act_done, 2), (out_ready, 2), (kept, 2)):
        s.passed(k)
    ckT = p.big[0:HD, 5376:5376 + 256]
    turn(p, [([ck_keep[:, 0, g, :]], ckT[:, g * P:g * P + N_CMP]) for g in range(2)])
    return ck_keep, ckT


def nsa_heads(p):
    def beside(pool, taken):
        chain, junk = pool_chain(p, pool), p.work[:, 1024:3072]
        for a, n, gain, chunks in ((0, 8, p.row(ROWS2, "nsa_q"), 2), (768, 2, p.row(ROWS2, "nsa_k", 1, HD), 4),
                                   (1024, 2, p.row(ROWS2, "nsa_k", 2, HD), 5)):
            pool.wait_ge(*taken(chunks))
            v = heads_of(p.proj, a, n)
            norm_rows(p, chain, pool, v, [(0, n, gain)], junk, True)
            rope_rows(chain, pool, v, p.con_at(CON2, "rope_c", NT), p.con_at(CON2, "rope_s", NT), junk)
    return beside


def nsa(p, w1, w2):
    proj = p.proj
    ck, ckT = nsa_compress(p, w1, w2)
    qT = p.big[:, 0:8 * T].rearrange("p (h n) -> p h n", h=8)
    kT = p.big[:, 3072:3072 + 4 * T].rearrange("p (h n) -> p h n", h=4)

    def to(dst, first):
        return lambda h, m: dst[0:HD, first + h:first + h + m, :].rearrange("p h t -> p (h t)")
    turn(p, heads_to_T(proj, 0, 8, to(qT, 0)) + heads_to_T(proj, 768, 2, to(kT, 0))
         + heads_to_T(proj, 1024, 2, to(kT, 2)))
    ow = p.projc[:].rearrange("p t c -> p (t c)")[:, 0:2048].rearrange("p (w t c) -> p w t c", w=2, t=NT)
    items = []
    for h in range(8):
        for t in range(NT):
            g = h // 4
            items.append(dict(qk=[(qT[0:HD, h, t * P:t * P + P], ckT[:, g * P:g * P + N_CMP])],
                              v=[ck[:, 1, g, :]], mask=p.con_at(CON2, "cmp_mask", NT)[:, t, :],
                              valid=p.con_at(CON2, "cmp_valid", NT)[:, t, :], scale=HD ** -0.5,
                              out=proj[:, t, h * HD:h * HD + HD]))
    attention(p, items)
    items = []
    for w in range(2):
        for h in range(8):
            for t in range(NT):
                g, n = h // 4, (t + 1) * P
                a = 896 + 256 * w + g * HD
                items.append(dict(qk=[(qT[0:HD, h, t * P:t * P + P], kT[0:HD, 2 * w + g, 0:n])],
                                  v=[proj[:, b, a:a + HD] for b in range(t + 1)],
                                  mask=p.con_at(CON2, "causal", NT)[:, t, 0:n], scale=HD ** -0.5,
                                  out=ow[:, w, t, h * HD:h * HD + HD]))
    attention(p, items)
    gate_exp = p.sig("nsa_gate_exp")
    gx = p.small[:, 0:48].rearrange("p (t g) -> p t g", t=NT)
    with p.nc.Block(no_gpsimd_drain=True) as block:
        @block.scalar
        def _(act):
            act.activation(gx, proj[:, :, 1280:1304], ACT.Exp, scale=-1.0).then_inc(gate_exp.sem, 1)

        @block.vector
        def _(dve):
            chain = Chain(dve, p.sig("dve_chain"))
            dve.wait_ge(*gate_exp(1))
            chain(dve.tensor_scalar(gx, gx, 1.0, None, ALU.add))
            chain(dve.reciprocal(gx, gx))
            for t in range(NT):
                g3 = gx[:, t, :].rearrange("p (h c) -> p h c", c=3)
                outs = [v.rearrange("p (h d) -> p h d", h=8) for v in (proj[:, t, 0:512], ow[:, 0, t, :], ow[:, 1, t, :])]
                for c in range(3):
                    chain(dve.tensor_tensor(outs[c], outs[c], g3[:, :, c:c + 1].broadcast_to([P, 8, HD]), ALU.mult))
                chain(dve.tensor_tensor(outs[0], outs[0], outs[1], ALU.add))
                chain(dve.tensor_tensor(outs[0], outs[0], outs[2], ALU.add))
    gate_exp.passed(1)


def mla(p, w_uq, w_ukv):
    nc = p.nc
    proj = p.proj
    q = p.gates[:].rearrange("p a d -> p (a d)")[:, 0:1536].rearrange("p (t c) -> p t c", t=NT)
    flat = p.projc[:].rearrange("p t c -> p (t c)")
    kv = flat[:, 0:2048].rearrange("p (t c) -> p t c", t=NT)
    o = flat[:, 2048:3072].rearrange("p (t c) -> p t c", t=NT)
    big = p.big
    cT = big[:, 5120:5888].rearrange("p (k t) -> p k t", k=3)
    with nc.Block(no_gpsimd_drain=True) as block:
        @block.gpsimd
        def _(pool):
            rsqrts(p, pool, [NT, NT, NT])

        @block.vector
        def _(dve):
            chain = Chain(dve, p.sig("dve_chain"))
            for a, n, name in ((1304, 256, "cq"), (1560, 128, "ckv"), (1688, 64, "kr")):
                norm_rows(p, chain, dve, heads_of(proj, a, 1, n), [(0, 1, p.row(ROWS2, name))], p.work[:])
            rope_rows(chain, dve, heads_of(proj, 1688, 1), p.con_at(CON2, "rope_c", NT), p.con_at(CON2, "rope_s", NT),
                      p.work[:])
    turn(p, [([proj[:, t, 1304 + k * P:1304 + k * P + P] for t in range(NT)], cT[:, k, :]) for k in range(3)])
    up, kept = p.sig("mla_up"), p.sig("mla_kept")
    jobs = []
    for t in range(NT):
        for c in range(2):
            jobs.append((q[:, t, c * 384:c * 384 + 384],
                         [(cT[:, k, t * P:t * P + P], w_uq[:, k, c * 384:c * 384 + 384]) for k in range(2)]))
            jobs.append((kv[:, t, c * 512:c * 512 + 512],
                         [(cT[:, 2, t * P:t * P + P], w_ukv[:, c * 512:c * 512 + 512])]))
    with nc.Block(no_gpsimd_drain=True) as block:
        @block.gpsimd
        def _(pool):
            rsqrts(p, pool, [4 * NT, 4 * NT, 4 * NT])

        @block.tensor
        def _(pe):
            for j, (dst, pairs) in enumerate(jobs):
                for i, (a, b) in enumerate(pairs):
                    mm = pe.matmul(p.ps[j][:, 0:dst.shape[1]], a, b, start=i == 0, stop=i == len(pairs) - 1)
                mm.then_inc(up.sem, 1)

        @block.vector
        def _(dve):
            chain = Chain(dve, p.sig("dve_chain"))
            for j, (dst, _) in enumerate(jobs):
                dve.wait_ge(*up(j + 1))
                chain(dve.tensor_copy(dst, p.ps[j][:, 0:dst.shape[1]]))
            qh, kh = heads_of(q, 0, 4, 192), heads_of(kv, 0, 4, 256)
            norm_rows(p, chain, dve, qh[:, :, :, 0:128], [(0, 4, p.row(ROWS2, "qn"))], p.work[:])
            norm_rows(p, chain, dve, qh[:, :, :, 128:192], [(0, 4, p.row(ROWS2, "qr"))], p.work[:])
            rope_rows(chain, dve, qh[:, :, :, 128:192], p.con_at(CON2, "rope_c", NT), p.con_at(CON2, "rope_s", NT),
                      p.work[:])
            norm_rows(p, chain, dve, kh[:, :, :, 0:128], [(0, 4, p.row(ROWS2, "kn"))], p.work[:])
    up.passed(len(jobs))
    qn = big[:, 0:4 * T].rearrange("p (h n) -> p h n", h=4)
    kn = big[:, 4 * T:8 * T].rearrange("p (h n) -> p h n", h=4)
    qr = big[:, 8 * T:12 * T].rearrange("p (h n) -> p h n", h=4)
    kr = big[:, 12 * T:13 * T]

    def tiles(src, a, w):
        return [src[:, t, a:a + w] for t in range(NT)]
    turn(p, [(tiles(q, h * 192, 128), qn[:, h, :]) for h in range(4)]
         + [(tiles(kv, h * 256, 128), kn[:, h, :]) for h in range(4)]
         + [(tiles(q, h * 192 + 128, 64), qr[0:HD, h, :]) for h in range(4)]
         + [(tiles(proj, 1688, 64), kr[0:HD, :])])
    items = []
    for h in range(4):
        for t in range(NT):
            n = (t + 1) * P
            items.append(dict(qk=[(qn[:, h, t * P:t * P + P], kn[:, h, 0:n]),
                                  (qr[0:HD, h, t * P:t * P + P], kr[0:HD, 0:n])],
                              v=[kv[:, b, h * 256 + 128:h * 256 + 256] for b in range(t + 1)],
                              mask=p.con_at(CON2, "causal", NT)[:, t, 0:n], scale=192 ** -0.5,
                              out=o[:, t, h * P:h * P + P]))
    attention(p, items)
    return o


def route(p):
    nc = p.nc
    slot, weight = p.slot, p.weight
    logits = p.small[:, 0:16].rearrange("p (t e) -> p t e", t=NT)
    top = p.small[:, 16:24]
    idx = p.small[:, 24:32]
    hot = p.small[:, 64:80].rearrange("p (t e) -> p t e", t=NT)
    iota = p.con_at(CON2, "iota")[:, 0:NE]
    tri = p.con_at(CON2, "tri", NT)
    logit, diff, ex, chosen, counted, routed = (p.sig("logits"), p.sig("top_diff"), p.sig("top_exp"),
                                                p.sig("tokens_chosen"), p.sig("tokens_counted"), p.sig("routed"))
    with nc.Block(no_gpsimd_drain=True) as block:
        @block.tensor
        def _(pe):
            side_product(p, pe).then_inc(logit.sem, 1)
            pe.wait_ge(*chosen(1))
            for lt in range(NT):
                for t in range(NT):
                    pe.matmul(p.ps[1][:, lt * NE:lt * NE + NE], tri[:, t, lt * P:lt * P + P], hot[:, t, :],
                              start=t == 0, stop=t == NT - 1)
            for t in range(NT):
                mm = pe.matmul(p.ps[1][:, 2 * NE:3 * NE], tri[:, 0, P:2 * P], hot[:, t, :], start=t == 0,
                               stop=t == NT - 1)
            mm.then_inc(counted.sem, 1)

        @block.scalar
        def _(act):
            for t in range(NT):
                act.wait_ge(*diff(t + 1))
                act.activation(p.small[:, 49:50], p.small[:, 48:49], ACT.Exp).then_inc(ex.sem, 1)

        @block.vector
        def _(dve):
            chain = Chain(dve, p.sig("dve_chain"))
            chain(dve.memset(slot[:], -1.0))
            chain(dve.memset(weight[:], 0.0))
            dve.wait_ge(*logit(1))
            chain(dve.tensor_copy(logits, p.ps[0][:, 0:16].rearrange("p (t e) -> p t e", t=NT)))
            for t in range(NT):
                chain(dve.max(top, logits[:, t, :]))
                chain(dve.max_index(p.idx[:, :], top, logits[:, t, :]))
                chain(dve.tensor_copy(idx, p.idx[:, :]))
                dve.tensor_tensor(p.small[:, 48:49], top[:, 1:2], top[:, 0:1], ALU.subtract).then_inc(diff.sem, 1)
                first, second = p.small[:, 52:60], p.small[:, 80:88]
                chain(dve.tensor_scalar(first, iota, idx[:, 0:1], None, ALU.is_equal))
                chain(dve.tensor_scalar(second, iota, idx[:, 1:2], None, ALU.is_equal))
                chain(dve.tensor_tensor(hot[:, t, :], first, second, ALU.add))
                dve.wait_ge(*ex(t + 1))
                chain(dve.tensor_scalar(p.small[:, 50:51], p.small[:, 49:50], 1.0, None, ALU.add))
                chain(dve.reciprocal(p.small[:, 50:51], p.small[:, 50:51]))
                chain(dve.tensor_tensor(p.small[:, 51:52], p.small[:, 50:51], p.small[:, 49:50], ALU.mult))
                chain(dve.tensor_scalar(first, first, p.small[:, 50:51], None, ALU.mult))
                chain(dve.tensor_scalar(second, second, p.small[:, 51:52], None, ALU.mult))
                for half in range(2):
                    chain(dve.tensor_tensor(weight[:, t, half * NE:half * NE + NE], first, second, ALU.add))
            dve.sem_inc(chosen.sem, 1)
            dve.wait_ge(*counted(1))
            cum = p.ps[1][:, 0:16].rearrange("p (t e) -> p t e", t=NT)
            chain(dve.tensor_tensor(slot[:, :, 0:NE], cum, hot[:], ALU.mult))
            chain(dve.tensor_scalar(slot[:, :, 0:NE], slot[:, :, 0:NE], -1.0, None, ALU.add))
            chain(dve.tensor_scalar(slot[:, :, NE:2 * NE], slot[:, :, 0:NE], -float(P), None, ALU.add))
            most = p.small[:, 49:50]
            chain(dve.tensor_reduce(most, p.ps[1][:, 2 * NE:3 * NE], AX_X, ALU.max))
            chain(dve.tensor_scalar(most, most, float(P), 4.0, ALU.is_gt, ALU.mult))
            chain(dve.tensor_scalar(most, most, 4.0, None, ALU.add))
            dve.tensor_copy(p.trip[:, :], most).then_inc(routed.sem, 1)
    for s, k in ((logit, 1), (diff, 2), (ex, 2), (chosen, 1), (counted, 1), (routed, 1)):
        s.passed(k)


def moe(p, gain):
    nc = p.nc
    g0 = p.used
    DOWN = 2
    xn = p.xn
    hJ = p.projc[:].rearrange("p t c -> p (t c)")[:, 0:2048].rearrange("p (b k s) -> p b k s", b=2, k=KT)
    big = p.big
    pick = big[:, 0:512].rearrange("p (b t s) -> p b t s", b=2, t=NT)
    pickw = big[:, 512:1024].rearrange("p (b t s) -> p b t s", b=2, t=NT)
    WT = big[:, 1024:1536].rearrange("p (b n) -> p b n", b=2)
    yS = big[:, 1536:2560]
    ex = p.work[:, 0:256].rearrange("p (b t) -> p b t", b=2)
    rc = p.work[:, 256:512].rearrange("p (b t) -> p b t", b=2)
    aJ = p.work[:, 512:768].rearrange("p (b t) -> p b t", b=2)
    gu_ready, exp_ready, act_ready = p.sig("gate_up_ready"), p.sig("ffn_exp_ready"), p.sig("ffn_act_ready")
    half_ready = p.sig("ffn_half_ready")
    dve_step = p.sig("ffn_dve_step")
    a_ready, act_hi = p.sig("ffn_a_ready"), p.sig("ffn_act_hi")
    picked, gathered, hJ_ready = p.sig("pick_ready"), p.sig("tokens_gathered"), p.sig("hJ_ready")
    wt_turned, wt_kept = p.sig("wt_turned"), p.sig("wt_kept")
    y_kept, scattered, added = p.sig("job_y_kept"), p.sig("scattered"), p.sig("y_added")
    pair_rounds = 2 * FC // RING
    inner = (FC - 2) // RING

    def at(signal, i, per_pair, turn, per_turn, n):
        return signal.sem, i * per_pair + turn * per_turn + (signal.base + n)

    def chunks(eng, b, step):
        step(0, b * FC)
        step(0, b * FC + 1)
        with eng.Fori(0, inner) as turn:
            for r in range(RING):
                step(turn, b * FC + 2 + r)
        step(0, b * FC + FC)

    def piece(k, kind):
        return p.ring[:, (g0 + k) % RING, kind * PIECE:(kind + 1) * PIECE]

    with nc.Block(no_gpsimd_drain=True) as block:
        @block.sync
        def _(sp):
            pairs = sp.value_load(p.trip[0:1, 0:1], min_val=4, max_val=8)
            with sp.Fori(1, pairs * pair_rounds) as rnd:
                for r in range(RING):
                    g = g0 + r
                    sp.wait_ge(p.slot_free.sem, rnd * RING + (g - RING + 1))
                    chunk = (rnd % (4 * pair_rounds)) * RING + r
                    sp.dma_start(p.ring[:, g % RING, :],
                                 p.ap["moe"][bass.ds(chunk, 1)].rearrange("o p f -> (o p) f")
                                 ).then_inc(p.slot_loaded[g % RING].sem, 16)

        @block.tensor
        def _(pe):
            pairs = pe.value_load(p.trip[0:1, 0:1], min_val=4, max_val=8)

            def gather(i, j, part):
                for k in range(4 * part, 4 * part + 4):
                    for t in range(NT):
                        mm = pe.matmul(p.ps[6 + part][:, (k % 4) * P:(k % 4) * P + P], xn[:, t, k * P:k * P + P],
                                       pick[:, j % 2, t, :], start=t == 0, stop=t == NT - 1)
                mm.then_inc(gathered.sem, 1)

            def turn_weights(i, j):
                pe.wait_ge(*at(picked, i, 2, 0, 0, j + 1))
                pe.wait_ge(*at(added, i, 8, 0, 0, 4 * j))
                for t in range(NT):
                    mm = pe.transpose(p.ps[4][:, t * P:t * P + P], pickw[:, j % 2, t, :], p.ident[:, :])
                mm.then_inc(wt_turned.sem, 1)

            def down(i, turn, k):
                pe.wait_ge(*at(act_ready, i, 2 * FC, turn, RING, k + 1))
                pe.wait_ge(*at(p.w_lo[DOWN], i, 2 * FC, turn, RING, k + 1))
                for hf in range(2):
                    cut = slice(hf * 512, hf * 512 + 512)
                    mm = products(pe, p.ps[hf][:, :], [((p.actH[:, 0:P], p.actL[:, 0:P]),
                                                        (p.wH[:, DOWN, cut], p.wL[:, DOWN, cut]))],
                                  k % FC == 0, k % FC == FC - 1)
                mm.then_inc(p.w_used[DOWN].sem, 1)

            def up(i, turn, k):
                pe.wait_ge(*at(a_ready, i, 2 * FC, turn, RING, k - 1))
                g = g0 + k
                pe.wait_ge(p.slot_loaded[g % RING].sem, i * (16 * pair_rounds) + turn * 16 + 16 * (g // RING + 1))
                for u in range(2):
                    w = piece(k, u).rearrange("p (k f) -> p k f", k=KT)
                    for kt in range(KT):
                        mm = pe.matmul(p.ps[2 + k % 2][:, u * P:u * P + P], w[:, kt, :], hJ[:, k // FC, kt, :],
                                       start=kt == 0, stop=kt == KT - 1)
                mm.then_inc(gu_ready.sem, 1)

            turn_weights(0, 0)
            gather(0, 0, 0)
            gather(0, 0, 1)
            with pe.Fori(0, pairs) as i:
                for b in range(2):
                    k0 = b * FC
                    pe.wait_ge(*at(hJ_ready, i, 2, 0, 0, b + 1))
                    up(i, 0, k0)
                    up(i, 0, k0 + 1)
                    down(i, 0, k0)
                    with pe.Fori(0, inner) as turn:
                        for r in range(RING):
                            up(i, turn, k0 + 2 + r)
                            down(i, turn, k0 + 1 + r)
                    turn_weights(i, b + 1)
                    gather(i, b + 1, 0)
                    down(i, 0, k0 + FC - 1)
                    gather(i, b + 1, 1)
                    pe.wait_ge(*at(y_kept, i, 2, 0, 0, b + 1))
                    pe.wait_ge(*at(wt_kept, i, 2, 0, 0, b + 2))
                    pe.wait_ge(*at(hJ_ready, i, 2, 0, 0, b + 2))
                    for q in range(4):
                        t, hf = q // 2, q % 2
                        pe.matmul(p.ps[4 + q][:, :], WT[:, b, t * P:t * P + P], yS[:, hf * 512:hf * 512 + 512],
                                  start=True, stop=True).then_inc(scattered.sem, 1)

        @block.scalar
        def _(act):
            pairs = act.value_load(p.trip[0:1, 0:1], min_val=4, max_val=8)

            def keep_weights(i, j):
                act.wait_ge(*at(wt_turned, i, 2, 0, 0, j + 1))
                act.activation(WT[:, j % 2, :], p.ps[4][:, 0:T], ACT.Copy).then_inc(wt_kept.sem, 1)

            keep_weights(0, 0)
            with act.Fori(0, pairs) as i:
                for b in range(2):
                    def step(turn, k):
                        def at_chunk(signal, n):
                            return at(signal, i, 2 * FC, turn, RING, n)

                        if k > b * FC:
                            act.wait_ge(*at_chunk(gu_ready, k))
                            act.wait_ge(*at_chunk(a_ready, k - 2))
                            act.activation(ex[:, (k - 1) % 2, :], p.ps[2 + (k - 1) % 2][:, 0:P], ACT.Exp,
                                           scale=-1.0).then_inc(exp_ready.sem, 1)
                            act.wait_ge(*at_chunk(p.w_used[DOWN], k - 1))
                            act.activation(p.wH[:, DOWN, :], piece(k - 1, DOWN), ACT.Copy).then_inc(p.w_hi[DOWN].sem, 1)
                            act.wait_ge(*at_chunk(a_ready, k))
                            act.activation(p.actH[:, 0:P], aJ[:, (k - 1) % 2, :], ACT.Copy).then_inc(act_hi.sem, 1)
                    chunks(act, b, step)
                    keep_weights(i, b + 1)
                    act.wait_ge(*at(p.w_used[DOWN], i, 2 * FC, 0, 0, (b + 1) * FC))
                    act.activation(yS[:, 0:512], p.ps[0][:, :], ACT.Copy)
                    act.activation(yS[:, 512:1024], p.ps[1][:, :], ACT.Copy).then_inc(y_kept.sem, 1)
        @block.vector
        def _(dve):
            pairs = dve.value_load(p.trip[0:1, 0:1], min_val=4, max_val=8)
            iota = p.con_at(CON2, "iota")
            dve.sem_inc(added.sem, 4)

            def make_pick(i, j):
                for t in range(NT):
                    job = slice(0, 1) if isinstance(i, int) else bass.ds(i * 2 + j, 1)
                    sl, wt = p.slot[:, t, job], p.weight[:, t, job]
                    dve.tensor_scalar(pick[:, j % 2, t, :], iota, sl, None, ALU.is_equal)
                    ins = dve.tensor_scalar(pickw[:, j % 2, t, :], iota, sl, wt, ALU.is_equal, ALU.mult)
                ins.then_inc(picked.sem, 1)

            def keep_gathered(i, j):
                for part in range(2):
                    dve.wait_ge(*at(gathered, i, 4, 0, 0, 2 * j + part + 1))
                    ins = dve.tensor_tensor(hJ[:, j % 2, 4 * part:4 * part + 4, :],
                                            p.ps[6 + part][:, :].rearrange("p (k s) -> p k s", k=4),
                                            gain[:, 4 * part:4 * part + 4].unsqueeze(2).broadcast_to([P, 4, P]),
                                            ALU.mult)
                ins.then_inc(hJ_ready.sem, 1)

            make_pick(0, 0)
            keep_gathered(0, 0)
            with dve.Fori(0, pairs) as i:
                for b in range(2):
                    make_pick(i, b + 1)

                    def step(turn, k):
                        def at_chunk(signal, n):
                            return at(signal, i, 2 * FC, turn, RING, n)

                        def done(n):
                            return at(dve_step, i, 4 * FC, turn, 2 * RING, 2 * (k - 1) + n)

                        if k > b * FC:
                            a = (k - 1) % 2
                            e, r, bank = ex[:, a, :], rc[:, a, :], p.ps[2 + a]
                            dve.wait_ge(*at_chunk(exp_ready, k))
                            dve.tensor_scalar(e, e, 1.0, None, ALU.add).then_inc(dve_step.sem, 1)
                            dve.wait_ge(*done(1))
                            dve.reciprocal(r, e).then_inc(dve_step.sem, 1)
                            dve.wait_ge(*done(2))
                            dve.tensor_tensor(r, r, bank[:, 0:P], ALU.mult).then_inc(half_ready.sem, 1)
                            dve.wait_ge(*at_chunk(half_ready, k))
                            dve.tensor_tensor(aJ[:, a, :], r, bank[:, P:2 * P], ALU.mult).then_inc(a_ready.sem, 1)
                            dve.wait_ge(*at_chunk(act_hi, k))
                            dve.wait_ge(*at_chunk(a_ready, k))
                            dve.tensor_tensor(p.actL[:, 0:P], aJ[:, a, :], p.actH[:, 0:P].bitcast(F32),
                                              ALU.subtract).then_inc(act_ready.sem, 1)
                            dve.wait_ge(*at_chunk(p.w_hi[DOWN], k))
                            dve.tensor_tensor(p.wL[:, DOWN, :], piece(k - 1, DOWN), p.wH[:, DOWN, :].bitcast(F32),
                                              ALU.subtract).then_inc(p.w_lo[DOWN].sem, 1)
                            dve.wait_ge(*at_chunk(p.w_lo[DOWN], k))
                            dve.sem_inc(p.slot_free.sem, 1)
                    chunks(dve, b, step)
                    keep_gathered(i, b + 1)
                    for q in range(4):
                        t, hf = q // 2, q % 2
                        x = p.x[:, t, hf * 512:hf * 512 + 512]
                        dve.wait_ge(*at(scattered, i, 8, 0, 0, 4 * b + q + 1))
                        dve.tensor_tensor(x, x, p.ps[4 + q][:, :], ALU.add).then_inc(added.sem, 1)
    p.end_stream()


def odd_layer(p):
    norm_src(p, p.x, p.col("od_mix"))
    w1 = [v.rearrange("p a d -> p (a d)")[0:HD, :].rearrange("p (i j) -> p i j", i=32) for v in (p.gates[:], p.ctx[:])]
    free = p.oT[:].rearrange("p k t -> p (k t)")
    w2 = free[0:HD, 1536:1664].rearrange("p (k j) -> p k j", k=2)
    w_uq = free[:, 0:1536].rearrange("p (k c) -> p k c", k=2)
    w_ukv = p.projc[:].rearrange("p t c -> p (t c)")[:, 2048:3072]
    linear(p, None, 7, out=p.proj[:, :, 0:O_COLS], beside=nsa_heads(p), loads=[
                   (w1[0], p.ap["cmp_w1"][:, 0]), (w1[1], p.ap["cmp_w1"][:, 1]), (w2, p.ap["cmp_w2"]),
                   (w_uq, p.ap["w_uq"]), (w_ukv, p.ap["w_ukv"]), (p.side[:], p.ap["router"])])
    split_side(p)
    nsa(p, w1, w2)
    o = mla(p, w_uq, w_ukv)
    turn(p, o_groups(p, [(k, (lambda k: lambda t: p.proj[:, t, k * P:k * P + P])(k)) for k in range(4)])
         + o_groups(p, [(4 + k, (lambda k: lambda t: o[:, t, k * P:k * P + P])(k)) for k in range(4)]))
    linear(p, p.oT, 4, residual=p.x)
    norm_src(p, p.x, p.col("od_ffn"))
    route(p)
    moe(p, p.col("od_ffn"))


def build(nc, ap, dbg=None, upto=None):
    p = Program(nc, ap)
    dense = SLOT
    p.streams = [
        Stream("w_ada0", 24, KT * PC), Stream("w_in0", 6, KT * PC), Stream("w_in0", 6, KT * PC),
        Stream("w_out0", 4, KT * PC), Stream("ffn0", FC, dense),
        Stream("w_out0", 4, KT * PC), Stream("ffn0", FC, dense),
        Stream("w_ada1", 24, KT * PC), Stream("w_in1", 6, KT * PC), Stream("w_in1_kv", 3, KT * PC),
        Stream("w_out1", 4, KT * PC), Stream("ffn1", FC, dense),
        Stream("ev_in", 12, KT * PC), Stream("ev_out", 4, KT * PC), Stream("ffn_ev", FC, dense),
        Stream("od_in", 7, KT * PC), Stream("od_out", 4, KT * PC), Stream("moe", NE * FC, dense),
    ]
    load_small(p, [(p.cols[:], ap["cols"]), (p.ident[:], ap["ident"])])
    block1(p, [(p.x[:], ap["x"].rearrange("(t p) d -> p t d", p=P)),
               (p.ctx[:], ap["ctx"].rearrange("(t p) d -> p t d", p=P)), (p.side[:], ap["w_dt"]),
               (p.con[:, 0:N_CON1], ap["con1"]),
               (p.rows[:, 0:N_ROWS1], ap["rows1"].broadcast_to([P, N_ROWS1]))],
           [(p.con[:, 0:N_CON2], ap["con2"])])
    even_layer(p, [(p.rows[:, 0:N_ROWS2], ap["rows2"].broadcast_to([P, N_ROWS2])),
                   (p.gates[:, 0, 0:512], ap["ssm_norm"].broadcast_to([P, 512]))])
    odd_layer(p)
    stored = p.sig("stored")
    with nc.Block(no_gpsimd_drain=True) as block:
        @block.sync
        def _(sp):
            sp.dma_start(ap["out"].rearrange("(t p) d -> p t d", p=P), p.x[:]).then_inc(stored.sem, 16)
            sp.wait_ge(*stored(16))
    return p


def constants():
    f = np.float32
    q = np.arange(T)
    tile = lambda m: np.ascontiguousarray(m.reshape(NT, P, -1).transpose(1, 0, 2).reshape(P, -1)).astype(f)
    window = np.concatenate([np.zeros((T, T)), np.where(np.abs(q[None] - q[:, None]) <= 128, 0.0, NEG)], 1)
    ang = 2 * np.pi * (np.outer(q, q) % T) / T
    dft_seq = np.concatenate([np.cos(ang), np.sin(ang)], 1) / 16.0
    ch = np.arange(HD)
    a2 = 2 * np.pi * (np.outer(ch, ch) % HD) / HD
    two = np.eye(2)
    dft_cos, dft_sin = np.kron(two, np.cos(a2)) / 8.0, -np.kron(two, np.sin(a2)) / 8.0

    def tables(ang):
        c, s = np.cos(ang), np.sin(ang)
        return np.concatenate([c, c], 1), np.concatenate([-s, s], 1)
    inv1 = (f(10000.0) ** (-np.arange(0, 32, 2, dtype=f) / f(32))).astype(f)
    row, colp = (q // 64).astype(f), (q % 64).astype(f)
    c1, s1 = tables(np.concatenate([row[:, None] * inv1, colp[:, None] * inv1], 1).astype(f).astype(np.float64))
    inv2 = (f(1.0) / (f(10000.0) ** (np.arange(0, 64, 2, dtype=f) / f(64)))).astype(f)
    c2, s2 = tables((q.astype(f)[:, None] * inv2[None]).astype(f).astype(np.float64))
    end = np.arange(N_CMP) * 16 + 31
    pad = lambda m: np.concatenate([m, np.zeros((P - len(m), m.shape[1]))], 0).astype(f)
    valid = end[None] <= q[:, None]
    tri = (q[:, None] <= q[None]).astype(f)
    con1 = np.concatenate([tile(window), tile(dft_seq), dft_cos.astype(f), dft_sin.astype(f), tile(c1), tile(s1)], 1)
    con2 = np.concatenate([tile(np.where(q[None] <= q[:, None], 0.0, NEG)), tile(tri), tile(np.where(tri > 0, 0.0, NEG)),
                           tile(c2), tile(s2), pad(c2[end]), pad(s2[end]), tile(np.where(valid, 0.0, NEG)),
                           tile(valid.astype(f)), np.tile(np.arange(P, dtype=f), (P, 1))], 1)
    assert con1.shape[1] == N_CON1 and con2.shape[1] == N_CON2
    return con1, con2


def kernel(**inputs):
    import concourse.bacc as bacc
    from concourse.bass_utils import run_bass_kernel_spmd

    a = {k: np.asarray(v) for k, v in inputs.items()}
    arrays = {}

    def feature_columns(v):
        return v.reshape(-1, P).T

    def chunks(w, width):
        n = -(-w.shape[1] // width)
        if n * width != w.shape[1]:
            w = np.concatenate([w, np.zeros((w.shape[0], n * width - w.shape[1]), w.dtype)], 1)
        return np.ascontiguousarray(w.reshape(KT, P, n, width).transpose(2, 1, 0, 3).reshape(n, P, KT * width))

    def ffn_chunks(gate, up, down):
        n = gate.shape[-1] // P
        out = np.empty((n, P, 3, KT * P), gate.dtype)
        for i, w in enumerate((gate, up)):
            out[:, :, i].reshape(n, P, KT, P)[:] = w.reshape(KT, P, n, P).transpose(2, 1, 0, 3)
        out[:, :, 2] = down.reshape(n, P, D)
        return out.reshape(n, P, SLOT)

    arrays["x"] = a["x"].reshape(T, D)
    arrays["b_ada"] = a["b_ada"]
    arrays["ctx"] = a["ctx"].reshape(T, D)
    for l in range(2):
        arrays[f"w_ada{l}"] = chunks(a["w_ada"][l], PC)
        arrays[f"w_in{l}"] = chunks(a["w_in"][l], PC)
        arrays[f"w_out{l}"] = chunks(a["w_out"][l], PC)
        arrays[f"ffn{l}"] = ffn_chunks(a["w_gate"][l], a["w_up"][l], a["w_down"][l])
    arrays["w_in1_kv"] = arrays["w_in1"][[1, 2, 5]]
    ev = a["ev_w_in_2"][0]
    arrays["ev_in"] = chunks(ev[:, 0:3072], PC)
    arrays["w_dt"] = np.ascontiguousarray(ev[:, 3072:3080].reshape(KT, P, 8).transpose(1, 0, 2))
    arrays["ev_out"] = chunks(a["ev_w_out_2"][0], PC)
    arrays["ffn_ev"] = ffn_chunks(a["ffn_w_gate_2"][0], a["ffn_w_up_2"][0], a["ffn_w_down_2"][0])
    arrays["od_in"] = chunks(a["od_w_in_2"][0], PC)
    arrays["od_out"] = chunks(a["od_w_out_2"][0], PC)
    arrays["moe"] = np.concatenate([ffn_chunks(a["moe_w_gate_2"][0, e], a["moe_w_up_2"][0, e], a["moe_w_down_2"][0, e])
                                    for e in range(NE)])
    arrays["router"] = np.ascontiguousarray(a["moe_router_2"][0].reshape(KT, P, NE).transpose(1, 0, 2))
    arrays["cmp_w1"] = np.ascontiguousarray(a["nsa_cmp_w1_2"][0].reshape(2, 32, HD, HD).transpose(2, 0, 1, 3))
    arrays["cmp_w2"] = np.ascontiguousarray(a["nsa_cmp_w2_2"][0].transpose(1, 0, 2))
    arrays["w_uq"] = np.ascontiguousarray(a["mla_w_uq_2"][0].reshape(2, P, 768).transpose(1, 0, 2))
    arrays["w_ukv"] = a["mla_w_ukv_2"][0]
    pos = a["nsa_cmp_pos_2"][0].transpose(2, 0, 1).reshape(HD, 64)
    arrays["cols"] = np.concatenate([
        feature_columns(a["g_mix"]), feature_columns(a["g_ffn"]), feature_columns(a["ev_norm_mix_2"][0]),
        feature_columns(a["ev_norm_ffn_2"][0]), feature_columns(a["od_norm_mix_2"][0]),
        feature_columns(a["od_norm_ffn_2"][0]),
        np.stack([a["c"][0].reshape(KT, P), a["c_ctx"].reshape(KT, P)], -1).transpose(1, 0, 2).reshape(P, 16),
        a["ssm_conv_w_2"][0].reshape(4, KT, P).transpose(2, 1, 0).reshape(P, 32),
        feature_columns(a["ssm_conv_b_2"][0]), np.concatenate([pos, np.zeros_like(pos)], 0)], 1)
    arrays["rows1"] = np.concatenate([a[k].reshape(-1) for k in ("q_norm", "k_norm", "sink", "g_final")])[None]
    arrays["rows2"] = np.concatenate([a[k + "_2"].reshape(-1) for k in (
        "da_q_gain", "da_k_gain", "da_lambda", "da_subln_gain", "ssm_dt_bias", "ssm_a_log", "ssm_d",
        "nsa_q_gain", "nsa_k_gain", "mla_cq_gain", "mla_ckv_gain", "mla_qn_gain", "mla_qr_gain",
        "mla_kn_gain", "mla_kr_gain")])[None]
    arrays["ssm_norm"] = a["ssm_norm_gain_2"].reshape(1, 512)
    arrays["con1"], arrays["con2"] = constants()
    arrays["ident"] = np.eye(P, dtype=np.float32)

    nc = bacc.Bacc("TRN2", target_bir_lowering=False, num_devices=1)
    ap, maps = {}, {}
    for name, v in arrays.items():
        v = np.ascontiguousarray(v)
        maps[f"in_{name}"] = v
        ap[name] = nc.dram_tensor(f"in_{name}", v.shape, F32, kind="ExternalInput").ap()
    ap["out"] = nc.dram_tensor("out_x", (T, D), F32, kind="ExternalOutput").ap()
    build(nc, ap)
    r = run_bass_kernel_spmd(nc, [maps], core_ids=[0])
    return r.results[0]["out_x"].reshape(1, T, D)
```
